# Optimizing a Trainium2 kernel written in Bass

```python
import jax, jax.numpy as jnp
from jax import lax
import numpy as np

D_MODEL = 2048
BATCH = 1
SEQ = 256
DEPTH = 1

PE_DIM = 256
MIX_WIDTH = D_MODEL
ML_WIDTH = MIX_WIDTH // 2
ML_HEADS = 4
ML_DV = ML_WIDTH // ML_HEADS
ML_DQK = ML_DV // 2
ML_QK = ML_HEADS * ML_DQK
ML_CONV = 4
ML_CHUNK = 64
HG_WIDTH = MIX_WIDTH - ML_WIDTH
HG_EXPAND = 128
HG_HEADS = HG_WIDTH // HG_EXPAND
HG_DV = HG_WIDTH // HG_HEADS
HG_FDIM = HG_HEADS * HG_EXPAND
HG_CHUNK = 64
EPS = 1e-6

SPLIT_SIZES = (ML_QK, ML_QK, ML_WIDTH, ML_WIDTH, ML_WIDTH, ML_HEADS, ML_HEADS,
               HG_FDIM, HG_FDIM, HG_WIDTH, HG_WIDTH)
IN_COLS = sum(SPLIT_SIZES)


def rmsnorm(x, w):
    xf = x.astype(jnp.float32)
    return xf * lax.rsqrt(jnp.mean(xf * xf, axis=-1, keepdims=True) + EPS) * w.astype(jnp.float32)

def causal_dwconv(x, w, b):
    K = w.shape[0]
    S = x.shape[1]
    xp = jnp.pad(x, ((0, 0), (K - 1, 0), (0, 0)))
    y = xp[:, 0:S, :] * w[0]
    for k in range(1, K):
        y = y + xp[:, k:k + S, :] * w[k]
    return y + b

def to_chunks(x, L):
    Bn, S = x.shape[0], x.shape[1]
    x = x.reshape((Bn, S // L, L) + x.shape[2:])
    perm = (1, 0, 3, 2) + tuple(range(4, x.ndim))
    return x.transpose(perm)

def from_chunks(y):
    NC, Bn, H, L, d = y.shape
    return y.transpose(1, 0, 3, 2, 4).reshape(Bn, NC * L, H, d)

def mlstm_chunkwise(q, k, v, i_pre, f_pre):
    L = ML_CHUNK
    Bn, S, H, dqk = q.shape
    dv = v.shape[-1]
    k = k * (dqk ** -0.5)
    logf = jax.nn.log_sigmoid(f_pre)
    xs = (to_chunks(q, L), to_chunks(k, L), to_chunks(v, L), to_chunks(i_pre, L), to_chunks(logf, L))
    causal = jnp.tril(jnp.ones((L, L), dtype=bool))

    def step(carry, inp):
        C, n, m = carry
        qc, kc, vc, ig, lf = inp
        b = jnp.cumsum(lf, axis=-1)
        logD = jnp.where(causal, b[..., :, None] - b[..., None, :] + ig[..., None, :], -jnp.inf)
        inter_log = b + m[..., None]
        m_t = jnp.maximum(inter_log, jnp.max(logD, axis=-1))
        scores = jnp.einsum('bhtd,bhjd->bhtj', qc, kc) * jnp.exp(logD - m_t[..., None])
        w_inter = jnp.exp(inter_log - m_t)
        num = (jnp.einsum('bhtj,bhjv->bhtv', scores, vc)
               + w_inter[..., None] * jnp.einsum('bhtd,bhdv->bhtv', qc, C))
        den = jnp.sum(scores, axis=-1) + w_inter * jnp.einsum('bhtd,bhd->bht', qc, n)
        h = num / jnp.maximum(jnp.abs(den), jnp.exp(-m_t))[..., None]
        g = b[..., -1]
        a = g[..., None] - b + ig
        m_new = jnp.maximum(g + m, jnp.max(a, axis=-1))
        wa = jnp.exp(a - m_new[..., None])
        ws = jnp.exp(g + m - m_new)
        C_new = ws[..., None, None] * C + jnp.einsum('bhj,bhjd,bhjv->bhdv', wa, kc, vc)
        n_new = ws[..., None] * n + jnp.einsum('bhj,bhjd->bhd', wa, kc)
        return (C_new, n_new, m_new), h

    init = (jnp.zeros((Bn, H, dqk, dv), jnp.float32),
            jnp.zeros((Bn, H, dqk), jnp.float32),
            jnp.zeros((Bn, H), jnp.float32))
    _, hs = lax.scan(step, init, xs)
    return from_chunks(hs)

def hgrn2_chunkwise(q, k, logf, iv):
    L = HG_CHUNK
    Bn, S, H, E = q.shape
    dv = iv.shape[-1]
    xs = (to_chunks(q, L), to_chunks(k, L), to_chunks(logf, L), to_chunks(iv, L))
    causal = jnp.tril(jnp.ones((L, L), dtype=bool))[:, :, None]

    def step(Sst, inp):
        qc, kc, lf, vc = inp
        b = jnp.cumsum(lf, axis=2)
        decay = jnp.exp(jnp.where(causal, b[:, :, :, None, :] - b[:, :, None, :, :], -jnp.inf))
        A = jnp.einsum('bhte,bhje,bhtje->bhtj', qc, kc, decay)
        o = (jnp.einsum('bhtj,bhjv->bhtv', A, vc)
             + jnp.einsum('bhte,bhev->bhtv', qc * jnp.exp(b), Sst))
        g = b[:, :, -1, :]
        S_new = (jnp.exp(g)[..., None] * Sst
                 + jnp.einsum('bhje,bhjv->bhev', kc * jnp.exp(g[:, :, None, :] - b), vc))
        return S_new, o

    _, os_ = lax.scan(step, jnp.zeros((Bn, H, E, dv), jnp.float32), xs)
    return from_chunks(os_)

def first_inputs(seed: int = 0) -> dict:
    key = jax.random.key(seed)
    ks = jax.random.split(key, 16)
    f32 = jnp.float32
    nrm = lambda k, shape, s: jax.random.normal(k, shape, f32) * s
    x = jax.random.normal(ks[0], (BATCH, SEQ, D_MODEL), f32)
    p = jax.random.normal(ks[1], (DEPTH, BATCH, SEQ, PE_DIM), f32)
    norm_w = 1.0 + nrm(ks[2], (DEPTH, D_MODEL), 0.05)
    w_in = nrm(ks[3], (DEPTH, D_MODEL, IN_COLS), D_MODEL ** -0.5)
    conv_w = nrm(ks[4], (DEPTH, ML_CONV, 2 * ML_QK), ML_CONV ** -0.5)
    conv_b = nrm(ks[5], (DEPTH, 2 * ML_QK), 0.02)
    ml_b_i = nrm(ks[6], (DEPTH, ML_HEADS), 0.1)
    ml_b_f = jnp.linspace(3.0, 6.0, ML_HEADS, dtype=f32)[None, :] + nrm(ks[7], (DEPTH, ML_HEADS), 0.1)
    ml_norm_w = 1.0 + nrm(ks[8], (DEPTH, ML_WIDTH), 0.05)
    hg_lb = nrm(ks[9], (DEPTH + 1, HG_FDIM), 0.1)
    hg_norm_w = 1.0 + nrm(ks[10], (DEPTH, HG_WIDTH), 0.05)
    w_out = nrm(ks[11], (DEPTH, MIX_WIDTH, D_MODEL), MIX_WIDTH ** -0.5)
    pe_norm_w = 1.0 + nrm(ks[12], (DEPTH, D_MODEL), 0.05)
    w_pg = nrm(ks[13], (DEPTH, D_MODEL, D_MODEL), D_MODEL ** -0.5)
    w_pe = nrm(ks[14], (DEPTH, PE_DIM, D_MODEL), PE_DIM ** -0.5)
    final_norm_w = 1.0 + nrm(ks[15], (D_MODEL,), 0.05)
    return {"x": x, "p": p, "norm_w": norm_w, "w_in": w_in, "conv_w": conv_w,
            "conv_b": conv_b, "ml_b_i": ml_b_i, "ml_b_f": ml_b_f, "ml_norm_w": ml_norm_w,
            "hg_lb": hg_lb, "hg_norm_w": hg_norm_w, "w_out": w_out, "pe_norm_w": pe_norm_w,
            "w_pg": w_pg, "w_pe": w_pe, "final_norm_w": final_norm_w}

def first_block(x, p, norm_w, w_in, conv_w, conv_b, ml_b_i, ml_b_f, ml_norm_w,
              hg_lb, hg_norm_w, w_out, pe_norm_w, w_pg, w_pe, final_norm_w):
    Bn, S, _ = x.shape
    split_points = [int(s) for s in np.cumsum(SPLIT_SIZES)[:-1]]
    lb_all = jnp.cumsum(jax.nn.softmax(hg_lb.astype(jnp.float32), axis=0), axis=0)
    h = x.astype(jnp.float32)
    for l in range(DEPTH):
        u = rmsnorm(h, norm_w[l])
        proj = jnp.einsum('bsd,dc->bsc', u, w_in[l].astype(jnp.float32))
        (ml_q, ml_k, ml_v, ml_o, ml_z, ml_i, ml_f,
         hg_q, hg_f, hg_i, hg_g) = jnp.split(proj, split_points, axis=-1)

        qk = jax.nn.silu(causal_dwconv(jnp.concatenate([ml_q, ml_k], axis=-1),
                                       conv_w[l].astype(jnp.float32), conv_b[l].astype(jnp.float32)))
        q_a = qk[..., :ML_QK].reshape(Bn, S, ML_HEADS, ML_DQK)
        k_a = qk[..., ML_QK:].reshape(Bn, S, ML_HEADS, ML_DQK)
        v_a = ml_v.reshape(Bn, S, ML_HEADS, ML_DV)
        i_pre = ml_i + ml_b_i[l].astype(jnp.float32)
        f_pre = ml_f + ml_b_f[l].astype(jnp.float32)
        h_a = mlstm_chunkwise(q_a, k_a, v_a, i_pre, f_pre)
        h_a = rmsnorm(h_a, ml_norm_w[l].reshape(ML_HEADS, ML_DV)).reshape(Bn, S, ML_WIDTH)
        y_a = jax.nn.sigmoid(ml_o) * h_a * jax.nn.silu(ml_z)

        lb = lb_all[l]
        f_b = lb + (1.0 - lb) * jax.nn.sigmoid(hg_f)
        logf_b = jnp.log(f_b).reshape(Bn, S, HG_HEADS, HG_EXPAND)
        k_b = ((1.0 - lb) * jax.nn.sigmoid(-hg_f)).reshape(Bn, S, HG_HEADS, HG_EXPAND)
        q_b = hg_q.reshape(Bn, S, HG_HEADS, HG_EXPAND)
        i_b = hg_i.reshape(Bn, S, HG_HEADS, HG_DV)
        h_b = hgrn2_chunkwise(q_b, k_b, logf_b, i_b)
        h_b = rmsnorm(h_b, hg_norm_w[l].reshape(HG_HEADS, HG_DV)).reshape(Bn, S, HG_WIDTH)
        y_b = h_b * jax.nn.silu(hg_g)

        y = jnp.concatenate([y_a, y_b], axis=-1)
        h = h + jnp.einsum('bsc,cd->bsd', y, w_out[l].astype(jnp.float32))

        e = jnp.einsum('bsr,rd->bsd', p[l].astype(jnp.float32), w_pe[l].astype(jnp.float32))
        gate = jax.nn.sigmoid(jnp.einsum('bsd,de->bse', rmsnorm(h, pe_norm_w[l]), w_pg[l].astype(jnp.float32)))
        h = h + gate * e
    out = rmsnorm(h, final_norm_w)
    return out.astype(x.dtype)


PLE_DIM = 256
CHUNK = 128
SGU_GROUPS = 8
SGU_GROUP_DIM = 128
SGU_WIDTH = SGU_GROUPS * SGU_GROUP_DIM
SB_HEADS = 8
SB_HEAD_DIM = 128
SB_WIDTH = SB_HEADS * SB_HEAD_DIM
Q_BLOCK = 128
FFN_HIDDEN = ((8 * D_MODEL + 3 * 256 - 1) // (3 * 256)) * 256
IN_COLS_2 = 2 * SGU_WIDTH + 3 * SB_WIDTH + 2 * D_MODEL


def rmsnorm_2(x, g):
    xf = x.astype(jnp.float32)
    y = xf * lax.rsqrt(jnp.mean(xf * xf, axis=-1, keepdims=True) + EPS)
    return (y * g.astype(jnp.float32)).astype(x.dtype)

def chunked_spatial_gating(u, v, w_s, b_s):
    B, S, G, C = v.shape
    tri = jnp.tril(jnp.ones((CHUNK, CHUNK), dtype=w_s.dtype))
    ws = w_s * tri[None]
    vc = v.reshape(B, S // CHUNK, CHUNK, G, C)
    mixed = jnp.einsum('gts,bnsgc->bntgc', ws, vc)
    mixed = mixed + jnp.transpose(b_s)[None, None, :, :, None]
    return u * mixed.reshape(B, S, G, C)

def stick_breaking_attention(q, k, v):
    B, S, H, Dh = q.shape
    nb = S // Q_BLOCK
    scale = Dh ** -0.5
    qf = jnp.transpose(q, (0, 2, 1, 3))
    kf = jnp.transpose(k, (0, 2, 1, 3))
    vf = jnp.transpose(v, (0, 2, 1, 3))
    key_pos = jnp.arange(S, dtype=jnp.int32)

    def one_block(blk):
        start = blk * Q_BLOCK
        qi = lax.dynamic_slice_in_dim(qf, start, Q_BLOCK, axis=2)
        z = jnp.einsum('bhqd,bhkd->bhqk', qi, kf).astype(jnp.float32) * scale
        q_pos = start + jnp.arange(Q_BLOCK, dtype=jnp.int32)
        strict = key_pos[None, :] < q_pos[:, None]
        log_beta = jax.nn.log_sigmoid(z)
        log_1m = jnp.where(strict, jax.nn.log_sigmoid(-z), jnp.zeros_like(z))
        tail = lax.cumsum(log_1m, axis=3, reverse=True) - log_1m
        w = jnp.where(strict, jnp.exp(log_beta + tail), jnp.zeros_like(z))
        return jnp.einsum('bhqk,bhkd->bhqd', w.astype(vf.dtype), vf)

    out = lax.map(one_block, jnp.arange(nb, dtype=jnp.int32))
    out = jnp.transpose(out, (1, 0, 3, 2, 4))
    return out.reshape(B, S, H, Dh)

def second_inputs(seed: int = 0) -> dict:
    key = jax.random.key(seed)
    ks = jax.random.split(key, 20)
    f = jnp.float32

    def nrm(k, shape, fan_in):
        return jax.random.normal(k, shape, f) * (fan_in ** -0.5)

    def gain(k, shape):
        return 1.0 + 0.05 * jax.random.normal(k, shape, f)

    return {
        "x": jax.random.normal(ks[0], (BATCH, SEQ, D_MODEL), f),
        "p": jax.random.normal(ks[1], (DEPTH, BATCH, SEQ, PLE_DIM), f),
        "attn_norm_g": gain(ks[2], (DEPTH, D_MODEL)),
        "w_in": nrm(ks[3], (DEPTH, D_MODEL, IN_COLS_2), D_MODEL),
        "sgu_norm_g": gain(ks[4], (DEPTH, SGU_GROUPS, SGU_GROUP_DIM)),
        "w_s": nrm(ks[5], (DEPTH, SGU_GROUPS, CHUNK, CHUNK), CHUNK),
        "b_s": 1.0 + 0.1 * jax.random.normal(ks[6], (DEPTH, SGU_GROUPS, CHUNK), f),
        "q_norm_g": gain(ks[7], (DEPTH, SB_HEAD_DIM)),
        "k_norm_g": gain(ks[8], (DEPTH, SB_HEAD_DIM)),
        "w_up_a": nrm(ks[9], (DEPTH, SGU_WIDTH, D_MODEL), SGU_WIDTH),
        "w_up_b": nrm(ks[10], (DEPTH, SB_WIDTH, D_MODEL), SB_WIDTH),
        "w_o": nrm(ks[11], (DEPTH, D_MODEL, D_MODEL), D_MODEL),
        "ffn_norm_g": gain(ks[12], (DEPTH, D_MODEL)),
        "w_ffn_in": nrm(ks[13], (DEPTH, D_MODEL, 2 * FFN_HIDDEN), D_MODEL),
        "w_ffn_out": nrm(ks[14], (DEPTH, FFN_HIDDEN, D_MODEL), FFN_HIDDEN),
        "ple_norm_g": gain(ks[15], (DEPTH, D_MODEL)),
        "w_ple_gate": nrm(ks[16], (DEPTH, D_MODEL, D_MODEL), D_MODEL),
        "w_ple": nrm(ks[17], (DEPTH, PLE_DIM, D_MODEL), PLE_DIM),
    }

def second_block(x, p, attn_norm_g, w_in, sgu_norm_g, w_s, b_s, q_norm_g, k_norm_g,
              w_up_a, w_up_b, w_o, ffn_norm_g, w_ffn_in, w_ffn_out,
              ple_norm_g, w_ple_gate, w_ple):
    B, S, D = x.shape
    c0 = SGU_WIDTH
    c1 = c0 + SGU_WIDTH
    c2 = c1 + SB_WIDTH
    c3 = c2 + SB_WIDTH
    c4 = c3 + SB_WIDTH
    c5 = c4 + D_MODEL
    for i in range(DEPTH):
        h = rmsnorm_2(x, attn_norm_g[i])
        proj = h @ w_in[i]
        u = proj[..., :c0]
        v_sgu = proj[..., c0:c1]
        q = proj[..., c1:c2]
        k = proj[..., c2:c3]
        v_att = proj[..., c3:c4]
        g_a = proj[..., c4:c5]
        g_b = proj[..., c5:]

        u = jax.nn.gelu(u).reshape(B, S, SGU_GROUPS, SGU_GROUP_DIM)
        v_sgu = rmsnorm_2(jax.nn.gelu(v_sgu).reshape(B, S, SGU_GROUPS, SGU_GROUP_DIM), sgu_norm_g[i])
        y_a = chunked_spatial_gating(u, v_sgu, w_s[i], b_s[i]).reshape(B, S, SGU_WIDTH)

        q = rmsnorm_2(q.reshape(B, S, SB_HEADS, SB_HEAD_DIM), q_norm_g[i])
        k = rmsnorm_2(k.reshape(B, S, SB_HEADS, SB_HEAD_DIM), k_norm_g[i])
        v_att = v_att.reshape(B, S, SB_HEADS, SB_HEAD_DIM)
        y_b = stick_breaking_attention(q, k, v_att).reshape(B, S, SB_WIDTH)

        merged = jax.nn.sigmoid(g_a) * (y_a @ w_up_a[i]) + jax.nn.sigmoid(g_b) * (y_b @ w_up_b[i])
        x = x + merged @ w_o[i]

        h = rmsnorm_2(x, ffn_norm_g[i])
        hid = h @ w_ffn_in[i]
        gate = hid[..., :FFN_HIDDEN]
        up = hid[..., FFN_HIDDEN:]
        x = x + (jax.nn.silu(gate) * up) @ w_ffn_out[i]

        ple = p[i] @ w_ple[i]
        x = x + jax.nn.sigmoid(rmsnorm_2(x, ple_norm_g[i]) @ w_ple_gate[i]) * ple
    return x


def setup_inputs(seed=0):
    out = dict(first_inputs(seed))
    for name, value in second_inputs(seed + 1).items():
        if name != "x":
            out[name + "_2"] = value
    return out


def reference(
    x, p, norm_w, w_in, conv_w, conv_b, ml_b_i, ml_b_f, ml_norm_w, hg_lb, hg_norm_w, w_out,
    pe_norm_w, w_pg, w_pe, final_norm_w, p_2, attn_norm_g_2, w_in_2, sgu_norm_g_2, w_s_2, b_s_2,
    q_norm_g_2, k_norm_g_2, w_up_a_2, w_up_b_2, w_o_2, ffn_norm_g_2, w_ffn_in_2, w_ffn_out_2,
    ple_norm_g_2, w_ple_gate_2, w_ple_2,
):
    x = first_block(
        x, p, norm_w, w_in, conv_w, conv_b, ml_b_i, ml_b_f, ml_norm_w, hg_lb, hg_norm_w, w_out,
        pe_norm_w, w_pg, w_pe, final_norm_w,
    )
    return second_block(
        x, p_2, attn_norm_g_2, w_in_2, sgu_norm_g_2, w_s_2, b_s_2, q_norm_g_2, k_norm_g_2,
        w_up_a_2, w_up_b_2, w_o_2, ffn_norm_g_2, w_ffn_in_2, w_ffn_out_2, ple_norm_g_2,
        w_ple_gate_2, w_ple_2,
    )


_drawn_inputs = setup_inputs


def setup_inputs(seed=0):
    import zlib

    import numpy as np

    out = dict(_drawn_inputs(seed))
    spreads = {}
    factors = {'conv_b': 8.0,
     'ml_b_i': 64.0,
     'ml_norm_w': 5.791,
     'hg_norm_w': 3.029,
     'pe_norm_w': 6.096,
     'sgu_norm_g_2': 5.029,
     'q_norm_g_2': 8.0,
     'k_norm_g_2': 8.0,
     'ple_norm_g_2': 25.233,
     'b_s_2': 2.701}
    for name, (base, spread) in spreads.items():
        noise = np.random.default_rng([zlib.crc32(name.encode()), seed]).standard_normal(out[name].shape)
        drawn = base * np.exp(spread * noise) if base else spread * noise
        out[name] = __import__('jax').numpy.asarray(drawn.astype(out[name].dtype))
    for name, factor in factors.items():
        out[name] = (out[name] * factor).astype(out[name].dtype)
    return out
```

```python
from contextlib import ExitStack

import concourse.bass as bass
from concourse import mybir

F32 = mybir.dt.float32
F32R = mybir.dt.float32r
I32 = mybir.dt.int32
ACT = mybir.ActivationFunctionType
ALU = mybir.AluOpType
AX = mybir.AxisListType

P = 128
D = 2048
KD = D // P
S = 256
T = S // P
COLS = 512
PK = 2
RING = 4
EPS = 1e-6

ML_HEADS, ML_DQK, ML_DV, ML_TAPS = 4, 128, 256, 4
ML_W = ML_HEADS * ML_DV
HG_HEADS, HG_E = 8, 128
SB_HEADS, SB_D = 8, 128
GROUPS = 8
PE_DIM = 256
FFN = 5632

MQ, MK, MV, MO, MZ, MI = 0, 512, 1024, 2048, 3072, 4096
HQ, HF, HI, HG = 4104, 5128, 6152, 7176
U2, S2, Q2, K2, V2, GA2, GB2 = 0, 1024, 2048, 3072, 4096, 5120, 7168

A_COLS = [HF, HQ, HI, HF + 512, HQ + 512, HI + 512, MQ, MK, MV, MV + 512, MZ, MZ + 512, MO, MO + 512, HG, HG + 512]
E1_COLS = [Q2, Q2 + 512, K2, K2 + 512, V2, V2 + 512, S2, S2 + 512, U2, U2 + 512]
FFN_PARTS = [(0, 2048), (2048, 2048), (4096, 1536)]

C_NORM, C_PE, C_ATTN, C_FFN, C_PLE, C_LB, C_CONVW = 0, 16, 32, 48, 64, 80, 96
C_CONVB, C_QN, C_KN, C_BS, C_MIX, C_END = 128, 136, 137, 138, 146, 162

LEVELS = [128 >> n for n in range(8)]


def plan():
    phases = [("A", [8] * 16), ("C", [8] * 4), ("D", [1, 8] * 4), ("E1", [8] * 10), ("E2", [8, 4] * 4),
              ("E3", [8, 4] * 4), ("G", [8] * 4)]
    for i, (_, width) in enumerate(FFN_PARTS):
        phases.append((f"H{i}", [8, 8] * (width // COLS)))
        phases.append((f"O{i}", [width // P // PK] * 4))
    phases.append(("J", [1, 8] * 4))
    slabs, first, g = [], {}, 0
    for name, counts in phases:
        first[name] = len(slabs)
        for n in counts:
            slabs.append((g, n))
            g += n
    return slabs, first


def plan_aux():
    names = [("gains", 0), ("p", 0), ("p2", 0)] + [("xT", i) for i in range(8)]

    def two(name, *key):
        names.extend((name, *key, i) for i in range(2))

    def levels(half):
        two("diag", half)
        names.extend(("level", half, n) for n in range(8))

    two("tr", 0); two("tr", 1); levels(0); two("pv", 0)
    two("tr", 3); two("tr", 4); levels(1); two("pv", 1)
    two("tr", 6); names.append(("gates", 0)); two("tr", 7)
    names.extend([("gtr", 0), ("atr", 0), ("bc", 0), ("bc", 1)])
    names.extend(("st", h) for h in range(4))
    names.extend(("mpv", h, t) for h in range(4) for t in range(2))
    names.extend(("yT", i) for i in range(8))
    names.extend(("hD", i) for i in range(8))
    names.extend(("hE", i) for i in range(8))
    two("tr2", 0); two("ws"); two("tr2", 1); two("tr2", 2); two("tr2", 3)
    for b in range(2):
        names.extend(("z", b, h) for h in range(4))
        names.extend(("tail", b, h) for h in range(4))
        two("att", b)
    names.extend([("sgu", 0), ("sgu", 1), ("yaT", 0), ("yaT", 1), ("sgu", 2), ("sgu", 3), ("yaT", 2), ("yaT", 3)])
    names.extend(("ybT", i) for i in range(4))
    names.extend(("mT", i) for i in range(8))
    names.extend(("hH", i) for i in range(8))
    for part, (_, width) in enumerate(FFN_PARTS):
        names.extend(("hid", part, c) for c in range(width // P))
    names.extend(("hJ", i) for i in range(8))
    assert len(set(names)) == len(names)
    return {n: i for i, n in enumerate(names)}


def two_blocks_kernel(nc, A, out):
    SLABS, FIRST = plan()
    AUX = plan_aux()
    ctx = ExitStack()
    with ctx:
        def sb(name, shape, dt=F32, at=None):
            return (at or ctx).enter_context(nc.sbuf_tensor(name, shape, dt))

        sems = {}

        def sem(name):
            if name not in sems:
                sems[name] = ctx.enter_context(nc.semaphore(name))
            return sems[name]

        raw = sb("raw", [P, RING, PK, COLS])
        whi = sb("whi", [P, RING, PK, COLS], F32R)
        wlo = sb("wlo", [P, RING, PK, COLS], F32R)
        resid = sb("resid", [P, T, D])
        ra = ExitStack()
        actA = [sb(f"actA_{x}", [P, KD, S], F32R, at=ra) for x in ("hi", "lo")]
        ra.close()
        qT = sb("qT", [P, 8, S])
        kT = sb("kT", [P, 8, S])
        zt = sb("att_z", [P, 4, 384])
        Lp = sb("att_l", [P, 4, 384])
        sb("rest_of_actA", [P, 2 * KD * S - 16 * S - 8 * 384])
        actB = [sb(f"actB_{x}", [P, KD, S], F32R) for x in ("hi", "lo")]
        gate = [sb(f"gate{i}", [P, T, COLS]) for i in range(2)]
        pT = [[sb(f"p{n}T_{x}", [P, PK, S], F32R) for x in ("hi", "lo")] for n in range(2)]
        gains = sb("gains", [P, C_END])
        lb = sb("lb", [P, 4, 8])
        qn_scaled = sb("qn_scaled", [P, 1])
        ident = sb("ident", [P, P])
        ones = sb("ones", [P, S])
        causal = sb("causal", [P, P])
        strict = sb("strict", [P, P])
        later = sb("later", [P, P])
        lmask = sb("lmask", [P, 7, 64])
        minus_half = sb("minus_half", [P, 16])
        junk = sb("junk", [P, COLS])
        ss = sb("ss", [P, 16, 8])
        var = sb("var", [P, 16, 8])
        rstd = sb("rstd", [P, 16, 8])
        r_e = sb("r_e", [P, T])
        r1 = ExitStack()
        ob = sb("hg_v", [P, T, 1024], at=r1)
        gw = [sb("gw", [P, KD, 8], at=r1), sb("gw_hi", [P, KD, 8], F32R, at=r1), sb("gw_lo", [P, KD, 8], F32R, at=r1)]
        gbias = sb("gbias", [P, 8], at=r1)
        sel = sb("sel", [4, 4, P], at=r1)
        gtok = sb("gtok", [P, T, 8], at=r1)
        gtmp = sb("gtmp", [P, T, 4], at=r1)
        acol = sb("acol", [P, 16], at=r1)
        den = sb("den", [P, 8, 2], at=r1)
        rs = ExitStack()
        stage1 = sb("stage1", [P, P], at=rs)
        stage2 = sb("stage2", [C_END - P, P], at=rs)
        ptok = [sb(f"ptok{n}", [P, T, PE_DIM], at=rs) for n in range(2)]
        rs.close()
        rh = ExitStack()
        bF = sb("hg_b", [P, 1024], at=rh)
        qF = sb("hg_q", [P, 1024], at=rh)
        kF = sb("hg_k", [P, 1024], at=rh)
        Eb = [sb(f"hg_e{i}", [P, 1024], at=rh) for i in range(2)]
        Qp = [sb(f"hg_qd{i}", [P, 512], at=rh) for i in range(2)]
        Kp = [sb(f"hg_kd{i}", [P, 1024], at=rh) for i in range(2)]
        Am = sb("hg_a", [P, 8, P], at=rh)
        A01 = sb("hg_a01", [P, 4, P], at=rh)
        rh.close()
        rm = ExitStack()
        qk = sb("ml_qk", [P, 8, S], at=rm)
        hrow = sb("hrow", [4, 6, S], at=rm)
        Wd = sb("ml_w", [P, 4, 384], at=rm)
        hA = sb("ml_h", [P, T, ML_W], at=rm)
        vml = sb("ml_v", [P, T, 4, ML_DV + 2], at=rm)
        rm.close()
        rd = ExitStack()
        eb = [sb(f"ple_e{i}", [P, T, COLS], at=rd) for i in range(2)]
        fw = sb("final_gain", [P, D], at=rd)
        rd.close()
        r1.close()
        r2 = ExitStack()
        merged = sb("merged", [P, T, D], at=r2)
        r2f = ExitStack()
        actF = [sb(f"actF_{x}", [P, KD, S], F32R, at=r2f) for x in ("hi", "lo")]
        hid = sb("hid", [P, T, COLS], at=r2f)
        r2f.close()
        vA = sb("att_v", [P, T, 1024], at=r2)
        ab = sb("att_ab", [P, 4, 384], at=r2)
        gbc = sb("sgu_gain", [P, 1024], at=r2)
        wsT = sb("wsT", [P, 8, P], at=r2)
        r2.close()
        r2b = ExitStack()
        u2 = sb("sgu_u", [P, T, 1024], at=r2b)
        vs = sb("sgu_v", [P, T, 1024], at=r2b)
        r2b.close()
        wsr = zt[:, :, :].rearrange("p a b -> p (a b)")[:, 0:1024].rearrange("p (g s) -> p g s", g=8)

        acc = ctx.enter_context(nc.psum_tensor("acc", [P, 4, COLS], F32))
        aux = ctx.enter_context(nc.psum_tensor("aux", [P, 4, COLS], F32))

        raw_loaded = [sem(f"raw_loaded{i}") for i in range(RING)]
        hi_ready, lo_ready, piece_used = sem("hi_ready"), sem("lo_ready"), sem("piece_used")
        acc_free = [sem(f"acc_free{i}") for i in range(2)]
        aux_full = sem("aux_full")
        aux_free = [sem(f"aux_free{i}") for i in range(4)]
        split_hi_done = sem("split_hi_done")
        gate_ready = sem("gate_ready")
        pow_in, pow_out = sem("pow_in"), sem("pow_out")

        def view(w):
            return w.rearrange("(k p) n -> p k n", p=P)

        def aux_filled(eng, u, i=0):
            eng.wait_ge(aux_full, u + 1 + i * 4)

        def aux_taken(eng, u, i=0):
            eng.wait_ge(aux_free[u % 4], u // 4 + 1 + i)

        def slab_made(eng, n, i=0, per=0):
            eng.wait_ge(piece_used, sum(SLABS[n]) + i * per)

        def slab_taken(eng, n, i=0):
            eng.wait_ge(acc_free[n % 2], n // 2 + 1 + i)

        def bank(u, n=COLS):
            return aux[:, u % 4, 0:n]

        def acc2(n):
            return acc[:, 2 * (n % 2):2 * (n % 2) + 2, :]

        POWS = [("x", T), ("hB0", 8), ("hB1", 8), ("hA", 8), ("h1", T), ("f1", T), ("f2", T), ("qk0", 8), ("qk1", 8),
                ("qk2", 8), ("qk3", 8), ("s0", 8), ("s1", 8), ("ffn", T), ("ple", T)]
        SLOT = {n: i for i, (n, _) in enumerate(POWS)}

        def r_tok(name, t):
            return rstd[:, SLOT[name], t:t + 1]

        def powered(eng, name):
            eng.wait_ge(pow_out, SLOT[name] + 1)

        block = ctx.enter_context(nc.Block())

        @block.sync
        def _(sp):
            piece = [0]

            def load(src, dst=None):
                g = piece[0]
                piece[0] += 1
                if g >= RING:
                    sp.wait_ge(lo_ready, g - RING + 1)
                d = raw[:, g % RING] if dst is None else dst(raw[:, g % RING])
                sp.dma_start(d, src).then_inc(raw_loaded[g % RING], 16)

            def load_slab(w, c, n=8, k0=0):
                for p in range(n):
                    k = k0 + p * PK
                    load(view(w)[:, k:k + PK, c:c + COLS])

            for t in range(T):
                sp.dma_start(resid[:, t, :], A["x"][0, t * P:(t + 1) * P, :]).then_inc(sem("x_loaded"), 16)
            for c in A_COLS:
                load_slab(A["w_in"][0], c)
            for s in range(4):
                load_slab(A["w_out"][0], s * COLS)
            sp.wait_ge(sem("h_added"), 1)
            sp.dma_start(fw[:, :], A["final_norm_w"].partition_broadcast(P)).then_inc(sem("fw_loaded"), 16)
            for s in range(4):
                load_slab(A["w_pe"][0], s * COLS, 1)
                load_slab(A["w_pg"][0], s * COLS)
            for n, c in enumerate(E1_COLS):
                load_slab(A["w_in_2"][0], c)
                if n == 0:
                    sp.wait_ge(sem("block1_done"), 1)
                    sp.dma_start(wsr, A["w_s_2"][0].rearrange("g t s -> t g s")).then_inc(sem("ws_loaded"), 16)
                    sp.dma_start(gbc[:, :], A["sgu_norm_g_2"][0].rearrange("g c -> (g c)").partition_broadcast(P))\
                        .then_inc(sem("gbc_loaded"), 16)
            for c0, w_up in ((GA2, "w_up_a_2"), (GB2, "w_up_b_2")):
                for s in range(4):
                    load_slab(A["w_in_2"][0], c0 + s * COLS)
                    load_slab(A[w_up][0], s * COLS, 4)
            for s in range(4):
                load_slab(A["w_o_2"][0], s * COLS)
            for f0, width in FFN_PARTS:
                for s in range(width // COLS):
                    for h in range(2):
                        load_slab(A["w_ffn_in_2"][0], h * FFN + f0 + s * COLS)
                for s in range(4):
                    load_slab(A["w_ffn_out_2"][0], s * COLS, width // 256, f0 // P)
            for s in range(4):
                load_slab(A["w_ple_2"][0], s * COLS, 1)
                load_slab(A["w_ple_gate_2"][0], s * COLS)
            for s in range(4):
                for t in range(T):
                    sp.wait_ge(sem("out_ready"), s + 1)
                    sp.dma_start(out[0, t * P:(t + 1) * P, s * COLS:(s + 1) * COLS],
                                 resid[:, t, s * COLS:(s + 1) * COLS]).then_inc(sem("stored"), 16)
            sp.wait_ge(sem("stored"), 16 * 4 * T)

        @block.gpsimd
        def _(pool):
            made = [0]

            def link(ins):
                made[0] += 1
                ins.then_inc(sem("pool_step"), 1)

            def settle():
                pool.wait_ge(sem("pool_step"), made[0])

            link(pool.memset(ident[:, :], 0.0))
            link(pool.memset(ones[:, :], 1.0))
            link(pool.memset(lmask[:, :, :], 1.0))
            link(pool.memset(sel[:, :, :], 0.0))
            settle()
            link(pool.affine_select(out=ident[:, :], in_=ident[:, :], compare_op=ALU.not_equal, fill=1.0, base=0,
                                    pattern=[[-1, P]], channel_multiplier=1))
            link(pool.affine_select(out=causal[:, :], in_=ones[:, 0:P], compare_op=ALU.is_ge, fill=0.0, base=0,
                                    pattern=[[1, P]], channel_multiplier=-1))
            link(pool.affine_select(out=strict[:, :], in_=ones[:, 0:P], compare_op=ALU.is_gt, fill=0.0, base=0,
                                    pattern=[[1, P]], channel_multiplier=-1))
            link(pool.affine_select(out=later[:, :], in_=ones[:, 0:P], compare_op=ALU.is_gt, fill=0.0, base=0,
                                    pattern=[[-1, P]], channel_multiplier=1))
            link(pool.affine_select(out=sel[:, :, :], in_=sel[:, :, :], compare_op=ALU.not_equal, fill=1.0, base=0,
                                    pattern=[[-1, 4], [0, P]], channel_multiplier=1))
            for n, s in enumerate(LEVELS[1:]):
                m = lmask[:, n, :].rearrange("p (n s) -> p n s", s=s)
                link(pool.affine_select(out=m, in_=m, compare_op=ALU.is_ge, fill=0.0, base=0,
                                        pattern=[[-2 * s, 64 // s], [0, s]], channel_multiplier=1))
            settle()
            for n, s in enumerate(LEVELS[1:]):
                m = lmask[:, n, :].rearrange("p (n s) -> p n s", s=s)
                link(pool.affine_select(out=m, in_=m, compare_op=ALU.is_ge, fill=0.0, base=s - 1,
                                        pattern=[[2 * s, 64 // s], [0, s]], channel_multiplier=-1))
            link(pool.memset(minus_half[:, :], -0.5))
            settle()
            pool.memset(junk[:, 0:1], 0.0).then_inc(sem("consts_ready"), 1)
            for i, (name, n) in enumerate(POWS):
                if name == "qk0":
                    pool.wait_ge(sem("ws_loaded"), 16)
                    pool.affine_select(out=wsr, in_=wsr, compare_op=ALU.is_ge, fill=0.0, base=0,
                                       pattern=[[0, 8], [-1, P]], channel_multiplier=1).then_inc(sem("ws_masked"), 1)
                pool.wait_ge(pow_in, i + 1)
                pool.tensor_tensor(rstd[:, i, 0:n], var[:, i, 0:n], minus_half[:, 0:n], ALU.pow).then_inc(pow_out, 1)

        @block.scalar
        def _(act):
            steps = [0]
            gates = [0]

            def link(ins):
                steps[0] += 1
                ins.then_inc(sem("act_step"), 1)
                act.wait_ge(sem("act_step"), steps[0])

            def split_hi(g):
                act.wait_ge(raw_loaded[g % RING], 16 * (g // RING + 1))
                if g >= RING:
                    act.wait_ge(piece_used, g - RING + 1)
                act.activation(whi[:, g % RING], raw[:, g % RING], ACT.Copy).then_inc(hi_ready, 1)

            def act_split(u, dst, c0, gain=None, n=2):
                aux_filled(act, u)
                for c in range(n):
                    ins = act.activation(dst[0][:, c0 + c, :], bank(u)[:, c * S:(c + 1) * S], ACT.Copy,
                                         scale=1.0 if gain is None else gain[:, c0 + c:c0 + c + 1])
                ins.then_inc(split_hi_done, 1)

            def squares(src, dst):
                link(act.activation(junk[:, 0:src.shape[-1]], src, ACT.Square, accum_out=dst))

            def gated(n, func, r, dst=None):
                slab_made(act, n)
                j = gates[0]
                gates[0] += 1
                powered(act, r) if r in SLOT else act.wait_ge(sem("r_e_ready"), 1)
                for t in range(T):
                    scale = r_tok(r, t) if r in SLOT else r_e[:, t:t + 1]
                    ins = act.activation((gate[j % 2] if dst is None else dst)[:, t, :], acc2(n)[:, t, :], func, scale=scale)
                ins.then_inc(gate_ready if dst is None else acc_free[n % 2], 1)
                if dst is not None:
                    gates[0] -= 1

            small = sem("small_loaded")
            rows = [(stage1, C_NORM, A["norm_w"]), (stage1, C_PE, A["pe_norm_w"]), (stage1, C_ATTN, A["attn_norm_g_2"]),
                    (stage1, C_FFN, A["ffn_norm_g_2"]), (stage1, C_PLE, A["ple_norm_g_2"]), (stage1, C_LB, A["hg_lb"]),
                    (stage1, C_CONVW, A["conv_w"][0]), (stage2, C_CONVB, A["conv_b"]), (stage2, C_QN, A["q_norm_g_2"]),
                    (stage2, C_KN, A["k_norm_g_2"]), (stage2, C_BS, A["b_s_2"][0]), (stage2, C_MIX, A["ml_norm_w"]),
                    (stage2, C_MIX + 8, A["hg_norm_w"])]
            for dst, c, src in rows:
                c -= 0 if dst is stage1 else P
                flat = src.rearrange("a (r c) -> (a r) c", c=P)
                act.dma_start(dst[c:c + flat.shape[0], :], flat).then_inc(small, 16)
            for n, name in enumerate(("p", "p_2")):
                act.dma_start(ptok[n][:, :, :], A[name][0, 0].rearrange("(t p) c -> p t c", p=P)).then_inc(sem("p_loaded"), 16)
            act.dma_start(gw[0][:, :, :], view(A["w_in"][0])[:, :, MI:MI + 8]).then_inc(sem("gw_loaded"), 16)
            act.dma_start(gbias[:, 0:4], A["ml_b_i"][0].partition_broadcast(P)).then_inc(sem("gbias_loaded"), 16)
            act.dma_start(gbias[:, 4:8], A["ml_b_f"][0].partition_broadcast(P)).then_inc(sem("gbias_loaded"), 16)

            act.wait_ge(sem("lb_in"), 1)
            act.activation(lb[:, 2:4, :], lb[:, 0:2, :], ACT.Exp).then_inc(sem("lb_exp"), 1)
            for n in range(2):
                act_split(AUX[("p" if n == 0 else "p2", 0)], pT[n], 0)
            act.wait_ge(sem("gw_loaded"), 16)
            act.activation(gw[1][:, :, :], gw[0][:, :, :], ACT.Copy).then_inc(sem("gw_hi"), 1)
            act.wait_ge(sem("x_loaded"), 32)
            for i in range(8):
                act_split(AUX[("xT", i)], actA, 2 * i, gains[:, C_NORM:C_NORM + KD])
            for t in range(T):
                for c in range(4):
                    squares(resid[:, t, c * COLS:(c + 1) * COLS], ss[:, SLOT["x"], t * 4 + c:t * 4 + c + 1])
            act.sem_inc(sem("ss_x"), 1)

            g0 = SLABS[FIRST["A"]][0]
            for s in range(16):
                for p in range(8):
                    split_hi(g0 + s * 8 + p)
                    w = s * 8 + p
                    for half, L0 in ((0, 21), (1, 45)):
                        if w == L0 - 8:
                            for i in range(2):
                                u = AUX[("tr", 3 * half, i)]
                                aux_filled(act, u)
                                act.activation(Eb[1][:, i * 512:(i + 1) * 512], bank(u), ACT.Sigmoid)
                                act.activation(kF[:, i * 512:(i + 1) * 512], bank(u), ACT.Sigmoid, scale=-1.0)\
                                    .then_inc(aux_free[u % 4], 1)
                        if w == L0 - 6:
                            act.wait_ge(sem("hg_f"), half + 1)
                            act.activation(Eb[1][:, :], Eb[0][:, :], ACT.Ln).then_inc(sem("hg_logf"), 1)
                        n = w - L0
                        if 0 <= n < 8:
                            act.wait_ge(sem("hg_sub"), half * 8 + n + 1)
                            if n == 0:
                                act.activation(Eb[0][:, 0:512].rearrange("p (h t) -> p h t", h=4),
                                               bF[:, :].rearrange("p (h u t) -> p h u t", h=4, u=2)[:, :, 1, :], ACT.Exp)
                                act.activation(Eb[0][:, 512:1024], Eb[0][:, 512:1024], ACT.Exp).then_inc(sem("hg_exp"), 1)
                            else:
                                act.activation(Eb[n % 2][:, :], Eb[n % 2][:, :], ACT.Exp).then_inc(sem("hg_exp"), 1)
                        if w == L0 + 13:
                            act.wait_ge(sem("hg_out"), half + 1)
                            for t in range(T):
                                for h in range(4):
                                    c = (half * 4 + h) * P
                                    squares(ob[:, t, c:c + P], ss[:, SLOT[f"hB{half}"], t * 4 + h:t * 4 + h + 1])
                            act.sem_inc(sem("ss_hB"), 1)
                    if (s, p) in ((7, 7), (8, 7)):
                        act.wait_ge(sem("ml_conv"), s - 6)
                        x = qk[:, 4 * (s - 7):4 * (s - 6), :]
                        act.activation(x, x, ACT.Silu).then_inc(sem("ml_qk"), 1)
                    if (s, p) == (8, 1):
                        act.wait_ge(sem("ml_nf"), 1)
                        link(act.activation(gtmp[:, :, :], gtmp[:, :, :], ACT.Exp))
                        act.activation(gtmp[:, :, :], gtmp[:, :, :], ACT.Ln, bias=1.0).then_inc(sem("ml_ln"), 1)
                    if (s, p) == (9, 0):
                        act.wait_ge(sem("ml_rows"), 1)
                        act.activation(hrow[:, 5, :], hrow[:, 4, :], ACT.Exp, scale=-1.0).then_inc(sem("ml_em"), 1)
                    if (s, p) == (9, 4):
                        act.wait_ge(sem("ml_w_in"), 1)
                        act.activation(Wd[:, :, :], Wd[:, :, :], ACT.Exp).then_inc(sem("ml_w_exp"), 1)
                    if (s, p) == (11, 0):
                        act.wait_ge(sem("ml_h"), 1)
                        for t in range(T):
                            for h in range(4):
                                squares(hA[:, t, h * ML_DV:(h + 1) * ML_DV], ss[:, SLOT["hA"], t * 4 + h:t * 4 + h + 1])
                        act.sem_inc(sem("ss_hA"), 1)
                    if p == 3 and s >= 11:
                        gated(s - 1, ACT.Sigmoid if s - 1 in (12, 13) else ACT.Silu, "x")
                    if s == 15 and p == 4:
                        for i in range(4):
                            act_split(AUX[("yT", i)], actB, 2 * i, gains[:, C_MIX:C_MIX + KD])
                    if s == 15 and p == 6:
                        for i in range(4, 6):
                            act_split(AUX[("yT", i)], actB, 2 * i, gains[:, C_MIX:C_MIX + KD])

            for s in range(4):
                for p in range(8):
                    split_hi(SLABS[FIRST["C"] + s][0] + p)
                    if s == 0 and p == 3:
                        gated(FIRST["A"] + 15, ACT.Silu, "x")
                    if s == 0 and p == 4:
                        for i in range(6, 8):
                            act_split(AUX[("yT", i)], actB, 2 * i, gains[:, C_MIX:C_MIX + KD])
                    if s > 0 and p == 4:
                        act.wait_ge(sem("h_added"), s)
                        for t in range(T):
                            squares(resid[:, t, (s - 1) * COLS:s * COLS], ss[:, SLOT["h1"], t * 4 + s - 1:t * 4 + s])
                    if s > 0 and p == 5:
                        for i in range(2):
                            act_split(AUX[("hD", 2 * s - 2 + i)], actA, 4 * s - 4 + 2 * i, gains[:, C_PE:C_PE + KD])

            def d_squares(s, name, signal, count):
                act.wait_ge(sem(signal), count)
                for t in range(T):
                    squares(resid[:, t, s * COLS:(s + 1) * COLS], ss[:, SLOT[name], t * 4 + s:t * 4 + s + 1])
                act.sem_inc(sem("ss_" + name), 1)

            for s in range(4):
                split_hi(SLABS[FIRST["D"] + 2 * s][0])
                for p in range(8):
                    split_hi(SLABS[FIRST["D"] + 2 * s + 1][0] + p)
                    if s == 0 and p == 3:
                        act.wait_ge(sem("h_added"), 4)
                        for t in range(T):
                            squares(resid[:, t, 3 * COLS:4 * COLS], ss[:, SLOT["h1"], t * 4 + 3:t * 4 + 4])
                        act.sem_inc(sem("ss_h1"), 1)
                    if s == 0 and p == 4:
                        for i in range(6, 8):
                            act_split(AUX[("hD", i)], actA, 2 * i, gains[:, C_PE:C_PE + KD])
                    if s > 0:
                        if p == 2:
                            gated(FIRST["D"] + 2 * s - 1, ACT.Sigmoid, "h1")
                        if p == 4:
                            d_squares(s - 1, "f1", "h_gated", s)
                        if p == 6:
                            d_squares(s - 1, "f2", "h_final", s)
                        if p == 7:
                            for i in range(2):
                                act_split(AUX[("hE", 2 * s - 2 + i)], actB, 4 * s - 4 + 2 * i, gains[:, C_ATTN:C_ATTN + KD])

            for s in range(10):
                for p in range(8):
                    n = FIRST["E1"] + s
                    split_hi(SLABS[n][0] + p)
                    w = s * 8 + p
                    if s == 0:
                        if p == 3:
                            gated(n - 1, ACT.Sigmoid, "h1")
                        if p == 4:
                            d_squares(3, "f1", "h_gated", 4)
                        if p == 5:
                            d_squares(3, "f2", "h_final", 4)
                        if p == 6:
                            for i in range(6, 8):
                                act_split(AUX[("hE", i)], actB, 2 * i, gains[:, C_ATTN:C_ATTN + KD])
                    if 1 <= s <= 4 and p == 4:
                        act.wait_ge(sem("qk_tok"), s)
                        for t in range(T):
                            for h in range(4):
                                squares(gate[(s - 1) % 2][:, t, h * P:(h + 1) * P],
                                        ss[:, SLOT[f"qk{s - 1}"], t * 4 + h:t * 4 + h + 1])
                        act.sem_inc(sem("ss_qk"), 1)
                    for b, z0 in ((0, 45), (1, 58)):
                        if w == z0 + 1:
                            act.wait_ge(sem("att_z"), b + 1)
                            link(act.activation(ab[:, :, :], zt[:, :, :], ACT.Abs))
                            link(act.activation(ab[:, :, :], ab[:, :, :], ACT.Exp, scale=-1.0))
                        if w == z0 + 2:
                            act.activation(ab[:, :, :], ab[:, :, :], ACT.Ln, bias=1.0).then_inc(sem("att_ln"), 1)
                        if w == z0 + 8:
                            act.wait_ge(sem("att_arg"), b + 1)
                            act.activation(zt[:, :, :], zt[:, :, :], ACT.Exp).then_inc(sem("att_w"), 1)
                    if s in (7, 8) and p == 3:
                        gated(n - 1, ACT.Gelu_apprx_tanh, "r_e", vs[:, :, (s - 7) * COLS:(s - 6) * COLS])
                    if s == 9 and p == 3:
                        gated(n - 1, ACT.Gelu_apprx_tanh, "r_e", u2[:, :, 0:COLS])
                    if s in (7, 8) and p == 4:
                        slab_taken(act, n - 1)
                        for t in range(T):
                            for h in range(4):
                                c = ((s - 7) * 4 + h) * P
                                squares(vs[:, t, c:c + P], ss[:, SLOT[f"s{s - 7}"], t * 4 + h:t * 4 + h + 1])
                        act.sem_inc(sem("ss_s"), 1)
                    if s == 9 and p == 7:
                        for i in range(2):
                            act_split(AUX[("yaT", i)], actA, 2 * i)

            for ph in ("E2", "E3"):
                for s in range(8):
                    n = FIRST[ph] + s
                    for p in range(SLABS[n][1]):
                        split_hi(SLABS[n][0] + p)
                        if p == 3 and ph == "E2" and s == 0:
                            gated(n - 1, ACT.Gelu_apprx_tanh, "r_e", u2[:, :, COLS:2 * COLS])
                        if p == 3 and s % 2 == 1:
                            gated(n - 1, ACT.Sigmoid, "r_e")
                        if ph == "E2" and s == 0 and p == 6:
                            for i in range(2, 4):
                                act_split(AUX[("yaT", i)], actA, 2 * i)
                        if ph == "E2" and s == 0 and p == 7:
                            for i in range(4):
                                act_split(AUX[("ybT", i)], actA, 8 + 2 * i)
                        if ph == "E3" and s >= 2 and s % 2 == 0 and p == 6:
                            for i in range(2):
                                act_split(AUX[("mT", s - 2 + i)], actF, 2 * (s - 2 + i))

            def added_squares(s, name, count):
                act.wait_ge(sem("h_added"), count)
                for t in range(T):
                    squares(resid[:, t, s * COLS:(s + 1) * COLS], ss[:, SLOT[name], t * 4 + s:t * 4 + s + 1])

            for s in range(4):
                for p in range(8):
                    split_hi(SLABS[FIRST["G"] + s][0] + p)
                    if s == 0 and p == 5:
                        for i in range(6, 8):
                            act_split(AUX[("mT", i)], actF, 2 * i)
                    if s > 0 and p == 4:
                        added_squares(s - 1, "ffn", 4 + s)
                    if s > 0 and p == 5:
                        for i in range(2):
                            act_split(AUX[("hH", 2 * s - 2 + i)], actA, 4 * s - 4 + 2 * i, gains[:, C_FFN:C_FFN + KD])

            for part, (f0, width) in enumerate(FFN_PARTS):
                nh = width // COLS
                for s in range(2 * nh):
                    n = FIRST[f"H{part}"] + s
                    for p in range(8):
                        split_hi(SLABS[n][0] + p)
                        if s == 0 and part == 0:
                            if p == 4:
                                added_squares(3, "ffn", 8)
                                act.sem_inc(sem("ss_ffn"), 1)
                            if p == 5:
                                for i in range(6, 8):
                                    act_split(AUX[("hH", i)], actA, 2 * i, gains[:, C_FFN:C_FFN + KD])
                        if s % 2 == 1 and p == 3:
                            gated(n - 1, ACT.Silu, "ffn")
                        if s > 0 and s % 2 == 0 and p == 6:
                            for c in range(4):
                                act_split(AUX[("hid", part, 2 * s - 4 + c)], actF, 2 * s - 4 + c, n=1)
                for s in range(4):
                    n = FIRST[f"O{part}"] + s
                    for p in range(SLABS[n][1]):
                        split_hi(SLABS[n][0] + p)
                        if s == 0 and p == 4:
                            for c in range(4):
                                act_split(AUX[("hid", part, 4 * nh - 4 + c)], actF, 4 * nh - 4 + c, n=1)
                        if part == 2 and s > 0 and p == 4:
                            added_squares(s - 1, "ple", 16 + s)
                        if part == 2 and s > 0 and p == 5:
                            for i in range(2):
                                act_split(AUX[("hJ", 2 * s - 2 + i)], actB, 4 * s - 4 + 2 * i, gains[:, C_PLE:C_PLE + KD])

            for s in range(4):
                split_hi(SLABS[FIRST["J"] + 2 * s][0])
                for p in range(8):
                    split_hi(SLABS[FIRST["J"] + 2 * s + 1][0] + p)
                    if s == 0 and p == 3:
                        added_squares(3, "ple", 20)
                        act.sem_inc(sem("ss_ple"), 1)
                    if s == 0 and p == 4:
                        for i in range(6, 8):
                            act_split(AUX[("hJ", i)], actB, 2 * i, gains[:, C_PLE:C_PLE + KD])
                    if s > 0 and p == 2:
                        gated(FIRST["J"] + 2 * s - 1, ACT.Sigmoid, "ple")
            gated(FIRST["J"] + 7, ACT.Sigmoid, "ple")

        @block.tensor
        def _(pe):
            def transposes(name, src, c0, n=2):
                u = AUX[name]
                free(u)
                for c in range(n):
                    for t in range(T):
                        ins = pe.transpose(bank(u)[:, c * S + t * P:c * S + (t + 1) * P],
                                           src[:, t, (c0 + c) * P:(c0 + c + 1) * P], ident[:, :])
                ins.then_inc(aux_full, 1)

            def free(u):
                if u >= 4:
                    aux_taken(pe, u - 4)

            def piece(n, p, act, k, last):
                g = SLABS[n][0] + p
                if p == 0 and n >= 2:
                    slab_taken(pe, n - 2)
                pe.wait_ge(hi_ready, g + 1)
                for c in range(PK):
                    for t in range(T):
                        for x in range(2):
                            pe.matmul(acc2(n)[:, t, :], act[x][:, k + c, t * P:(t + 1) * P], whi[:, g % RING, c, :],
                                      start=(p == 0 and c == 0 and x == 0), stop=False)
                pe.wait_ge(lo_ready, g + 1)
                for c in range(PK):
                    for t in range(T):
                        ins = pe.matmul(acc2(n)[:, t, :], act[0][:, k + c, t * P:(t + 1) * P], wlo[:, g % RING, c, :],
                                        start=False, stop=(last and c == PK - 1))
                ins.then_inc(piece_used, 1)

            pe.wait_ge(sem("consts_ready"), 1)
            pe.wait_ge(sem("small_loaded"), 16 * 13)
            pe.transpose(bank(0)[:, 0:P], stage1[:, :], ident[:, :])
            pe.transpose(bank(0)[:, P:C_END], stage2[:, :], ident[0:C_END - P, 0:C_END - P]).then_inc(aux_full, 1)
            pe.wait_ge(sem("p_loaded"), 32)
            transposes(("p", 0), ptok[0], 0)
            transposes(("p2", 0), ptok[1], 0)
            pe.wait_ge(sem("x_loaded"), 32)
            for i in range(8):
                transposes(("xT", i), resid, 2 * i)

            def tr_slab(s):
                n = FIRST["A"] + s
                slab_taken(pe, n)
                for i in range(2):
                    transposes(("tr", s, i), gate[s % 2], 2 * i)

            def hg_diag(half):
                pe.wait_ge(sem("hg_k"), half + 1)
                aux_taken(pe, AUX[("tr", 3 * half + 1, 1)])
                for i in range(2):
                    u = AUX[("diag", half, i)]
                    free(u)
                    for j in range(4):
                        c = (4 * i + j) * P
                        ins = pe.matmul(bank(u)[:, j * P:(j + 1) * P], kF[:, c:c + P], qF[:, c:c + P], start=True, stop=True)
                    ins.then_inc(aux_full, 1)

            def hg_level(half, n):
                u = AUX[("level", half, n)]
                pe.wait_ge(sem("hg_mul"), half * 8 + n + 1)
                free(u)
                for j in range(4 if n == 0 else 8):
                    m = P if n == 0 else 64
                    c = (2 * j if n == 0 else j) * P
                    ins = pe.matmul(bank(u)[:, j * m:(j + 1) * m], Kp[n % 2][:, c:c + P], Qp[n % 2][:, j * m:(j + 1) * m],
                                    start=True, stop=True)
                ins.then_inc(aux_full, 1)

            def hg_pv(half):
                aux_taken(pe, AUX[("level", half, 7)])
                slab_taken(pe, FIRST["A"] + 2 + 3 * half)
                for t in range(T):
                    u = AUX[("pv", half, t)]
                    free(u)
                    for h in range(4):
                        c = (half * 4 + h) * P
                        o = bank(u)[:, h * P:(h + 1) * P]
                        if t == 1:
                            pe.matmul(o, A01[:, h, :], ob[:, 0, c:c + P], start=True, stop=False)
                        ins = pe.matmul(o, Am[:, 2 * h + t, :], ob[:, t, c:c + P], start=(t == 0), stop=True)
                    ins.then_inc(aux_full, 1)

            def ml_gates():
                u = AUX[("gates", 0)]
                pe.wait_ge(sem("gw_lo"), 1)
                free(u)
                for t in range(T):
                    o = bank(u)[:, t * 8:(t + 1) * 8]
                    for k in range(KD):
                        for x, w in ((0, 1), (1, 1), (0, 2)):
                            ins = pe.matmul(o, actA[x][:, k, t * P:(t + 1) * P], gw[w][:, k, :],
                                            start=(k == 0 and (x, w) == (0, 1)), stop=(k == KD - 1 and w == 2))
                ins.then_inc(aux_full, 1)

            def ml_gates_tr():
                u = AUX[("gtr", 0)]
                pe.wait_ge(sem("ml_lf"), 1)
                free(u)
                for x in range(2):
                    for t in range(T):
                        ins = pe.transpose(aux[0:4, u % 4, x * S + t * P:x * S + (t + 1) * P], gtok[:, t, 4 * x:4 * x + 4],
                                           ident[:, :])
                ins.then_inc(aux_full, 1)

            def ml_cols():
                u = AUX[("atr", 0)]
                pe.wait_ge(sem("ml_em"), 1)
                free(u)
                for x, row in ((0, 1), (1, 5)):
                    for t in range(T):
                        ins = pe.transpose(bank(u)[:, x * 8 + t * 4:x * 8 + t * 4 + 4], hrow[:, row, t * P:(t + 1) * P],
                                           ident[0:4, 0:4])
                ins.then_inc(aux_full, 1)
                for i in range(2):
                    u = AUX[("bc", i)]
                    free(u)
                    for h in range(2):
                        ins = pe.matmul(bank(u)[:, h * S:(h + 1) * S], sel[:, 2 * i + h, :], hrow[:, 3, :], start=True, stop=True)
                    ins.then_inc(aux_full, 1)

            def ml_scores():
                pe.wait_ge(sem("ml_qk"), 2)
                for h in range(4):
                    u = AUX[("st", h)]
                    free(u)
                    pe.matmul(bank(u)[:, 0:S], qk[:, 4 + h, 0:P], qk[:, h, :], start=True, stop=True)
                    pe.matmul(bank(u)[:, S:S + P], qk[:, 4 + h, P:S], qk[:, h, P:S], start=True, stop=True).then_inc(aux_full, 1)

            def ml_pv(h):
                aux_taken(pe, AUX[("st", h)])
                slab_taken(pe, FIRST["A"] + 8 + h // 2)
                for t in range(T):
                    u = AUX[("mpv", h, t)]
                    free(u)
                    o = bank(u)[:, 0:ML_DV + 1]
                    if t == 0:
                        ins = pe.matmul(o, Wd[:, h, 0:P], vml[:, 0, h, 0:ML_DV + 1], start=True, stop=True)
                    else:
                        pe.matmul(o, Wd[:, h, P:S], vml[:, 0, h, 0:ML_DV + 1], start=True, stop=False)
                        ins = pe.matmul(o, Wd[:, h, S:S + P], vml[:, 1, h, 0:ML_DV + 1], start=False, stop=True)
                    ins.then_inc(aux_full, 1)

            for s in range(16):
                n = FIRST["A"] + s
                for p in range(8):
                    if s == 0:
                        aux_taken(pe, AUX[("xT", p)])
                    piece(n, p, actA, p * PK, p == 7)
                    w = s * 8 + p
                    if p == 0 and s - 1 in (0, 1, 3, 4, 6, 7):
                        tr_slab(s - 1)
                    for half, L0 in ((0, 21), (1, 45)):
                        if w == L0 - 3:
                            hg_diag(half)
                        if 0 <= w - (L0 - 2) < 8:
                            hg_level(half, w - (L0 - 2))
                        if w == L0 + 7:
                            hg_pv(half)
                    if (s, p) == (7, 4):
                        ml_gates()
                    if (s, p) == (8, 2):
                        ml_gates_tr()
                    if (s, p) == (8, 6):
                        ml_cols()
                    if (s, p) == (9, 2):
                        ml_scores()
                    if s == 10 and 1 <= p <= 4:
                        ml_pv(p - 1)
                    if (s, p) == (15, 0):
                        pe.wait_ge(sem("ya_ready"), 1)
                        for i in range(4):
                            transposes(("yT", i), hA, 2 * i)
                    if (s, p) == (15, 2):
                        pe.wait_ge(sem("yb_ready"), 1)
                        for i in range(4, 6):
                            transposes(("yT", i), ob, 2 * i - 8)

            for s in range(4):
                n = FIRST["C"] + s
                for p in range(8):
                    if s == 0:
                        aux_taken(pe, AUX[("yT", p)])
                    piece(n, p, actB, p * PK, p == 7)
                    if s == 0 and p == 0:
                        pe.wait_ge(sem("yb_ready"), 2)
                        for i in range(6, 8):
                            transposes(("yT", i), ob, 2 * i - 8)
                    if s > 0 and p == 1:
                        pe.wait_ge(sem("h_added"), s)
                        for i in range(2):
                            transposes(("hD", 2 * s - 2 + i), resid, 4 * s - 4 + 2 * i)

            for s in range(4):
                n = FIRST["D"] + 2 * s
                piece(n, 0, pT[0], 0, True)
                if s == 0:
                    pe.wait_ge(sem("h_added"), 4)
                    for i in range(6, 8):
                        transposes(("hD", i), resid, 2 * i)
                for p in range(8):
                    if s == 0:
                        aux_taken(pe, AUX[("hD", p)])
                    piece(n + 1, p, actA, p * PK, p == 7)
                    if s > 0 and p == 3:
                        pe.wait_ge(sem("h_final"), s)
                        for i in range(2):
                            transposes(("hE", 2 * s - 2 + i), resid, 4 * s - 4 + 2 * i)

            def tr2_slab(s):
                pe.wait_ge(sem("qk_normed"), s + 1)
                for i in range(2):
                    transposes(("tr2", s, i), gate[s % 2], 2 * i)

            def spatial_weights():
                pe.wait_ge(sem("ws_masked"), 1)
                for i in range(2):
                    u = AUX[("ws", i)]
                    free(u)
                    for j in range(4):
                        ins = pe.transpose(bank(u)[:, j * P:(j + 1) * P], wsr[:, 4 * i + j, :], ident[:, :])
                    ins.then_inc(aux_full, 1)

            def att_scores(b):
                aux_taken(pe, AUX[("tr2", 1 if b else 0, 1)])
                aux_taken(pe, AUX[("tr2", 3 if b else 2, 1)])
                for j in range(4):
                    u, h = AUX[("z", b, j)], 4 * b + j
                    free(u)
                    pe.matmul(bank(u)[:, 0:S], kT[:, h, 0:P], qT[:, h, :], start=True, stop=True)
                    pe.matmul(bank(u)[:, S:S + P], kT[:, h, P:S], qT[:, h, P:S], start=True, stop=True).then_inc(aux_full, 1)

            def att_tail(b):
                pe.wait_ge(sem("att_l"), b + 1)
                for j in range(4):
                    u = AUX[("tail", b, j)]
                    free(u)
                    o = bank(u)
                    pe.matmul(o[:, 0:S], later[:, :], Lp[:, j, 0:S], start=True, stop=False)
                    pe.matmul(o[:, P:S], ones[:, 0:P], Lp[:, j, S:S + P], start=False, stop=True)
                    pe.matmul(o[:, S:S + P], later[:, :], Lp[:, j, S:S + P], start=True, stop=True).then_inc(aux_full, 1)

            def att_pv(b):
                pe.wait_ge(sem("att_masked"), b + 1)
                slab_taken(pe, FIRST["E1"] + 4 + b)
                for t in range(T):
                    u = AUX[("att", b, t)]
                    free(u)
                    for j in range(4):
                        c = (4 * b + j) * P
                        o = bank(u)[:, j * P:(j + 1) * P]
                        if t == 0:
                            ins = pe.matmul(o, zt[:, j, 0:P], vA[:, 0, c:c + P], start=True, stop=True)
                        else:
                            pe.matmul(o, zt[:, j, P:S], vA[:, 0, c:c + P], start=True, stop=False)
                            ins = pe.matmul(o, zt[:, j, S:S + P], vA[:, 1, c:c + P], start=False, stop=True)
                    ins.then_inc(aux_full, 1)

            def spatial_mix(half):
                pe.wait_ge(sem("vs_ready"), half + 1)
                for i in range(2):
                    u = AUX[("sgu", 2 * half + i)]
                    free(u)
                    for j in range(2):
                        g = 4 * half + 2 * i + j
                        ins = pe.matmul(bank(u)[:, j * S:(j + 1) * S].rearrange("p (t c) -> p t c", t=T), wsT[:, g, :],
                                        vs[:, :, g * P:(g + 1) * P], start=True, stop=True)
                    ins.then_inc(aux_full, 1)

            for s in range(10):
                n = FIRST["E1"] + s
                for p in range(8):
                    if s == 0:
                        aux_taken(pe, AUX[("hE", p)])
                    piece(n, p, actB, p * PK, p == 7)
                    w = s * 8 + p
                    if s == 0 and p == 2:
                        pe.wait_ge(sem("h_final"), 4)
                        for i in range(6, 8):
                            transposes(("hE", i), resid, 2 * i)
                    if 1 <= s <= 4 and p == 3:
                        tr2_slab(s - 1)
                    if (s, p) == (2, 1):
                        spatial_weights()
                    for b, z0 in ((0, 45), (1, 58)):
                        if w == z0 - 3:
                            att_scores(b)
                        if w == z0 + 1:
                            att_tail(b)
                        if w == z0 + 7:
                            att_pv(b)
                    if (s, p) == (9, 1):
                        spatial_mix(0)
                    if (s, p) == (9, 3):
                        pe.wait_ge(sem("ya2_ready"), 1)
                        for i in range(2):
                            transposes(("yaT", i), u2, 2 * i)

            for ph in ("E2", "E3"):
                for s in range(8):
                    n = FIRST[ph] + s
                    for p in range(SLABS[n][1]):
                        if s % 2 == 0:
                            piece(n, p, actB, p * PK, p == 7)
                        else:
                            if s == 1:
                                aux_taken(pe, AUX[("yaT" if ph == "E2" else "ybT", p)])
                            piece(n, p, actA, (0 if ph == "E2" else 8) + p * PK, p == 3)
                        if ph == "E2" and s == 0:
                            if p == 0:
                                spatial_mix(1)
                            if p == 3:
                                pe.wait_ge(sem("ya2_ready"), 2)
                                for i in range(2, 4):
                                    transposes(("yaT", i), u2, 2 * i)
                            if p == 4:
                                for i in range(4):
                                    aux_taken(pe, AUX[("att", i // 2, 1)])
                                    transposes(("ybT", i), vA, 2 * i)
                        if ph == "E3" and s >= 2 and s % 2 == 0 and p == 1:
                            pe.wait_ge(sem("merged_ready"), s // 2)
                            for i in range(2):
                                transposes(("mT", s - 2 + i), merged, 2 * (s - 2 + i))

            for s in range(4):
                n = FIRST["G"] + s
                for p in range(8):
                    if s == 0:
                        aux_taken(pe, AUX[("mT", p)])
                    piece(n, p, actF, p * PK, p == 7)
                    if s == 0 and p == 1:
                        pe.wait_ge(sem("merged_ready"), 4)
                        for i in range(6, 8):
                            transposes(("mT", i), merged, 2 * i)
                    if s > 0 and p == 1:
                        pe.wait_ge(sem("h_added"), 4 + s)
                        for i in range(2):
                            transposes(("hH", 2 * s - 2 + i), resid, 4 * s - 4 + 2 * i)

            def tr_hidden(part, j):
                pe.wait_ge(sem("hid_ready"), sum(w // COLS for _, w in FFN_PARTS[:part]) + j + 1)
                for c in range(4):
                    transposes(("hid", part, 4 * j + c), hid, c, n=1)

            for part, (f0, width) in enumerate(FFN_PARTS):
                nh = width // COLS
                for s in range(2 * nh):
                    n = FIRST[f"H{part}"] + s
                    for p in range(8):
                        if s == 0 and part == 0:
                            aux_taken(pe, AUX[("hH", p)])
                        piece(n, p, actA, p * PK, p == 7)
                        if s == 0 and part == 0 and p == 1:
                            pe.wait_ge(sem("h_added"), 8)
                            for i in range(6, 8):
                                transposes(("hH", i), resid, 2 * i)
                        if s > 0 and s % 2 == 0 and p == 1:
                            tr_hidden(part, s // 2 - 1)
                for s in range(4):
                    n = FIRST[f"O{part}"] + s
                    for p in range(2 * nh):
                        if s == 0:
                            aux_taken(pe, AUX[("hid", part, 2 * p)])
                            aux_taken(pe, AUX[("hid", part, 2 * p + 1)])
                        piece(n, p, actF, p * PK, p == 2 * nh - 1)
                        if s == 0 and p == 1:
                            tr_hidden(part, nh - 1)
                        if part == 2 and s > 0 and p == 1:
                            pe.wait_ge(sem("h_added"), 16 + s)
                            for i in range(2):
                                transposes(("hJ", 2 * s - 2 + i), resid, 4 * s - 4 + 2 * i)

            for s in range(4):
                n = FIRST["J"] + 2 * s
                piece(n, 0, pT[1], 0, True)
                if s == 0:
                    pe.wait_ge(sem("h_added"), 20)
                    for i in range(6, 8):
                        transposes(("hJ", i), resid, 2 * i)
                for p in range(8):
                    if s == 0:
                        aux_taken(pe, AUX[("hJ", p)])
                    piece(n + 1, p, actB, p * PK, p == 7)

        @block.vector
        def _(dve):
            steps = [0]
            gates = [0]

            def link(ins):
                steps[0] += 1
                ins.then_inc(sem("dve_step"), 1)
                dve.wait_ge(sem("dve_step"), steps[0])

            def split_lo(g):
                dve.wait_ge(hi_ready, g + 1)
                dve.tensor_tensor(wlo[:, g % RING], raw[:, g % RING], whi[:, g % RING].bitcast(F32), ALU.subtract)\
                    .then_inc(lo_ready, 1)

            splits = [0]

            def lo_split(u, dst, c0, gain=None, n=2):
                splits[0] += 1
                dve.wait_ge(split_hi_done, splits[0])
                for c in range(n):
                    x = bank(u)[:, c * S:(c + 1) * S]
                    hi = dst[0][:, c0 + c, :].bitcast(F32)
                    if gain is None:
                        ins = dve.tensor_tensor(dst[1][:, c0 + c, :], x, hi, ALU.subtract)
                    else:
                        ins = dve.scalar_tensor_tensor(out=dst[1][:, c0 + c, :], in0=x, scalar=gain[:, c0 + c:c0 + c + 1],
                                                       in1=hi, op0=ALU.mult, op1=ALU.subtract)
                ins.then_inc(aux_free[u % 4], 1)

            def variance(name, width, sums=None):
                i, n = SLOT[name], dict(POWS)[name]
                dve.tensor_scalar(var[:, i, 0:n], ss[:, i, 0:n] if sums is None else sums, 1.0 / width, EPS, ALU.mult, ALU.add)\
                    .then_inc(pow_in, 1)

            def row_variance(name):
                i = SLOT[name]
                link(dve.tensor_reduce(var[:, i, 4:6], ss[:, i, :].rearrange("p (t c) -> p t c", t=T), AX.X, ALU.add))
                variance(name, D, var[:, i, 4:6])

            def scaled(n, dst, r):
                slab_made(dve, n)
                for t in range(T):
                    x = acc2(n)[:, t, :]
                    d = dst[:, t]
                    if len(d.shape) == 3:
                        x = x.rearrange("p (h c) -> p h c", h=d.shape[1])
                    ins = dve.tensor_scalar(d, x, r(t), None, ALU.mult)
                return ins

            def next_gate():
                gates[0] += 1
                dve.wait_ge(gate_ready, gates[0])
                return gate[(gates[0] - 1) % 2]

            aux_filled(dve, 0)
            dve.tensor_copy(gains[:, :], bank(0, C_END)).then_inc(aux_free[0], 1)
            aux_taken(dve, 0)
            dve.tensor_scalar(qn_scaled[:, :], gains[:, C_QN:C_QN + 1], SB_D ** -0.5, None, ALU.mult)
            lb_rows = gains[:, C_LB:C_LB + 16].rearrange("p (l h) -> p l h", l=2)
            link(dve.tensor_tensor(lb[:, 2, :], lb_rows[:, 0, :], lb_rows[:, 1, :], ALU.max))
            dve.tensor_tensor(lb[:, 0:2, :], lb_rows, lb[:, 2:3, :].to_broadcast([P, 2, 8]), ALU.subtract).then_inc(sem("lb_in"), 1)
            dve.memset(Kp[0][:, :], 0.0)
            dve.memset(Kp[1][:, :], 0.0)
            dve.wait_ge(sem("lb_exp"), 1)
            link(dve.tensor_tensor(lb[:, 0, :], lb[:, 2, :], lb[:, 3, :], ALU.add))
            link(dve.reciprocal(lb[:, 1, :], lb[:, 0, :]))
            link(dve.tensor_tensor(lb[:, 0, :], lb[:, 2, :], lb[:, 1, :], ALU.mult))
            link(dve.tensor_scalar(lb[:, 1, :], lb[:, 0, :], -1.0, 1.0, ALU.mult, ALU.add))
            for n in range(2):
                lo_split(AUX[("p" if n == 0 else "p2", 0)], pT[n], 0)
            dve.wait_ge(sem("gw_hi"), 1)
            dve.tensor_tensor(gw[2][:, :, :], gw[0][:, :, :], gw[1][:, :, :].bitcast(F32), ALU.subtract).then_inc(sem("gw_lo"), 1)
            for i in range(8):
                lo_split(AUX[("xT", i)], actA, 2 * i, gains[:, C_NORM:C_NORM + KD])

            def hg_forget(half):
                aux_taken(dve, AUX[("tr", 3 * half, 1)])
                for h in range(4):
                    c = slice(h * S, (h + 1) * S)
                    e = half * 4 + h
                    ins = dve.tensor_scalar(Eb[0][:, c], Eb[1][:, c], lb[:, 1, e:e + 1], lb[:, 0, e:e + 1], ALU.mult, ALU.add)
                ins.then_inc(sem("hg_f"), 1)

            def hg_cumsum(half):
                dve.wait_ge(sem("hg_logf"), half + 1)
                for h in range(4):
                    e = half * 4 + h
                    c = slice(h * S, (h + 1) * S)
                    ins = dve.tensor_scalar(kF[:, c], kF[:, c], lb[:, 1, e:e + 1], None, ALU.mult)
                ins.then_inc(sem("hg_k"), 1)
                for j in range(8):
                    c = slice(j * P, (j + 1) * P)
                    ins = dve.tensor_tensor_scan(bF[:, c], ones[:, 0:P], Eb[1][:, c], 0.0, ALU.mult, ALU.add)
                link(ins)

            def hg_queries(half):
                for i in range(2):
                    u = AUX[("tr", 3 * half + 1, i)]
                    aux_filled(dve, u)
                    dve.tensor_copy(qF[:, i * 512:(i + 1) * 512], bank(u)).then_inc(aux_free[u % 4], 1)

            def hg_diagonal(half):
                for i in range(2):
                    u = AUX[("diag", half, i)]
                    aux_filled(dve, u)
                    dve.tensor_tensor(Am[:, 4 * i:4 * i + 4, :], bank(u).rearrange("p (g t) -> p g t", g=4),
                                      ident[:, :].unsqueeze(1).to_broadcast([P, 4, P]), ALU.mult).then_inc(aux_free[u % 4], 1)

            def halves(x, s):
                return x[:, :].rearrange("p (n u s) -> p n u s", u=2, s=s)

            def hg_sub(half, n):
                s = LEVELS[n]
                b, nb = halves(bF, s), 512 // s
                mid = b[:, :, 0, s - 1:s].to_broadcast([P, nb, s])
                e = Eb[n % 2][:, :].rearrange("p (x n s) -> p x n s", x=2, s=s)
                if n > 0:
                    dve.tensor_tensor(e[:, 0], b[:, :, 1, :], mid, ALU.subtract)
                dve.tensor_tensor(e[:, 1], mid, b[:, :, 0, :], ALU.subtract).then_inc(sem("hg_sub"), 1)

            def hg_mul(half, n):
                s = LEVELS[n]
                dve.wait_ge(sem("hg_exp"), half * 8 + n + 1)
                if n >= 2:
                    aux_filled(dve, AUX[("level", half, n - 2)])
                e = Eb[n % 2][:, :].rearrange("p (x n s) -> p x n s", x=2, s=s)
                dve.tensor_tensor(Qp[n % 2][:, :].rearrange("p (n s) -> p n s", s=s), halves(qF, s)[:, :, 1, :], e[:, 0], ALU.mult)
                dve.tensor_tensor(halves(Kp[n % 2], s)[:, :, 0, :], halves(kF, s)[:, :, 0, :], e[:, 1], ALU.mult)\
                    .then_inc(sem("hg_mul"), 1)

            def hg_take(half, n):
                s = LEVELS[n]
                u = AUX[("level", half, n)]
                aux_filled(dve, u)
                if n == 0:
                    ins = dve.tensor_copy(A01[:, :, :], bank(u).rearrange("p (h t) -> p h t", h=4))
                else:
                    nb = 64 // s
                    dst = Am[:, :, :].rearrange("p g (n u s) -> p g n u s", u=2, s=s)[:, :, :, 1, :]
                    m = lmask[:, n - 1, :].bitcast(I32).rearrange("p (n s) -> p n s", s=s).unsqueeze(1).to_broadcast([P, 8, nb, s])
                    ins = dve.copy_predicated(dst, m, bank(u).rearrange("p (g n s) -> p g n s", g=8, s=s))
                ins.then_inc(aux_free[u % 4], 1)

            def hg_output(half):
                aux_filled(dve, AUX[("pv", half, 1)])
                for t in range(T):
                    u = AUX[("pv", half, t)]
                    dve.tensor_copy(ob[:, t, half * 512:(half + 1) * 512], bank(u)).then_inc(aux_free[u % 4], 1)
                for t in range(T):
                    aux_taken(dve, AUX[("pv", half, t)])
                dve.sem_inc(sem("hg_out"), 1)

            def ml_conv(s):
                for i in range(2):
                    u = AUX[("tr", s, i)]
                    aux_filled(dve, u)
                    for tap in range(ML_TAPS - 1, -1, -1):
                        back = ML_TAPS - 1 - tap
                        for c in range(2):
                            ch = 4 * (s - 6) + 2 * i + c
                            x, y = bank(u)[:, c * S:(c + 1) * S], qk[:, ch, :]
                            w = gains[:, C_CONVW + tap * 8 + ch:C_CONVW + tap * 8 + ch + 1]
                            if back == 0:
                                ins = dve.tensor_scalar(y, x, w, gains[:, C_CONVB + ch:C_CONVB + ch + 1], ALU.mult, ALU.add)
                            else:
                                ins = dve.scalar_tensor_tensor(out=y[:, back:S], in0=x[:, 0:S - back], scalar=w,
                                                               in1=y[:, back:S], op0=ALU.mult, op1=ALU.add)
                            if tap > 0 and c == 1:
                                link(ins)
                    ins.then_inc(aux_free[u % 4], 1)
                    aux_taken(dve, u)
                dve.sem_inc(sem("ml_conv"), 1)

            def ml_gates():
                u = AUX[("gates", 0)]
                aux_filled(dve, u)
                dve.wait_ge(sem("gbias_loaded"), 32)
                for t in range(T):
                    ins = dve.scalar_tensor_tensor(out=gtok[:, t, :], in0=bank(u)[:, t * 8:(t + 1) * 8], scalar=r_tok("x", t),
                                                   in1=gbias[:, :], op0=ALU.mult, op1=ALU.add)
                ins.then_inc(aux_free[u % 4], 1)
                aux_taken(dve, u)
                f = gtok[:, :, 4:8]
                dve.scalar_tensor_tensor(out=gtmp[:, :, :], in0=f, scalar=-1.0, in1=f, op0=ALU.mult, op1=ALU.min)\
                    .then_inc(sem("ml_nf"), 1)

            def ml_logf():
                f = gtok[:, :, 4:8]
                dve.wait_ge(sem("ml_ln"), 1)
                dve.scalar_tensor_tensor(out=f, in0=f, scalar=0.0, in1=gtmp[:, :, :], op0=ALU.min, op1=ALU.subtract)\
                    .then_inc(sem("ml_lf"), 1)

            def ml_rows():
                u = AUX[("gtr", 0)]
                aux_filled(dve, u)
                gi, lf = aux[0:4, u % 4, 0:S], aux[0:4, u % 4, S:2 * S]
                link(dve.tensor_tensor_scan(hrow[:, 0, :], ones[0:4, :], lf, 0.0, ALU.mult, ALU.add))
                dve.tensor_tensor(hrow[:, 1, :], gi, hrow[:, 0, :], ALU.subtract).then_inc(aux_free[u % 4], 1)
                aux_taken(dve, u)
                link(dve.tensor_tensor_scan(hrow[:, 2, :], ones[0:4, :], hrow[:, 1, :], 0.0, ALU.mult, ALU.max))
                dve.tensor_scalar(hrow[:, 3, :], hrow[:, 2, :], -1.0, None, ALU.mult)
                dve.tensor_tensor(hrow[:, 4, :], hrow[:, 0, :], hrow[:, 2, :], ALU.add).then_inc(sem("ml_rows"), 1)

            def ml_weights():
                u = AUX[("atr", 0)]
                aux_filled(dve, u)
                dve.tensor_copy(acol[:, :], bank(u, 16)).then_inc(aux_free[u % 4], 1)
                aux_taken(dve, u)
                for i in range(2):
                    u = AUX[("bc", i)]
                    aux_filled(dve, u)
                    for j in range(2):
                        h = 2 * i + j
                        x = bank(u)[:, j * S:(j + 1) * S]
                        dve.tensor_scalar(Wd[:, h, 0:S], x, acol[:, h:h + 1], 0.0, ALU.add, ALU.min)
                        ins = dve.tensor_scalar(Wd[:, h, S:S + P], x[:, P:S], acol[:, 4 + h:5 + h], 0.0, ALU.add, ALU.min)
                    ins.then_inc(aux_free[u % 4], 1)
                aux_taken(dve, AUX[("bc", 1)])
                dve.sem_inc(sem("ml_w_in"), 1)

            def diagonal_blocks(x):
                return x[:, :, :].rearrange("p h (b t) -> p h b t", b=3)[:, :, 0:3:2, :]

            def ml_mask():
                dve.wait_ge(sem("ml_w_exp"), 1)
                d = diagonal_blocks(Wd)
                link(dve.tensor_tensor(d, d, causal[:, :].unsqueeze(1).unsqueeze(1).to_broadcast([P, 4, 2, P]), ALU.mult))
                dve.memset(vml[:, :, :, ML_DV:ML_DV + 2], 1.0)

            def ml_scores():
                for h in range(4):
                    u = AUX[("st", h)]
                    aux_filled(dve, u)
                    dve.scalar_tensor_tensor(out=Wd[:, h, :], in0=bank(u, 384), scalar=ML_DQK ** -0.5, in1=Wd[:, h, :],
                                             op0=ALU.mult, op1=ALU.mult).then_inc(aux_free[u % 4], 1)

            def ml_output(h):
                for t in range(T):
                    u = AUX[("mpv", h, t)]
                    aux_filled(dve, u)
                    d = den[:, h * 2 + t, :]
                    dn = bank(u)[:, ML_DV:ML_DV + 1]
                    link(dve.tensor_scalar(d[:, 0:1], dn, -1.0, acol[:, 8 + t * 4 + h:9 + t * 4 + h], ALU.mult, ALU.max))
                    link(dve.tensor_tensor(d[:, 0:1], d[:, 0:1], dn, ALU.max))
                    link(dve.reciprocal(d[:, 1:2], d[:, 0:1]))
                    dve.tensor_scalar(hA[:, t, h * ML_DV:(h + 1) * ML_DV], bank(u, ML_DV), d[:, 1:2], None, ALU.mult)\
                        .then_inc(aux_free[u % 4], 1)
                if h == 3:
                    for hh in range(2, 4):
                        for t in range(T):
                            aux_taken(dve, AUX[("mpv", hh, t)])
                    dve.sem_inc(sem("ml_h"), 1)

            def per_head(name):
                return rstd[:, SLOT[name], :].rearrange("p (t h) -> p t h", t=T)

            def a_evacuate(s):
                n = FIRST["A"] + s
                if s == 0:
                    powered(dve, "x")
                r = lambda t: r_tok("x", t)
                if s in (0, 1, 3, 4, 6, 7):
                    scaled(n, gate[s % 2], r).then_inc(acc_free[n % 2], 1)
                elif s in (2, 5):
                    h = (s - 2) // 3
                    scaled(n, ob[:, :, h * 512:(h + 1) * 512], r).then_inc(acc_free[n % 2], 1)
                elif s in (8, 9):
                    scaled(n, vml[:, :, 2 * (s - 8):2 * (s - 7), 0:ML_DV], r).then_inc(acc_free[n % 2], 1)
                else:
                    y = (hA if s < 14 else ob)[:, :, (s % 2) * COLS:(s % 2 + 1) * COLS]
                    link(dve.tensor_tensor(y, y, next_gate()[:, :, :], ALU.mult))
                    dve.sem_inc(acc_free[n % 2], 1)
                    if s >= 14:
                        dve.sem_inc(sem("yb_ready"), 1)
                    if s == 13:
                        dve.sem_inc(sem("ya_ready"), 1)

            for s in range(16):
                for p in range(8):
                    split_lo(SLABS[FIRST["A"] + s][0] + p)
                    w = s * 8 + p
                    if (s, p) == (0, 4):
                        dve.wait_ge(sem("ss_x"), 1)
                        row_variance("x")
                    if p == 3 and s > 0:
                        a_evacuate(s - 1)
                    for half, L0 in ((0, 21), (1, 45)):
                        if w == L0 - 7:
                            hg_forget(half)
                        if w == L0 - 5:
                            hg_cumsum(half)
                        if w == L0 - 1:
                            hg_queries(half)
                        if w == L0 + 1:
                            hg_diagonal(half)
                        n = w - L0
                        if 0 <= n - 2 < 8:
                            hg_take(half, n - 2)
                        if 0 <= n < 8:
                            hg_sub(half, n)
                        if 0 <= n - 1 < 8:
                            hg_mul(half, n - 1)
                        if n == 11:
                            hg_output(half)
                        if n == 14:
                            dve.wait_ge(sem("ss_hB"), half + 1)
                            variance(f"hB{half}", HG_E)
                    if (s, p) in ((7, 5), (8, 5)):
                        ml_conv(s - 1)
                    if (s, p) == (8, 0):
                        ml_gates()
                    if (s, p) == (8, 2):
                        ml_logf()
                    if (s, p) == (8, 7):
                        ml_rows()
                    if (s, p) == (9, 2):
                        ml_weights()
                    if (s, p) == (9, 5):
                        ml_mask()
                    if (s, p) == (9, 7):
                        ml_scores()
                    if s == 10 and p >= 4:
                        ml_output(p - 4)
                    if (s, p) == (11, 1):
                        dve.wait_ge(sem("ss_hA"), 1)
                        variance("hA", ML_DV)
                    if (s, p) == (11, 5):
                        powered(dve, "hA")
                        x = hA[:, :, :].rearrange("p t (h c) -> p t h c", h=4)
                        link(dve.tensor_tensor(x, x, per_head("hA").unsqueeze(3).to_broadcast([P, T, 4, ML_DV]), ALU.mult))
                    if (s, p) == (12, 5):
                        for half in range(2):
                            x = ob[:, :, half * 512:(half + 1) * 512].rearrange("p t (h c) -> p t h c", h=4)
                            link(dve.tensor_tensor(x, x, per_head(f"hB{half}").unsqueeze(3).to_broadcast([P, T, 4, P]), ALU.mult))
                    if s == 15 and p == 4:
                        for i in range(4):
                            lo_split(AUX[("yT", i)], actB, 2 * i, gains[:, C_MIX:C_MIX + KD])
                    if s == 15 and p == 6:
                        for i in range(4, 6):
                            lo_split(AUX[("yT", i)], actB, 2 * i, gains[:, C_MIX:C_MIX + KD])

            def add_slab(n, s):
                slab_made(dve, n)
                x = resid[:, :, s * COLS:(s + 1) * COLS]
                dve.tensor_tensor(x, x, acc2(n), ALU.add).then_inc(acc_free[n % 2], 1)
                slab_taken(dve, n)
                dve.sem_inc(sem("h_added"), 1)

            for s in range(4):
                for p in range(8):
                    split_lo(SLABS[FIRST["C"] + s][0] + p)
                    if s == 0 and p == 3:
                        a_evacuate(15)
                    if s == 0 and p == 4:
                        for i in range(6, 8):
                            lo_split(AUX[("yT", i)], actB, 2 * i, gains[:, C_MIX:C_MIX + KD])
                    if s > 0 and p == 3:
                        add_slab(FIRST["C"] + s - 1, s - 1)
                    if s > 0 and p == 5:
                        for i in range(2):
                            lo_split(AUX[("hD", 2 * s - 2 + i)], actA, 4 * s - 4 + 2 * i, gains[:, C_PE:C_PE + KD])

            def d_gate(s):
                g = next_gate()
                n = FIRST["D"] + 2 * s + 1
                link(dve.tensor_tensor(g[:, :, :], g[:, :, :], eb[s % 2][:, :, :], ALU.mult))
                dve.sem_inc(acc_free[n % 2], 1)
                x = resid[:, :, s * COLS:(s + 1) * COLS]
                dve.tensor_tensor(x, x, g[:, :, :], ALU.add).then_inc(sem("h_gated"), 1)

            def d_final(s):
                dve.wait_ge(sem("ss_f1"), s + 1)
                x = resid[:, :, s * COLS:(s + 1) * COLS]
                dve.tensor_tensor(x, x, fw[:, s * COLS:(s + 1) * COLS].unsqueeze(1).to_broadcast([P, T, COLS]), ALU.mult)\
                    .then_inc(sem("h_final"), 1)

            for s in range(4):
                n = FIRST["D"] + 2 * s
                split_lo(SLABS[n][0])
                if s == 0:
                    pass
                for p in range(8):
                    split_lo(SLABS[n + 1][0] + p)
                    if s == 0 and p == 2:
                        add_slab(FIRST["C"] + 3, 3)
                    if s == 0 and p == 4:
                        for i in range(6, 8):
                            lo_split(AUX[("hD", i)], actA, 2 * i, gains[:, C_PE:C_PE + KD])
                    if s == 0 and p == 5:
                        dve.wait_ge(sem("ss_h1"), 1)
                        row_variance("h1")
                        dve.wait_ge(sem("fw_loaded"), 16)
                    if s > 0 and p == 2:
                        d_gate(s - 1)
                    if s > 0 and p == 5:
                        d_final(s - 1)
                    if s > 0 and p == 7:
                        for i in range(2):
                            lo_split(AUX[("hE", 2 * s - 2 + i)], actB, 4 * s - 4 + 2 * i, gains[:, C_ATTN:C_ATTN + KD])
                    if p == 3:
                        slab_made(dve, n)
                        dve.tensor_copy(eb[s % 2][:, :, :], acc2(n)).then_inc(acc_free[n % 2], 1)
                        slab_taken(dve, n)

            def rE(t):
                return r_e[:, t:t + 1]

            def qk_normalise(s):
                dve.wait_ge(sem("ss_qk"), s + 1)
                variance(f"qk{s}", SB_D)

            def qk_scale(s):
                powered(dve, f"qk{s}")
                x = gate[s % 2][:, :, :].rearrange("p t (h c) -> p t h c", h=4)
                dve.tensor_tensor(x, x, per_head(f"qk{s}").unsqueeze(3).to_broadcast([P, T, 4, P]), ALU.mult)\
                    .then_inc(sem("qk_normed"), 1)

            def qk_transposed(s):
                dst, gain = (qT, qn_scaled) if s < 2 else (kT, gains[:, C_KN:C_KN + 1])
                for i in range(2):
                    u = AUX[("tr2", s, i)]
                    aux_filled(dve, u)
                    c = 4 * (s % 2) + 2 * i
                    dve.tensor_scalar(dst[:, c:c + 2, :], bank(u).rearrange("p (h t) -> p h t", h=2), gain[:, 0:1], None, ALU.mult)\
                        .then_inc(aux_free[u % 4], 1)

            def att_take(b):
                for j in range(4):
                    u = AUX[("z", b, j)]
                    aux_filled(dve, u)
                    dve.tensor_copy(zt[:, j, :], bank(u, 384)).then_inc(aux_free[u % 4], 1)
                for j in range(4):
                    aux_taken(dve, AUX[("z", b, j)])
                dve.sem_inc(sem("att_z"), 1)

            def strict_blocks(x):
                d = diagonal_blocks(x)
                return dve.tensor_tensor(d, d, strict[:, :].unsqueeze(1).unsqueeze(1).to_broadcast([P, 4, 2, P]), ALU.mult)

            def att_logs(b):
                dve.wait_ge(sem("att_ln"), b + 1)
                link(dve.scalar_tensor_tensor(out=Lp[:, :, :], in0=zt[:, :, :], scalar=0.0, in1=ab[:, :, :], op0=ALU.max, op1=ALU.add))
                strict_blocks(Lp).then_inc(sem("att_l"), 1)
                link(dve.scalar_tensor_tensor(out=zt[:, :, :], in0=zt[:, :, :], scalar=0.0, in1=ab[:, :, :], op0=ALU.min,
                                              op1=ALU.subtract))

            def att_arg(b):
                for j in range(4):
                    u = AUX[("tail", b, j)]
                    aux_filled(dve, u)
                    dve.tensor_tensor(zt[:, j, :], zt[:, j, :], bank(u, 384), ALU.subtract).then_inc(aux_free[u % 4], 1)
                for j in range(4):
                    aux_taken(dve, AUX[("tail", b, j)])
                dve.sem_inc(sem("att_arg"), 1)

            def att_mask(b):
                dve.wait_ge(sem("att_w"), b + 1)
                strict_blocks(zt).then_inc(sem("att_masked"), 1)

            def att_output(b):
                aux_filled(dve, AUX[("att", b, 1)])
                for t in range(T):
                    u = AUX[("att", b, t)]
                    dve.tensor_copy(vA[:, t, b * 512:(b + 1) * 512], bank(u)).then_inc(aux_free[u % 4], 1)

            def vs_scale(half):
                powered(dve, f"s{half}")
                x = vs[:, :, half * 512:(half + 1) * 512].rearrange("p t (h c) -> p t h c", h=4)
                dve.tensor_tensor(x, x, per_head(f"s{half}").unsqueeze(3).to_broadcast([P, T, 4, P]), ALU.mult)\
                    .then_inc(sem("vs_ready"), 1)

            def spatial_gate(half):
                dve.wait_ge(sem("gbc_loaded"), 16)
                for i in range(2):
                    u = AUX[("sgu", 2 * half + i)]
                    aux_filled(dve, u)
                    g = 4 * half + 2 * i
                    t4 = ab[:, 0:2, 0:S].rearrange("p g (t c) -> p g t c", t=T)
                    for j in range(2):
                        ins = dve.tensor_tensor(t4[:, j], bank(u)[:, j * S:(j + 1) * S].rearrange("p (t c) -> p t c", t=T),
                                                gbc[:, (g + j) * P:(g + j + 1) * P].unsqueeze(1).to_broadcast([P, T, P]), ALU.mult)
                    ins.then_inc(aux_free[u % 4], 1)
                    aux_taken(dve, u)
                    for j in range(2):
                        x = u2[:, :, (g + j) * P:(g + j + 1) * P]
                        ins = dve.scalar_tensor_tensor(out=x, in0=t4[:, j], scalar=gains[:, C_BS + g + j:C_BS + g + j + 1], in1=x,
                                                       op0=ALU.add, op1=ALU.mult)
                    if i == 0:
                        link(ins)
                ins.then_inc(sem("ya2_ready"), 1)

            for s in range(10):
                n = FIRST["E1"] + s
                for p in range(8):
                    split_lo(SLABS[n][0] + p)
                    w = s * 8 + p
                    if s == 0:
                        if p == 3:
                            d_gate(3)
                        if p == 5:
                            d_final(3)
                            dve.wait_ge(sem("h_final"), 4)
                            dve.sem_inc(sem("block1_done"), 1)
                        if p == 6:
                            for i in range(6, 8):
                                lo_split(AUX[("hE", i)], actB, 2 * i, gains[:, C_ATTN:C_ATTN + KD])
                        if p == 7:
                            dve.wait_ge(sem("ss_f1"), 4)
                            row_variance("f1")
                    if (s, p) == (1, 0):
                        dve.wait_ge(sem("ss_f2"), 4)
                        powered(dve, "f1")
                        i, j = SLOT["f1"], SLOT["f2"]
                        link(dve.tensor_reduce(var[:, j, 4:6], ss[:, j, :].rearrange("p (t c) -> p t c", t=T), AX.X, ALU.add))
                        for _ in range(2):
                            link(dve.tensor_tensor(var[:, j, 4:6], var[:, j, 4:6], rstd[:, i, 0:T], ALU.mult))
                        variance("f2", D, var[:, j, 4:6])
                    if (s, p) == (1, 1):
                        powered(dve, "f2")
                        dve.tensor_tensor(r_e[:, :], rstd[:, SLOT["f1"], 0:T], rstd[:, SLOT["f2"], 0:T], ALU.mult)\
                            .then_inc(sem("r_e_ready"), 1)
                        dve.wait_ge(sem("r_e_ready"), 1)
                    if 1 <= s <= 4:
                        if p == 3:
                            scaled(n - 1, gate[(s - 1) % 2], rE).then_inc(acc_free[(n - 1) % 2], 1)
                            slab_taken(dve, n - 1)
                            dve.sem_inc(sem("qk_tok"), 1)
                        if p == 5:
                            qk_normalise(s - 1)
                        if p == 6:
                            qk_scale(s - 1)
                    if 2 <= s <= 5 and p == 0:
                        qk_transposed(s - 2)
                    if (s, p) == (2, 4):
                        for i in range(2):
                            u = AUX[("ws", i)]
                            aux_filled(dve, u)
                            dve.tensor_copy(wsT[:, 4 * i:4 * i + 4, :], bank(u).rearrange("p (g t) -> p g t", g=4))\
                                .then_inc(aux_free[u % 4], 1)
                    if s == 2 and p in (5, 6):
                        t = p - 5
                        link(dve.tensor_scalar(resid[:, t, :], resid[:, t, :], r_tok("f1", t), None, ALU.mult))
                    if s in (5, 6) and p == 3:
                        scaled(n - 1, vA[:, :, (s - 5) * 512:(s - 4) * 512], rE).then_inc(acc_free[(n - 1) % 2], 1)
                    for b, z0 in ((0, 45), (1, 58)):
                        if w == z0:
                            att_take(b)
                        if w == z0 + 3:
                            att_logs(b)
                        if w == z0 + 7:
                            att_arg(b)
                        if w == z0 + 9:
                            att_mask(b)
                        if w == z0 + 12:
                            att_output(b)
                    if s in (7, 8) and p == 5:
                        dve.wait_ge(sem("ss_s"), s - 6)
                        variance(f"s{s - 7}", P)
                    if s in (7, 8) and p == 7:
                        vs_scale(s - 7)
                    if (s, p) == (9, 4):
                        slab_taken(dve, n - 1)
                        spatial_gate(0)
                    if (s, p) == (9, 7):
                        for i in range(2):
                            lo_split(AUX[("yaT", i)], actA, 2 * i)

            pair_gate = [None]
            for ph in ("E2", "E3"):
                for s in range(8):
                    n = FIRST[ph] + s
                    for p in range(SLABS[n][1]):
                        split_lo(SLABS[n][0] + p)
                        if ph == "E2" and s == 0:
                            if p == 4:
                                slab_taken(dve, n - 1)
                                spatial_gate(1)
                            if p == 6:
                                for i in range(2, 4):
                                    lo_split(AUX[("yaT", i)], actA, 2 * i)
                            if p == 7:
                                for i in range(4):
                                    lo_split(AUX[("ybT", i)], actA, 8 + 2 * i)
                        if p == 3 and s % 2 == 1:
                            pair_gate[0] = next_gate()
                            dve.sem_inc(acc_free[(n - 1) % 2], 1)
                        if p == 3 and s % 2 == 0 and (s > 0 or ph == "E3"):
                            merge_phase2 = ph == "E3" and s > 0
                            col = (s // 2 - 1) % 4
                            x = merged[:, :, col * COLS:(col + 1) * COLS]
                            slab_made(dve, n - 1)
                            if not merge_phase2:
                                dve.tensor_tensor(x, pair_gate[0][:, :, :], acc2(n - 1), ALU.mult).then_inc(acc_free[(n - 1) % 2], 1)
                                slab_taken(dve, n - 1)
                            else:
                                gt = pair_gate[0][:, :, :]
                                dve.tensor_tensor(gt, gt, acc2(n - 1), ALU.mult).then_inc(acc_free[(n - 1) % 2], 1)
                                slab_taken(dve, n - 1)
                                dve.tensor_tensor(x, x, gt, ALU.add).then_inc(sem("merged_ready"), 1)
                        if ph == "E3" and s >= 2 and s % 2 == 0 and p == 6:
                            for i in range(2):
                                lo_split(AUX[("mT", s - 2 + i)], actF, 2 * (s - 2 + i))

            for s in range(4):
                n = FIRST["G"] + s
                for p in range(8):
                    split_lo(SLABS[n][0] + p)
                    if s == 0 and p == 3:
                        gt = pair_gate[0][:, :, :]
                        x = merged[:, :, 3 * COLS:4 * COLS]
                        slab_made(dve, n - 1)
                        dve.tensor_tensor(gt, gt, acc2(n - 1), ALU.mult).then_inc(acc_free[(n - 1) % 2], 1)
                        slab_taken(dve, n - 1)
                        dve.tensor_tensor(x, x, gt, ALU.add).then_inc(sem("merged_ready"), 1)
                    if s == 0 and p == 5:
                        for i in range(6, 8):
                            lo_split(AUX[("mT", i)], actF, 2 * i)
                    if s > 0 and p == 3:
                        add_slab(n - 1, s - 1)
                    if s > 0 and p == 5:
                        for i in range(2):
                            lo_split(AUX[("hH", 2 * s - 2 + i)], actA, 4 * s - 4 + 2 * i, gains[:, C_FFN:C_FFN + KD])

            def take_gate(n):
                pair_gate[0] = next_gate()
                dve.sem_inc(acc_free[n % 2], 1)

            def hidden(n, j):
                slab_made(dve, n)
                for t in range(T):
                    ins = dve.scalar_tensor_tensor(out=hid[:, t, :], in0=acc2(n)[:, t, :], scalar=r_tok("ffn", t),
                                                   in1=pair_gate[0][:, t, :], op0=ALU.mult, op1=ALU.mult)
                ins.then_inc(acc_free[n % 2], 1)
                slab_taken(dve, n)
                dve.sem_inc(sem("hid_ready"), 1)

            for part, (f0, width) in enumerate(FFN_PARTS):
                nh = width // COLS
                for s in range(2 * nh):
                    n = FIRST[f"H{part}"] + s
                    for p in range(8):
                        split_lo(SLABS[n][0] + p)
                        if s == 0 and p == 3:
                            add_slab(n - 1, 3)
                        if s == 0 and part == 0:
                            if p == 5:
                                for i in range(6, 8):
                                    lo_split(AUX[("hH", i)], actA, 2 * i, gains[:, C_FFN:C_FFN + KD])
                            if p == 6:
                                dve.wait_ge(sem("ss_ffn"), 1)
                                row_variance("ffn")
                        if s % 2 == 1 and p == 3:
                            take_gate(n - 1)
                        if s > 0 and s % 2 == 0 and p == 3:
                            hidden(n - 1, s // 2 - 1)
                        if s > 0 and s % 2 == 0 and p == 6:
                            for c in range(4):
                                lo_split(AUX[("hid", part, 2 * s - 4 + c)], actF, 2 * s - 4 + c, n=1)
                for s in range(4):
                    n = FIRST[f"O{part}"] + s
                    for p in range(SLABS[n][1]):
                        split_lo(SLABS[n][0] + p)
                        if s == 0 and p == 3:
                            hidden(n - 1, nh - 1)
                        if s == 0 and p == 4:
                            for c in range(4):
                                lo_split(AUX[("hid", part, 4 * nh - 4 + c)], actF, 4 * nh - 4 + c, n=1)
                        if s > 0 and p == 3:
                            add_slab(n - 1, s - 1)
                        if part == 2 and s > 0 and p == 5:
                            for i in range(2):
                                lo_split(AUX[("hJ", 2 * s - 2 + i)], actB, 4 * s - 4 + 2 * i, gains[:, C_PLE:C_PLE + KD])

            def j_gate(s):
                g = next_gate()
                n = FIRST["J"] + 2 * s + 1
                link(dve.tensor_tensor(g[:, :, :], g[:, :, :], merged[:, :, (s % 2) * COLS:(s % 2 + 1) * COLS], ALU.mult))
                dve.sem_inc(acc_free[n % 2], 1)
                x = resid[:, :, s * COLS:(s + 1) * COLS]
                dve.tensor_tensor(x, x, g[:, :, :], ALU.add).then_inc(sem("out_ready"), 1)

            for s in range(4):
                n = FIRST["J"] + 2 * s
                split_lo(SLABS[n][0])
                for p in range(8):
                    split_lo(SLABS[n + 1][0] + p)
                    if s == 0 and p == 2:
                        add_slab(n - 1, 3)
                    if s == 0 and p == 4:
                        for i in range(6, 8):
                            lo_split(AUX[("hJ", i)], actB, 2 * i, gains[:, C_PLE:C_PLE + KD])
                    if s == 0 and p == 5:
                        dve.wait_ge(sem("ss_ple"), 1)
                        row_variance("ple")
                    if s > 0 and p == 2:
                        j_gate(s - 1)
                    if p == 3:
                        slab_made(dve, n)
                        dve.tensor_copy(merged[:, :, (s % 2) * COLS:(s % 2 + 1) * COLS], acc2(n)).then_inc(acc_free[n % 2], 1)
                        slab_taken(dve, n)
            j_gate(3)


_INS = ["x", "p", "norm_w", "w_in", "conv_w", "conv_b", "ml_b_i", "ml_b_f", "ml_norm_w", "hg_lb", "hg_norm_w", "w_out",
        "pe_norm_w", "w_pg", "w_pe", "final_norm_w", "p_2", "attn_norm_g_2", "w_in_2", "sgu_norm_g_2", "w_s_2", "b_s_2",
        "q_norm_g_2", "k_norm_g_2", "w_up_a_2", "w_up_b_2", "w_o_2", "ffn_norm_g_2", "w_ffn_in_2", "w_ffn_out_2",
        "ple_norm_g_2", "w_ple_gate_2", "w_ple_2"]


def kernel(**inputs):
    import numpy as _np
    import concourse.bacc as _bacc
    from concourse.bass_utils import run_bass_kernel_spmd as _run

    nc = _bacc.Bacc("TRN2", target_bir_lowering=False, num_devices=1)
    arrays, aps = {}, {}
    for name in _INS:
        a = _np.ascontiguousarray(inputs[name])
        arrays[f"in_{name}"] = a
        aps[name] = nc.dram_tensor(f"in_{name}", a.shape, mybir.dt.from_np(a.dtype), kind="ExternalInput").ap()
    out = nc.dram_tensor("out_0", (1, S, D), F32, kind="ExternalOutput").ap()
    two_blocks_kernel(nc, aps, out)
    r = _run(nc, [arrays], core_ids=[0])
    return r.results[0]["out_0"]
```

```python
from contextlib import ExitStack

import concourse.bass as bass
from concourse import mybir

F32 = mybir.dt.float32
F32R = mybir.dt.float32r
I32 = mybir.dt.int32
ACT = mybir.ActivationFunctionType
ALU = mybir.AluOpType
AX = mybir.AxisListType

P = 128
D = 2048
KD = D // P
S = 256
T = S // P
COLS = 512
PK = 2
RING = 4
EPS = 1e-6

ML_HEADS, ML_DQK, ML_DV, ML_TAPS = 4, 128, 256, 4
ML_W = ML_HEADS * ML_DV
HG_HEADS, HG_E = 8, 128
SB_HEADS, SB_D = 8, 128
GROUPS = 8
PE_DIM = 256
FFN = 5632

MQ, MK, MV, MO, MZ, MI = 0, 512, 1024, 2048, 3072, 4096
HQ, HF, HI, HG = 4104, 5128, 6152, 7176
U2, S2, Q2, K2, V2, GA2, GB2 = 0, 1024, 2048, 3072, 4096, 5120, 7168

A_COLS = [HF, HQ, HI, HF + 512, HQ + 512, HI + 512, HG, MQ, MK, MV, MV + 512, HG + 512, MZ, MZ + 512, MO, MO + 512]
E1_COLS = [Q2, Q2 + 512, K2, K2 + 512, V2, V2 + 512, S2, S2 + 512, U2, U2 + 512]
FFN_PARTS = [(0, 2048), (2048, 2048), (4096, 1536)]

C_NORM, C_PE, C_ATTN, C_FFN, C_PLE, C_LB, C_CONVW = 0, 16, 32, 48, 64, 80, 96
C_CONVB, C_QN, C_KN, C_BS, C_MIX, C_FW, C_END = 128, 136, 137, 138, 146, 162, 178

LEVELS = [128 >> n for n in range(8)]
A_TRANSPOSED = (0, 1, 3, 4, 7, 8)
A_GATED = (6, 11, 12, 13, 14, 15)
HG_START = (23, 49)
ATT_START = (42, 57)


def plan():
    phases = [("A", [8] * 16), ("C", [8] * 4), ("D", [1, 8] * 4), ("E1", [8] * 10), ("E2", [8, 4] * 4),
              ("E3", [8, 4] * 4), ("G", [8] * 4)]
    for i, (_, width) in enumerate(FFN_PARTS):
        phases.append((f"H{i}", [8, 8] * (width // COLS)))
        phases.append((f"O{i}", [width // P // PK] * 4))
    phases.append(("J", [1, 8] * 4))
    slabs, first, g = [], {}, 0
    for name, counts in phases:
        first[name] = len(slabs)
        for n in counts:
            slabs.append((g, n))
            g += n
    return slabs, first


def plan_aux():
    names = [("gains", 0)] + [("xT", i) for i in range(8)]

    def two(name, *key):
        names.extend((name, *key, i) for i in range(2))

    two("tr", 0)
    names.extend([("p", 0), ("p2", 0)])
    two("tr", 1); two("diag", 0)
    names.extend(("level", 0, n) for n in range(6))
    two("tr", 3)
    names.extend(("level", 0, n) for n in range(6, 8))
    two("pv", 0); two("tr", 4); two("diag", 1)
    names.extend(("level", 1, n) for n in range(8))
    two("tr", 7); two("pv", 1); two("tr", 8)
    names.extend([("gates", 0), ("gatesT", 0), ("gtr", 0), ("atr", 0), ("bc", 0), ("bc", 1)])
    names.extend(("st", h) for h in range(4))
    names.extend(("mpv", h, t) for h in range(4) for t in range(2))
    names.extend(("yT", i) for i in (4, 5, 6, 7, 0, 1, 2, 3))
    names.extend(("hD", i) for i in range(8))
    names.extend(("hE", i) for i in range(8))
    two("tr2", 0); two("ws"); two("tr2", 1); two("tr2", 2); two("tr2", 3)
    for b in range(2):
        names.extend(("z", b, h) for h in range(4))
        names.extend(("tail", b, h) for h in range(4))
        two("att", b)
    names.extend([("sgu", 0), ("sgu", 1), ("yaT", 0), ("yaT", 1), ("sgu", 2), ("sgu", 3), ("yaT", 2), ("yaT", 3)])
    names.extend(("ybT", i) for i in range(4))
    names.extend(("mT", i) for i in range(8))
    names.extend(("hH", i) for i in range(8))
    for part, (_, width) in enumerate(FFN_PARTS):
        names.extend(("hid", part, c) for c in range(width // P))
    names.extend(("hJ", i) for i in range(8))
    assert len(set(names)) == len(names)
    return {n: i for i, n in enumerate(names)}


def two_blocks_kernel(nc, A, out):
    SLABS, FIRST = plan()
    AUX = plan_aux()
    ctx = ExitStack()
    with ctx:
        def sb(name, shape, dt=F32, at=None):
            return (at or ctx).enter_context(nc.sbuf_tensor(name, shape, dt))

        sems = {}

        def sem(name):
            if name not in sems:
                sems[name] = ctx.enter_context(nc.semaphore(name))
            return sems[name]

        raw = sb("raw", [P, RING, PK, COLS])
        whi = sb("whi", [P, RING, PK, COLS], F32R)
        wlo = sb("wlo", [P, RING, PK, COLS], F32R)
        resid = sb("resid", [P, T, D])
        ra = ExitStack()
        actA = [sb(f"actA_{x}", [P, KD, S], F32R, at=ra) for x in ("hi", "lo")]
        ra.close()
        qT = sb("qT", [P, 8, S])
        kT = sb("kT", [P, 8, S])
        zt = sb("att_z", [P, 4, 384])
        Lp = sb("att_l", [P, 4, 384])
        sb("rest_of_actA", [P, 2 * KD * S - 16 * S - 8 * 384])
        actB = [sb(f"actB_{x}", [P, KD, S], F32R) for x in ("hi", "lo")]
        gate = [sb(f"gate{i}", [P, T, COLS]) for i in range(2)]
        pT = [[sb(f"p{n}T_{x}", [P, PK, S], F32R) for x in ("hi", "lo")] for n in range(2)]
        gains = sb("gains", [P, C_END])
        gain_e = sb("gain_e", [P, KD])
        lb = sb("lb", [P, 4, 8])
        qn_scaled = sb("qn_scaled", [P, 1])
        ident = sb("ident", [P, P])
        ones = sb("ones", [P, S])
        causal = sb("causal", [P, P])
        strict = sb("strict", [P, P])
        later = sb("later", [P, P])
        lmask = sb("lmask", [P, 7, 64])
        minus_half = sb("minus_half", [P, 16])
        junk = sb("junk", [P, COLS])
        ss = sb("ss", [P, 16, 8])
        var = sb("var", [P, 16, 8])
        rstd = sb("rstd", [P, 16, 8])
        r_e = sb("r_e", [P, T])
        r1 = ExitStack()
        ob = sb("hg_v", [P, T, 1024], at=r1)
        gw = sb("gw", [P, KD, 8], at=r1)
        gw_hi_lo = sb("gw_hi_lo", [P, KD, 16], F32R, at=r1)
        gates_ch = sb("gates_ch", [16, S], at=r1)
        gbias = sb("gbias", [P, 8], at=r1)
        sel = sb("sel", [4, 4, P], at=r1)
        gtok = sb("gtok", [P, T, 8], at=r1)
        gtmp = sb("gtmp", [P, T, 4], at=r1)
        acol = sb("acol", [P, 16], at=r1)
        den = sb("den", [P, 8, 2], at=r1)
        rs = ExitStack()
        stage1 = sb("stage1", [P, P], at=rs)
        stage2 = sb("stage2", [C_END - P, P], at=rs)
        ptok = [sb(f"ptok{n}", [P, T, PE_DIM], at=rs) for n in range(2)]
        rs.close()
        rh = ExitStack()
        bF = sb("hg_b", [P, 1024], at=rh)
        qF = sb("hg_q", [P, 1024], at=rh)
        kF = sb("hg_k", [P, 1024], at=rh)
        Eb = [sb(f"hg_e{i}", [P, 1024], at=rh) for i in range(2)]
        Qp = [sb(f"hg_qd{i}", [P, 512], at=rh) for i in range(2)]
        Kp = [sb(f"hg_kd{i}", [P, 1024], at=rh) for i in range(2)]
        Am = sb("hg_a", [P, 8, P], at=rh)
        A01 = sb("hg_a01", [P, 4, P], at=rh)
        rh.close()
        rm = ExitStack()
        qk = sb("ml_qk", [P, 8, S], at=rm)
        hrow = sb("hrow", [4, 6, S], at=rm)
        Wd = sb("ml_w", [P, 4, 384], at=rm)
        hA = sb("ml_h", [P, T, ML_W], at=rm)
        vml = sb("ml_v", [P, T, 4, ML_DV + 2], at=rm)
        rm.close()
        rd = ExitStack()
        eb = [sb(f"ple_e{i}", [P, T, COLS], at=rd) for i in range(2)]
        fw = sb("final_gain", [P, D], at=rd)
        rd.close()
        r1.close()
        r2 = ExitStack()
        merged = sb("merged", [P, T, D], at=r2)
        r2f = ExitStack()
        actF = [sb(f"actF_{x}", [P, KD, S], F32R, at=r2f) for x in ("hi", "lo")]
        hid = sb("hid", [P, T, COLS], at=r2f)
        r2f.close()
        vA = sb("att_v", [P, T, 1024], at=r2)
        ab = sb("att_ab", [P, 4, 384], at=r2)
        gbc = sb("sgu_gain", [P, 1024], at=r2)
        wsT = sb("wsT", [P, 8, P], at=r2)
        r2.close()
        r2b = ExitStack()
        u2 = sb("sgu_u", [P, T, 1024], at=r2b)
        vs = sb("sgu_v", [P, T, 1024], at=r2b)
        r2b.close()
        wsr = zt[:, :, :].rearrange("p a b -> p (a b)")[:, 0:1024].rearrange("p (g s) -> p g s", g=8)

        acc = ctx.enter_context(nc.psum_tensor("acc", [P, 4, COLS], F32))
        aux = ctx.enter_context(nc.psum_tensor("aux", [P, 4, COLS], F32))

        raw_loaded = [sem(f"raw_loaded{i}") for i in range(RING)]
        hi_ready, lo_ready, piece_used = sem("hi_ready"), sem("lo_ready"), sem("piece_used")
        acc_free = [sem(f"acc_free{i}") for i in range(2)]
        aux_full = sem("aux_full")
        aux_free = [sem(f"aux_free{i}") for i in range(4)]
        split_hi_done = sem("split_hi_done")
        gate_ready = sem("gate_ready")
        pow_in, pow_out = sem("pow_in"), sem("pow_out")

        def view(w):
            return w.rearrange("(k p) n -> p k n", p=P)

        def aux_filled(eng, u, i=0):
            eng.wait_ge(aux_full, u + 1 + i * 4)

        def aux_taken(eng, u, i=0):
            eng.wait_ge(aux_free[u % 4], u // 4 + 1 + i)

        def slab_made(eng, n, i=0, per=0):
            eng.wait_ge(piece_used, sum(SLABS[n]) + i * per)

        def slab_taken(eng, n, i=0):
            eng.wait_ge(acc_free[n % 2], n // 2 + 1 + i)

        def bank(u, n=COLS):
            return aux[:, u % 4, 0:n]

        def acc2(n):
            return acc[:, 2 * (n % 2):2 * (n % 2) + 2, :]

        POWS = [("x", T), ("hB0", 8), ("hB1", 8), ("hA", 8), ("h1", T), ("f1", T), ("f2", T), ("qk0", 8), ("qk1", 8),
                ("qk2", 8), ("qk3", 8), ("s0", 8), ("s1", 8), ("ffn", T), ("ple", T)]
        SLOT = {n: i for i, (n, _) in enumerate(POWS)}

        def r_tok(name, t):
            return rstd[:, SLOT[name], t:t + 1]

        def powered(eng, name):
            eng.wait_ge(pow_out, SLOT[name] + 1)

        block = ctx.enter_context(nc.Block())

        @block.sync
        def _(sp):
            piece = [0]

            def load(src, dst=None):
                g = piece[0]
                piece[0] += 1
                if g >= RING:
                    sp.wait_ge(lo_ready, g - RING + 1)
                d = raw[:, g % RING] if dst is None else dst(raw[:, g % RING])
                sp.dma_start(d, src).then_inc(raw_loaded[g % RING], 16)

            def load_slab(w, c, n=8, k0=0):
                for p in range(n):
                    k = k0 + p * PK
                    load(view(w)[:, k:k + PK, c:c + COLS])

            def load_x(c):
                sp.dma_start(resid[:, :, c * COLS:(c + 1) * COLS],
                             A["x"][0].rearrange("(t p) c -> p t c", p=P)[:, :, c * COLS:(c + 1) * COLS])\
                    .then_inc(sem(f"x_loaded{c}"), 16)

            load_x(0)
            load_slab(A["w_in"][0], A_COLS[0], 2)
            load_x(1)
            load_slab(A["w_in"][0], A_COLS[0], 2, 2 * PK)
            load_x(2)
            load_x(3)
            load_slab(A["w_in"][0], A_COLS[0], 4, 4 * PK)
            for c in A_COLS[1:]:
                load_slab(A["w_in"][0], c)
            for s in range(4):
                load_slab(A["w_out"][0], s * COLS, 4, KD // 2)
                load_slab(A["w_out"][0], s * COLS, 4)
            sp.wait_ge(sem("h_added"), 1)
            sp.dma_start(fw[:, :], A["final_norm_w"].partition_broadcast(P)).then_inc(sem("fw_loaded"), 16)
            for s in range(4):
                load_slab(A["w_pe"][0], s * COLS, 1)
                load_slab(A["w_pg"][0], s * COLS)
            for n, c in enumerate(E1_COLS):
                load_slab(A["w_in_2"][0], c)
                if n == 0:
                    sp.wait_ge(sem("block1_done"), 1)
                    sp.dma_start(wsr, A["w_s_2"][0].rearrange("g t s -> t g s")).then_inc(sem("ws_loaded"), 16)
                    sp.dma_start(gbc[:, :], A["sgu_norm_g_2"][0].rearrange("g c -> (g c)").partition_broadcast(P))\
                        .then_inc(sem("gbc_loaded"), 16)
            for c0, w_up in ((GA2, "w_up_a_2"), (GB2, "w_up_b_2")):
                for s in range(4):
                    load_slab(A["w_in_2"][0], c0 + s * COLS)
                    load_slab(A[w_up][0], s * COLS, 4)
            for s in range(4):
                load_slab(A["w_o_2"][0], s * COLS)
            for f0, width in FFN_PARTS:
                for s in range(width // COLS):
                    for h in range(2):
                        load_slab(A["w_ffn_in_2"][0], h * FFN + f0 + s * COLS)
                for s in range(4):
                    load_slab(A["w_ffn_out_2"][0], s * COLS, width // 256, f0 // P)
            for s in range(4):
                load_slab(A["w_ple_2"][0], s * COLS, 1)
                load_slab(A["w_ple_gate_2"][0], s * COLS)
            for s in range(4):
                for t in range(T):
                    sp.wait_ge(sem("out_ready"), s + 1)
                    sp.dma_start(out[0, t * P:(t + 1) * P, s * COLS:(s + 1) * COLS],
                                 resid[:, t, s * COLS:(s + 1) * COLS]).then_inc(sem("stored"), 16)
            sp.wait_ge(sem("stored"), 16 * 4 * T)

        @block.gpsimd
        def _(pool):
            made = [0]

            def link(ins):
                made[0] += 1
                ins.then_inc(sem("pool_step"), 1)

            def settle():
                pool.wait_ge(sem("pool_step"), made[0])

            link(pool.memset(ident[:, :], 0.0))
            settle()
            link(pool.affine_select(out=ident[:, :], in_=ident[:, :], compare_op=ALU.not_equal, fill=1.0, base=0,
                                    pattern=[[-1, P]], channel_multiplier=1))
            settle()
            pool.sem_inc(sem("ident_ready"), 1)
            link(pool.memset(ones[:, :], 1.0))
            link(pool.memset(lmask[:, :, :], 1.0))
            link(pool.memset(sel[:, :, :], 0.0))
            settle()
            link(pool.affine_select(out=causal[:, :], in_=ones[:, 0:P], compare_op=ALU.is_ge, fill=0.0, base=0,
                                    pattern=[[1, P]], channel_multiplier=-1))
            link(pool.affine_select(out=strict[:, :], in_=ones[:, 0:P], compare_op=ALU.is_gt, fill=0.0, base=0,
                                    pattern=[[1, P]], channel_multiplier=-1))
            link(pool.affine_select(out=later[:, :], in_=ones[:, 0:P], compare_op=ALU.is_gt, fill=0.0, base=0,
                                    pattern=[[-1, P]], channel_multiplier=1))
            link(pool.affine_select(out=sel[:, :, :], in_=sel[:, :, :], compare_op=ALU.not_equal, fill=1.0, base=0,
                                    pattern=[[-1, 4], [0, P]], channel_multiplier=1))
            for n, s in enumerate(LEVELS[1:]):
                m = lmask[:, n, :].rearrange("p (n s) -> p n s", s=s)
                link(pool.affine_select(out=m, in_=m, compare_op=ALU.is_ge, fill=0.0, base=0,
                                        pattern=[[-2 * s, 64 // s], [0, s]], channel_multiplier=1))
            settle()
            for n, s in enumerate(LEVELS[1:]):
                m = lmask[:, n, :].rearrange("p (n s) -> p n s", s=s)
                link(pool.affine_select(out=m, in_=m, compare_op=ALU.is_ge, fill=0.0, base=s - 1,
                                        pattern=[[2 * s, 64 // s], [0, s]], channel_multiplier=-1))
            link(pool.memset(minus_half[:, :], -0.5))
            settle()
            pool.sem_inc(sem("consts_ready"), 1)
            for i, (name, n) in enumerate(POWS):
                if name == "qk0":
                    pool.wait_ge(sem("ws_loaded"), 16)
                    pool.affine_select(out=wsr, in_=wsr, compare_op=ALU.is_ge, fill=0.0, base=0,
                                       pattern=[[0, 8], [-1, P]], channel_multiplier=1).then_inc(sem("ws_masked"), 1)
                pool.wait_ge(pow_in, i + 1)
                pool.tensor_tensor(rstd[:, i, 0:n], var[:, i, 0:n], minus_half[:, 0:n], ALU.pow).then_inc(pow_out, 1)

        @block.scalar
        def _(act):
            steps = [0]
            gates = [0]

            def link(ins):
                steps[0] += 1
                ins.then_inc(sem("act_step"), 1)
                act.wait_ge(sem("act_step"), steps[0])

            def split_hi(g):
                act.wait_ge(raw_loaded[g % RING], 16 * (g // RING + 1))
                if g >= RING:
                    act.wait_ge(piece_used, g - RING + 1)
                act.activation(whi[:, g % RING], raw[:, g % RING], ACT.Copy).then_inc(hi_ready, 1)

            def act_split(u, dst, c0, gain=None, n=2):
                aux_filled(act, u)
                for c in range(n):
                    ins = act.activation(dst[0][:, c0 + c, :], bank(u)[:, c * S:(c + 1) * S], ACT.Copy,
                                         scale=1.0 if gain is None else gain[:, c0 + c:c0 + c + 1])
                ins.then_inc(split_hi_done, 1)

            def squares(src, dst):
                link(act.activation(junk[:, 0:src.shape[-1]], src, ACT.Square, accum_out=dst))

            def gated(n, func, r, dst=None):
                slab_made(act, n)
                j = gates[0]
                gates[0] += 1
                powered(act, r) if r in SLOT else act.wait_ge(sem("r_e_ready"), 1)
                for t in range(T):
                    scale = r_tok(r, t) if r in SLOT else r_e[:, t:t + 1]
                    ins = act.activation((gate[j % 2] if dst is None else dst)[:, t, :], acc2(n)[:, t, :], func, scale=scale)
                ins.then_inc(gate_ready if dst is None else acc_free[n % 2], 1)
                if dst is not None:
                    gates[0] -= 1

            small = sem("small_loaded")
            rows = [(stage1, C_NORM, A["norm_w"]), (stage1, C_PE, A["pe_norm_w"]), (stage1, C_ATTN, A["attn_norm_g_2"]),
                    (stage1, C_FFN, A["ffn_norm_g_2"]), (stage1, C_PLE, A["ple_norm_g_2"]), (stage1, C_LB, A["hg_lb"]),
                    (stage1, C_CONVW, A["conv_w"][0]), (stage2, C_CONVB, A["conv_b"]), (stage2, C_QN, A["q_norm_g_2"]),
                    (stage2, C_KN, A["k_norm_g_2"]), (stage2, C_BS, A["b_s_2"][0]), (stage2, C_MIX, A["ml_norm_w"]),
                    (stage2, C_MIX + 8, A["hg_norm_w"])]
            for dst, c, src in rows:
                c -= 0 if dst is stage1 else P
                flat = src.rearrange("a (r c) -> (a r) c", c=P)
                act.dma_start(dst[c:c + flat.shape[0], :], flat).then_inc(small, 16)
            act.dma_start(stage2[C_FW - P:C_END - P, :], A["final_norm_w"].rearrange("(r c) -> r c", c=P)).then_inc(small, 16)

            for s in range(16):
                for p in range(8):
                    split_hi(SLABS[FIRST["A"] + s][0] + p)
                    w = s * 8 + p
                    if s == 0:
                        if p == 0:
                            aux_taken(act, AUX[("gains", 0)])
                        act_split(AUX[("xT", p)], actA, 2 * p, gains[:, C_NORM:C_NORM + KD])
                        if p == 2:
                            act.wait_ge(sem("lb_in"), 1)
                            act.activation(lb[:, 2:4, :], lb[:, 0:2, :], ACT.Exp).then_inc(sem("lb_exp"), 1)
                        if p == 4:
                            for n, name in enumerate(("p", "p_2")):
                                act.dma_start(ptok[n][:, :, :], A[name][0, 0].rearrange("(t p) c -> p t c", p=P))\
                                    .then_inc(sem("p_loaded"), 16)
                            act.dma_start(gw[:, :, :], view(A["w_in"][0])[:, :, MI:MI + 8]).then_inc(sem("gw_loaded"), 16)
                            act.dma_start(gbias[:, 0:4], A["ml_b_i"][0].partition_broadcast(P)).then_inc(sem("gbias_loaded"), 16)
                            act.dma_start(gbias[:, 4:8], A["ml_b_f"][0].partition_broadcast(P)).then_inc(sem("gbias_loaded"), 16)
                        if p >= 4:
                            c = p - 4
                            for t in range(T):
                                squares(resid[:, t, c * COLS:(c + 1) * COLS], ss[:, SLOT["x"], t * 4 + c:t * 4 + c + 1])
                        if p == 7:
                            act.sem_inc(sem("ss_x"), 1)
                    if (s, p) == (1, 6):
                        act.wait_ge(sem("gw_loaded"), 16)
                        act.activation(gw_hi_lo[:, :, 0:8], gw[:, :, :], ACT.Copy).then_inc(sem("gw_hi"), 1)
                    if (s, p) == (2, 0):
                        for n in range(2):
                            act_split(AUX[("p" if n == 0 else "p2", 0)], pT[n], 0)
                    for half, L0 in enumerate(HG_START):
                        if w == L0 - 8:
                            if half == 1:
                                act.wait_ge(sem("hg_mul"), 8)
                            for i in range(2):
                                u = AUX[("tr", 3 * half, i)]
                                aux_filled(act, u)
                                act.activation(Eb[1][:, i * 512:(i + 1) * 512], bank(u), ACT.Sigmoid)
                                act.activation(kF[:, i * 512:(i + 1) * 512], bank(u), ACT.Sigmoid, scale=-1.0)\
                                    .then_inc(aux_free[u % 4], 1)
                        if w == L0 - 6:
                            act.wait_ge(sem("hg_f"), half + 1)
                            act.activation(Eb[1][:, :], Eb[0][:, :], ACT.Ln).then_inc(sem("hg_logf"), 1)
                        n, odd = divmod(w - L0, 2)
                        if 0 <= n < 8 and odd:
                            act.wait_ge(sem("hg_sub"), half * 8 + n + 1)
                            if n == 0:
                                act.activation(Eb[0][:, 0:512].rearrange("p (h t) -> p h t", h=4),
                                               bF[:, :].rearrange("p (h u t) -> p h u t", h=4, u=2)[:, :, 1, :], ACT.Exp)
                                act.activation(Eb[0][:, 512:1024], Eb[0][:, 512:1024], ACT.Exp).then_inc(sem("hg_exp"), 1)
                            else:
                                act.activation(Eb[n % 2][:, :], Eb[n % 2][:, :], ACT.Exp).then_inc(sem("hg_exp"), 1)
                        if w == L0 + 24:
                            act.wait_ge(sem("hg_out"), half + 1)
                            for t in range(T):
                                for h in range(4):
                                    c = (half * 4 + h) * P
                                    squares(ob[:, t, c:c + P], ss[:, SLOT[f"hB{half}"], t * 4 + h:t * 4 + h + 1])
                            act.sem_inc(sem("ss_hB"), 1)
                    if (s, p) in ((9, 3), (10, 1)):
                        act.wait_ge(sem("ml_conv"), s - 8)
                        x = qk[:, 4 * (s - 9):4 * (s - 8), :]
                        act.activation(x, x, ACT.Silu).then_inc(sem("ml_qk"), 1)
                    if (s, p) == (10, 5):
                        act.wait_ge(sem("ml_nf"), 1)
                        link(act.activation(gtmp[:, :, :], gtmp[:, :, :], ACT.Exp))
                        act.activation(gtmp[:, :, :], gtmp[:, :, :], ACT.Ln, bias=1.0).then_inc(sem("ml_ln"), 1)
                    if (s, p) == (11, 1):
                        act.wait_ge(sem("ml_rows"), 1)
                        act.activation(hrow[:, 5, :], hrow[:, 4, :], ACT.Exp, scale=-1.0).then_inc(sem("ml_em"), 1)
                    if (s, p) == (11, 5):
                        act.wait_ge(sem("ml_w_in"), 1)
                        act.activation(Wd[:, :, :], Wd[:, :, :], ACT.Exp).then_inc(sem("ml_w_exp"), 1)
                    if (s, p) == (12, 7):
                        act.wait_ge(sem("ml_h"), 1)
                        for t in range(T):
                            for h in range(4):
                                squares(hA[:, t, h * ML_DV:(h + 1) * ML_DV], ss[:, SLOT["hA"], t * 4 + h:t * 4 + h + 1])
                        act.sem_inc(sem("ss_hA"), 1)
                    if p == 3 and s - 1 in A_GATED:
                        gated(FIRST["A"] + s - 1, ACT.Sigmoid if s - 1 >= 14 else ACT.Silu, "x")
                    if (s, p) == (15, 0):
                        for i in range(4, 8):
                            act_split(AUX[("yT", i)], actB, 2 * i, gains[:, C_MIX:C_MIX + KD])
                    if (s, p) == (15, 6):
                        for i in range(2):
                            act_split(AUX[("yT", i)], actB, 2 * i, gains[:, C_MIX:C_MIX + KD])

            for s in range(4):
                for p in range(8):
                    split_hi(SLABS[FIRST["C"] + s][0] + p)
                    if s == 0 and p == 3:
                        gated(FIRST["A"] + 15, ACT.Sigmoid, "x")
                    if s == 0 and p == 5:
                        for i in range(2, 4):
                            act_split(AUX[("yT", i)], actB, 2 * i, gains[:, C_MIX:C_MIX + KD])
                    if s > 0 and p == 4:
                        act.wait_ge(sem("h_added"), s)
                        for t in range(T):
                            squares(resid[:, t, (s - 1) * COLS:s * COLS], ss[:, SLOT["h1"], t * 4 + s - 1:t * 4 + s])
                    if s > 0 and p == 5:
                        for i in range(2):
                            act_split(AUX[("hD", 2 * s - 2 + i)], actA, 4 * s - 4 + 2 * i, gains[:, C_PE:C_PE + KD])

            def d_squares(s, name, signal, count):
                act.wait_ge(sem(signal), count)
                for t in range(T):
                    squares(resid[:, t, s * COLS:(s + 1) * COLS], ss[:, SLOT[name], t * 4 + s:t * 4 + s + 1])
                act.sem_inc(sem("ss_" + name), 1)

            for s in range(4):
                split_hi(SLABS[FIRST["D"] + 2 * s][0])
                for p in range(8):
                    split_hi(SLABS[FIRST["D"] + 2 * s + 1][0] + p)
                    if s == 0 and p == 3:
                        act.wait_ge(sem("h_added"), 4)
                        for t in range(T):
                            squares(resid[:, t, 3 * COLS:4 * COLS], ss[:, SLOT["h1"], t * 4 + 3:t * 4 + 4])
                        act.sem_inc(sem("ss_h1"), 1)
                    if s == 0 and p == 5:
                        for i in range(6, 8):
                            act_split(AUX[("hD", i)], actA, 2 * i, gains[:, C_PE:C_PE + KD])
                    if s > 0:
                        if p == 1:
                            gated(FIRST["D"] + 2 * s - 1, ACT.Sigmoid, "h1")
                        if p == 4:
                            d_squares(s - 1, "f1", "h_gated", s)
                        if p == 6:
                            for i in range(2):
                                act_split(AUX[("hE", 2 * s - 2 + i)], actB, 4 * s - 4 + 2 * i, gain_e)
                        if p == 7:
                            d_squares(s - 1, "f2", "h_final", s)

            for s in range(10):
                for p in range(8):
                    n = FIRST["E1"] + s
                    split_hi(SLABS[n][0] + p)
                    w = s * 8 + p
                    if s == 0:
                        if p == 2:
                            gated(n - 1, ACT.Sigmoid, "h1")
                        if p == 4:
                            d_squares(3, "f1", "h_gated", 4)
                        if p == 5:
                            for i in range(6, 8):
                                act_split(AUX[("hE", i)], actB, 2 * i, gain_e)
                        if p == 7:
                            d_squares(3, "f2", "h_final", 4)
                    if 1 <= s <= 4 and p == 4:
                        act.wait_ge(sem("qk_tok"), s)
                        for t in range(T):
                            for h in range(4):
                                squares(gate[(s - 1) % 2][:, t, h * P:(h + 1) * P],
                                        ss[:, SLOT[f"qk{s - 1}"], t * 4 + h:t * 4 + h + 1])
                        act.sem_inc(sem("ss_qk"), 1)
                    for b, z0 in enumerate(ATT_START):
                        if w == z0 + 6:
                            act.wait_ge(sem("att_z"), b + 1)
                            link(act.activation(ab[:, :, :], zt[:, :, :], ACT.Abs))
                            link(act.activation(ab[:, :, :], ab[:, :, :], ACT.Exp, scale=-1.0))
                        if w == z0 + 7:
                            act.activation(ab[:, :, :], ab[:, :, :], ACT.Ln, bias=1.0).then_inc(sem("att_ln"), 1)
                        if w == z0 + 14:
                            act.wait_ge(sem("att_arg"), b + 1)
                            act.activation(zt[:, :, :], zt[:, :, :], ACT.Exp).then_inc(sem("att_w"), 1)
                    if s in (7, 8) and p == 3:
                        gated(n - 1, ACT.Gelu_apprx_tanh, "r_e", vs[:, :, (s - 7) * COLS:(s - 6) * COLS])
                    if s == 9 and p == 3:
                        gated(n - 1, ACT.Gelu_apprx_tanh, "r_e", u2[:, :, 0:COLS])
                    if s in (7, 8) and p == 4:
                        slab_taken(act, n - 1)
                        for t in range(T):
                            for h in range(4):
                                c = ((s - 7) * 4 + h) * P
                                squares(vs[:, t, c:c + P], ss[:, SLOT[f"s{s - 7}"], t * 4 + h:t * 4 + h + 1])
                        act.sem_inc(sem("ss_s"), 1)
                    if s == 9 and p == 7:
                        for i in range(2):
                            act_split(AUX[("yaT", i)], actA, 2 * i)

            for ph in ("E2", "E3"):
                for s in range(8):
                    n = FIRST[ph] + s
                    for p in range(SLABS[n][1]):
                        split_hi(SLABS[n][0] + p)
                        if p == 3 and ph == "E2" and s == 0:
                            gated(n - 1, ACT.Gelu_apprx_tanh, "r_e", u2[:, :, COLS:2 * COLS])
                        if p == 3 and s % 2 == 1:
                            gated(n - 1, ACT.Sigmoid, "r_e")
                        if ph == "E2" and s == 0 and p == 6:
                            for i in range(2, 4):
                                act_split(AUX[("yaT", i)], actA, 2 * i)
                        if ph == "E2" and s == 0 and p == 7:
                            for i in range(4):
                                act_split(AUX[("ybT", i)], actA, 8 + 2 * i)
                        if ph == "E3" and s >= 2 and s % 2 == 0 and p == 6:
                            for i in range(2):
                                act_split(AUX[("mT", s - 2 + i)], actF, 2 * (s - 2 + i))

            def added_squares(s, name, count):
                act.wait_ge(sem("h_added"), count)
                for t in range(T):
                    squares(resid[:, t, s * COLS:(s + 1) * COLS], ss[:, SLOT[name], t * 4 + s:t * 4 + s + 1])

            for s in range(4):
                for p in range(8):
                    split_hi(SLABS[FIRST["G"] + s][0] + p)
                    if s == 0 and p == 5:
                        for i in range(6, 8):
                            act_split(AUX[("mT", i)], actF, 2 * i)
                    if s > 0 and p == 4:
                        added_squares(s - 1, "ffn", 4 + s)
                    if s > 0 and p == 5:
                        for i in range(2):
                            act_split(AUX[("hH", 2 * s - 2 + i)], actA, 4 * s - 4 + 2 * i, gains[:, C_FFN:C_FFN + KD])

            for part, (f0, width) in enumerate(FFN_PARTS):
                nh = width // COLS
                for s in range(2 * nh):
                    n = FIRST[f"H{part}"] + s
                    for p in range(8):
                        split_hi(SLABS[n][0] + p)
                        if s == 0 and part == 0:
                            if p == 4:
                                added_squares(3, "ffn", 8)
                                act.sem_inc(sem("ss_ffn"), 1)
                            if p == 5:
                                for i in range(6, 8):
                                    act_split(AUX[("hH", i)], actA, 2 * i, gains[:, C_FFN:C_FFN + KD])
                        if s % 2 == 1 and p == 3:
                            gated(n - 1, ACT.Silu, "ffn")
                        if s > 0 and s % 2 == 0 and p == 6:
                            for c in range(4):
                                act_split(AUX[("hid", part, 2 * s - 4 + c)], actF, 2 * s - 4 + c, n=1)
                for s in range(4):
                    n = FIRST[f"O{part}"] + s
                    for p in range(SLABS[n][1]):
                        split_hi(SLABS[n][0] + p)
                        if s == 0 and p == 4:
                            for c in range(4):
                                act_split(AUX[("hid", part, 4 * nh - 4 + c)], actF, 4 * nh - 4 + c, n=1)
                        if part == 2 and s > 0 and p == 4:
                            added_squares(s - 1, "ple", 16 + s)
                        if part == 2 and s > 0 and p == 5:
                            for i in range(2):
                                act_split(AUX[("hJ", 2 * s - 2 + i)], actB, 4 * s - 4 + 2 * i, gains[:, C_PLE:C_PLE + KD])

            for s in range(4):
                split_hi(SLABS[FIRST["J"] + 2 * s][0])
                for p in range(8):
                    split_hi(SLABS[FIRST["J"] + 2 * s + 1][0] + p)
                    if s == 0 and p == 3:
                        added_squares(3, "ple", 20)
                        act.sem_inc(sem("ss_ple"), 1)
                    if s == 0 and p == 5:
                        for i in range(6, 8):
                            act_split(AUX[("hJ", i)], actB, 2 * i, gains[:, C_PLE:C_PLE + KD])
                    if s > 0 and p == 1:
                        if s > 2:
                            act.wait_ge(sem("out_ready"), s - 2)
                        gated(FIRST["J"] + 2 * s - 1, ACT.Sigmoid, "ple")
            act.wait_ge(sem("out_ready"), 2)
            gated(FIRST["J"] + 7, ACT.Sigmoid, "ple")

        @block.tensor
        def _(pe):
            def transposes(name, src, c0, n=2):
                u = AUX[name]
                free(u)
                for c in range(n):
                    for t in range(T):
                        ins = pe.transpose(bank(u)[:, c * S + t * P:c * S + (t + 1) * P],
                                           src[:, t, (c0 + c) * P:(c0 + c + 1) * P], ident[:, :])
                ins.then_inc(aux_full, 1)

            def free(u):
                if u >= 4:
                    aux_taken(pe, u - 4)

            def piece(n, p, act, k, last):
                g = SLABS[n][0] + p
                if p == 0 and n >= 2:
                    slab_taken(pe, n - 2)
                pe.wait_ge(hi_ready, g + 1)
                for c in range(PK):
                    for t in range(T):
                        for x in range(2):
                            pe.matmul(acc2(n)[:, t, :], act[x][:, k + c, t * P:(t + 1) * P], whi[:, g % RING, c, :],
                                      start=(p == 0 and c == 0 and x == 0), stop=False)
                pe.wait_ge(lo_ready, g + 1)
                for c in range(PK):
                    for t in range(T):
                        ins = pe.matmul(acc2(n)[:, t, :], act[0][:, k + c, t * P:(t + 1) * P], wlo[:, g % RING, c, :],
                                        start=False, stop=(last and c == PK - 1))
                ins.then_inc(piece_used, 1)

            pe.wait_ge(sem("ident_ready"), 1)
            pe.wait_ge(sem("small_loaded"), 16 * 14)
            pe.transpose(bank(0)[:, 0:P], stage1[:, :], ident[:, :])
            pe.transpose(bank(0)[:, P:C_END], stage2[:, :], ident[0:C_END - P, 0:C_END - P]).then_inc(aux_full, 1)

            def transpose_x(i):
                if i % 2 == 0:
                    pe.wait_ge(sem(f"x_loaded{i // 2}"), 16)
                transposes(("xT", i), resid, 2 * i)

            for i in range(4):
                transpose_x(i)

            def tr_slab(s):
                n = FIRST["A"] + s
                slab_taken(pe, n)
                for i in range(2):
                    transposes(("tr", s, i), gate[s % 2], 2 * i)

            def hg_diag(half):
                pe.wait_ge(sem("hg_k"), half + 1)
                aux_taken(pe, AUX[("tr", 3 * half + 1, 1)])
                for i in range(2):
                    u = AUX[("diag", half, i)]
                    free(u)
                    for j in range(4):
                        c = (4 * i + j) * P
                        ins = pe.matmul(bank(u)[:, j * P:(j + 1) * P], kF[:, c:c + P], qF[:, c:c + P], start=True, stop=True)
                    ins.then_inc(aux_full, 1)

            def hg_level(half, n):
                u = AUX[("level", half, n)]
                pe.wait_ge(sem("hg_mul"), half * 8 + n + 1)
                free(u)
                for j in range(4 if n == 0 else 8):
                    m = P if n == 0 else 64
                    c = (2 * j if n == 0 else j) * P
                    ins = pe.matmul(bank(u)[:, j * m:(j + 1) * m], Kp[n % 2][:, c:c + P], Qp[n % 2][:, j * m:(j + 1) * m],
                                    start=True, stop=True)
                ins.then_inc(aux_full, 1)

            def hg_pv(half):
                aux_taken(pe, AUX[("level", half, 7)])
                slab_taken(pe, FIRST["A"] + 2 + 3 * half)
                for t in range(T):
                    u = AUX[("pv", half, t)]
                    free(u)
                    for h in range(4):
                        c = (half * 4 + h) * P
                        o = bank(u)[:, h * P:(h + 1) * P]
                        if t == 1:
                            pe.matmul(o, A01[:, h, :], ob[:, 0, c:c + P], start=True, stop=False)
                        ins = pe.matmul(o, Am[:, 2 * h + t, :], ob[:, t, c:c + P], start=(t == 0), stop=True)
                    ins.then_inc(aux_full, 1)

            def ml_gates():
                u = AUX[("gates", 0)]
                pe.wait_ge(sem("gw_lo"), 1)
                free(u)
                for k in range(KD):
                    pe.matmul(aux[0:16, u % 4, 0:S], gw_hi_lo[:, k, :], actA[0][:, k, :], start=(k == 0), stop=False)
                    ins = pe.matmul(aux[0:8, u % 4, 0:S], gw_hi_lo[:, k, 0:8], actA[1][:, k, :], start=False, stop=(k == KD - 1))
                ins.then_inc(aux_full, 1)

            def ml_gates_by_token():
                u = AUX[("gatesT", 0)]
                aux_taken(pe, AUX[("gates", 0)])
                free(u)
                for t in range(T):
                    ins = pe.transpose(bank(u)[:, t * 16:(t + 1) * 16], gates_ch[:, t * P:(t + 1) * P], ident[0:16, 0:16])
                ins.then_inc(aux_full, 1)

            def ml_gates_tr():
                u = AUX[("gtr", 0)]
                pe.wait_ge(sem("ml_lf"), 1)
                free(u)
                for x in range(2):
                    for t in range(T):
                        ins = pe.transpose(aux[0:4, u % 4, x * S + t * P:x * S + (t + 1) * P], gtok[:, t, 4 * x:4 * x + 4],
                                           ident[:, :])
                ins.then_inc(aux_full, 1)

            def ml_cols():
                u = AUX[("atr", 0)]
                pe.wait_ge(sem("ml_em"), 1)
                free(u)
                for x, row in ((0, 1), (1, 5)):
                    for t in range(T):
                        ins = pe.transpose(bank(u)[:, x * 8 + t * 4:x * 8 + t * 4 + 4], hrow[:, row, t * P:(t + 1) * P],
                                           ident[0:4, 0:4])
                ins.then_inc(aux_full, 1)
                for i in range(2):
                    u = AUX[("bc", i)]
                    free(u)
                    for h in range(2):
                        ins = pe.matmul(bank(u)[:, h * S:(h + 1) * S], sel[:, 2 * i + h, :], hrow[:, 3, :], start=True, stop=True)
                    ins.then_inc(aux_full, 1)

            def ml_scores():
                pe.wait_ge(sem("ml_qk"), 2)
                for h in range(4):
                    u = AUX[("st", h)]
                    free(u)
                    pe.matmul(bank(u)[:, 0:S], qk[:, 4 + h, 0:P], qk[:, h, :], start=True, stop=True)
                    pe.matmul(bank(u)[:, S:S + P], qk[:, 4 + h, P:S], qk[:, h, P:S], start=True, stop=True).then_inc(aux_full, 1)

            def ml_pv(h):
                aux_taken(pe, AUX[("st", h)])
                slab_taken(pe, FIRST["A"] + 9 + h // 2)
                for t in range(T):
                    u = AUX[("mpv", h, t)]
                    free(u)
                    o = bank(u)[:, 0:ML_DV + 1]
                    if t == 0:
                        ins = pe.matmul(o, Wd[:, h, 0:P], vml[:, 0, h, 0:ML_DV + 1], start=True, stop=True)
                    else:
                        pe.matmul(o, Wd[:, h, P:S], vml[:, 0, h, 0:ML_DV + 1], start=True, stop=False)
                        ins = pe.matmul(o, Wd[:, h, S:S + P], vml[:, 1, h, 0:ML_DV + 1], start=False, stop=True)
                    ins.then_inc(aux_full, 1)

            for s in range(16):
                n = FIRST["A"] + s
                for p in range(8):
                    if s == 0:
                        aux_taken(pe, AUX[("xT", p)])
                    piece(n, p, actA, p * PK, p == 7)
                    w = s * 8 + p
                    if s == 0 and p < 4:
                        transpose_x(p + 4)
                    if p == 2 and s - 1 in A_TRANSPOSED:
                        tr_slab(s - 1)
                    if (s, p) == (1, 4):
                        pe.wait_ge(sem("p_loaded"), 32)
                        transposes(("p", 0), ptok[0], 0)
                        transposes(("p2", 0), ptok[1], 0)
                    for half, L0 in enumerate(HG_START):
                        if w == L0 - 3:
                            hg_diag(half)
                        n_level, odd = divmod(w - L0, 2)
                        if 0 <= n_level < 8 and not odd:
                            hg_level(half, n_level)
                        if w == L0 + 18:
                            hg_pv(half)
                    if (s, p) == (9, 4):
                        ml_gates()
                    if (s, p) == (9, 7):
                        ml_gates_by_token()
                    if (s, p) == (10, 4):
                        ml_gates_tr()
                    if (s, p) == (10, 7):
                        ml_cols()
                    if (s, p) == (11, 4):
                        ml_scores()
                    for h in range(4):
                        if w == 95 + h:
                            ml_pv(h)
                    if (s, p) == (14, 4):
                        pe.wait_ge(sem("yb_ready"), 2)
                        for i in range(4, 8):
                            transposes(("yT", i), ob, 2 * i - 8)
                    if (s, p) == (15, 2):
                        pe.wait_ge(sem("ya_ready"), 1)
                        for i in range(2):
                            transposes(("yT", i), hA, 2 * i)

            for s in range(4):
                n = FIRST["C"] + s
                for p in range(8):
                    k = (KD // 2 + p * PK) % KD
                    if s == 0:
                        aux_taken(pe, AUX[("yT", k // PK)])
                    piece(n, p, actB, k, p == 7)
                    if s == 0 and p == 1:
                        pe.wait_ge(sem("ya_ready"), 2)
                        for i in range(2, 4):
                            transposes(("yT", i), hA, 2 * i)
                    if s > 0 and p == 1:
                        pe.wait_ge(sem("h_added"), s)
                        for i in range(2):
                            transposes(("hD", 2 * s - 2 + i), resid, 4 * s - 4 + 2 * i)

            for s in range(4):
                n = FIRST["D"] + 2 * s
                piece(n, 0, pT[0], 0, True)
                for p in range(8):
                    if s == 0:
                        aux_taken(pe, AUX[("hD", p)])
                    piece(n + 1, p, actA, p * PK, p == 7)
                    if s == 0 and p == 1:
                        pe.wait_ge(sem("h_added"), 4)
                        for i in range(6, 8):
                            transposes(("hD", i), resid, 2 * i)
                    if s > 0 and p == 2:
                        pe.wait_ge(sem("h_gated"), s)
                        for i in range(2):
                            transposes(("hE", 2 * s - 2 + i), resid, 4 * s - 4 + 2 * i)

            def tr2_slab(s):
                pe.wait_ge(sem("qk_normed"), s + 1)
                for i in range(2):
                    transposes(("tr2", s, i), gate[s % 2], 2 * i)

            def spatial_weights():
                pe.wait_ge(sem("ws_masked"), 1)
                for i in range(2):
                    u = AUX[("ws", i)]
                    free(u)
                    for j in range(4):
                        ins = pe.transpose(bank(u)[:, j * P:(j + 1) * P], wsr[:, 4 * i + j, :], ident[:, :])
                    ins.then_inc(aux_full, 1)

            def att_scores(b):
                aux_taken(pe, AUX[("tr2", 1 if b else 0, 1)])
                aux_taken(pe, AUX[("tr2", 3 if b else 2, 1)])
                for j in range(4):
                    u, h = AUX[("z", b, j)], 4 * b + j
                    free(u)
                    pe.matmul(bank(u)[:, 0:S], kT[:, h, 0:P], qT[:, h, :], start=True, stop=True)
                    pe.matmul(bank(u)[:, S:S + P], kT[:, h, P:S], qT[:, h, P:S], start=True, stop=True).then_inc(aux_full, 1)

            def att_tail(b):
                pe.wait_ge(sem("att_l"), b + 1)
                for j in range(4):
                    u = AUX[("tail", b, j)]
                    free(u)
                    o = bank(u)
                    pe.matmul(o[:, 0:S], later[:, :], Lp[:, j, 0:S], start=True, stop=False)
                    pe.matmul(o[:, P:S], ones[:, 0:P], Lp[:, j, S:S + P], start=False, stop=True)
                    pe.matmul(o[:, S:S + P], later[:, :], Lp[:, j, S:S + P], start=True, stop=True).then_inc(aux_full, 1)

            def att_pv(b):
                pe.wait_ge(sem("att_masked"), b + 1)
                slab_taken(pe, FIRST["E1"] + 4 + b)
                for t in range(T):
                    u = AUX[("att", b, t)]
                    free(u)
                    for j in range(4):
                        c = (4 * b + j) * P
                        o = bank(u)[:, j * P:(j + 1) * P]
                        if t == 0:
                            ins = pe.matmul(o, zt[:, j, 0:P], vA[:, 0, c:c + P], start=True, stop=True)
                        else:
                            pe.matmul(o, zt[:, j, P:S], vA[:, 0, c:c + P], start=True, stop=False)
                            ins = pe.matmul(o, zt[:, j, S:S + P], vA[:, 1, c:c + P], start=False, stop=True)
                    ins.then_inc(aux_full, 1)

            def spatial_mix(half):
                pe.wait_ge(sem("vs_ready"), half + 1)
                for i in range(2):
                    u = AUX[("sgu", 2 * half + i)]
                    free(u)
                    for j in range(2):
                        g = 4 * half + 2 * i + j
                        ins = pe.matmul(bank(u)[:, j * S:(j + 1) * S].rearrange("p (t c) -> p t c", t=T), wsT[:, g, :],
                                        vs[:, :, g * P:(g + 1) * P], start=True, stop=True)
                    ins.then_inc(aux_full, 1)

            for s in range(10):
                n = FIRST["E1"] + s
                for p in range(8):
                    if s == 0:
                        aux_taken(pe, AUX[("hE", p)])
                    piece(n, p, actB, p * PK, p == 7)
                    w = s * 8 + p
                    if s == 0 and p == 2:
                        pe.wait_ge(sem("h_gated"), 4)
                        for i in range(6, 8):
                            transposes(("hE", i), resid, 2 * i)
                    if 1 <= s <= 4 and p == 5:
                        tr2_slab(s - 1)
                    if (s, p) == (2, 1):
                        spatial_weights()
                    for b, z0 in enumerate(ATT_START):
                        if w == z0:
                            att_scores(b)
                        if w == z0 + 7:
                            att_tail(b)
                        if w == z0 + 14:
                            att_pv(b)
                    if (s, p) == (9, 1):
                        spatial_mix(0)
                    if (s, p) == (9, 3):
                        pe.wait_ge(sem("ya2_ready"), 1)
                        for i in range(2):
                            transposes(("yaT", i), u2, 2 * i)

            for ph in ("E2", "E3"):
                for s in range(8):
                    n = FIRST[ph] + s
                    for p in range(SLABS[n][1]):
                        if s % 2 == 0:
                            piece(n, p, actB, p * PK, p == 7)
                        else:
                            if s == 1:
                                aux_taken(pe, AUX[("yaT" if ph == "E2" else "ybT", p)])
                            piece(n, p, actA, (0 if ph == "E2" else 8) + p * PK, p == 3)
                        if ph == "E2" and s == 0:
                            if p == 0:
                                spatial_mix(1)
                            if p == 3:
                                pe.wait_ge(sem("ya2_ready"), 2)
                                for i in range(2, 4):
                                    transposes(("yaT", i), u2, 2 * i)
                            if p == 4:
                                for i in range(4):
                                    aux_taken(pe, AUX[("att", i // 2, 1)])
                                    transposes(("ybT", i), vA, 2 * i)
                        if ph == "E3" and s >= 2 and s % 2 == 0 and p == 1:
                            pe.wait_ge(sem("merged_ready"), s // 2)
                            for i in range(2):
                                transposes(("mT", s - 2 + i), merged, 2 * (s - 2 + i))

            for s in range(4):
                n = FIRST["G"] + s
                for p in range(8):
                    if s == 0:
                        aux_taken(pe, AUX[("mT", p)])
                    piece(n, p, actF, p * PK, p == 7)
                    if s == 0 and p == 1:
                        pe.wait_ge(sem("merged_ready"), 4)
                        for i in range(6, 8):
                            transposes(("mT", i), merged, 2 * i)
                    if s > 0 and p == 1:
                        pe.wait_ge(sem("h_added"), 4 + s)
                        for i in range(2):
                            transposes(("hH", 2 * s - 2 + i), resid, 4 * s - 4 + 2 * i)

            def tr_hidden(part, j):
                pe.wait_ge(sem("hid_ready"), sum(w // COLS for _, w in FFN_PARTS[:part]) + j + 1)
                for c in range(4):
                    transposes(("hid", part, 4 * j + c), hid, c, n=1)

            for part, (f0, width) in enumerate(FFN_PARTS):
                nh = width // COLS
                for s in range(2 * nh):
                    n = FIRST[f"H{part}"] + s
                    for p in range(8):
                        if s == 0 and part == 0:
                            aux_taken(pe, AUX[("hH", p)])
                        piece(n, p, actA, p * PK, p == 7)
                        if s == 0 and part == 0 and p == 1:
                            pe.wait_ge(sem("h_added"), 8)
                            for i in range(6, 8):
                                transposes(("hH", i), resid, 2 * i)
                        if s > 0 and s % 2 == 0 and p == 1:
                            tr_hidden(part, s // 2 - 1)
                for s in range(4):
                    n = FIRST[f"O{part}"] + s
                    for p in range(2 * nh):
                        if s == 0:
                            aux_taken(pe, AUX[("hid", part, 2 * p)])
                            aux_taken(pe, AUX[("hid", part, 2 * p + 1)])
                        piece(n, p, actF, p * PK, p == 2 * nh - 1)
                        if s == 0 and p == 1:
                            tr_hidden(part, nh - 1)
                        if part == 2 and s > 0 and p == 1:
                            pe.wait_ge(sem("h_added"), 16 + s)
                            for i in range(2):
                                transposes(("hJ", 2 * s - 2 + i), resid, 4 * s - 4 + 2 * i)

            for s in range(4):
                n = FIRST["J"] + 2 * s
                piece(n, 0, pT[1], 0, True)
                for p in range(8):
                    if s == 0:
                        aux_taken(pe, AUX[("hJ", p)])
                    piece(n + 1, p, actB, p * PK, p == 7)
                    if s == 0 and p == 1:
                        pe.wait_ge(sem("h_added"), 20)
                        for i in range(6, 8):
                            transposes(("hJ", i), resid, 2 * i)

        @block.vector
        def _(dve):
            steps = [0]
            gates = [0]

            def link(ins):
                steps[0] += 1
                ins.then_inc(sem("dve_step"), 1)
                dve.wait_ge(sem("dve_step"), steps[0])

            def split_lo(g):
                dve.wait_ge(hi_ready, g + 1)
                dve.tensor_tensor(wlo[:, g % RING], raw[:, g % RING], whi[:, g % RING].bitcast(F32), ALU.subtract)\
                    .then_inc(lo_ready, 1)

            splits = [0]

            def lo_split(u, dst, c0, gain=None, n=2):
                splits[0] += 1
                dve.wait_ge(split_hi_done, splits[0])
                for c in range(n):
                    x = bank(u)[:, c * S:(c + 1) * S]
                    hi = dst[0][:, c0 + c, :].bitcast(F32)
                    if gain is None:
                        ins = dve.tensor_tensor(dst[1][:, c0 + c, :], x, hi, ALU.subtract)
                    else:
                        ins = dve.scalar_tensor_tensor(out=dst[1][:, c0 + c, :], in0=x, scalar=gain[:, c0 + c:c0 + c + 1],
                                                       in1=hi, op0=ALU.mult, op1=ALU.subtract)
                ins.then_inc(aux_free[u % 4], 1)

            def variance(name, width, sums=None):
                i, n = SLOT[name], dict(POWS)[name]
                dve.tensor_scalar(var[:, i, 0:n], ss[:, i, 0:n] if sums is None else sums, 1.0 / width, EPS, ALU.mult, ALU.add)\
                    .then_inc(pow_in, 1)

            def row_variance(name):
                i = SLOT[name]
                link(dve.tensor_reduce(var[:, i, 4:6], ss[:, i, :].rearrange("p (t c) -> p t c", t=T), AX.X, ALU.add))
                variance(name, D, var[:, i, 4:6])

            def scaled(n, dst, r):
                slab_made(dve, n)
                for t in range(T):
                    x = acc2(n)[:, t, :]
                    d = dst[:, t]
                    if len(d.shape) == 3:
                        x = x.rearrange("p (h c) -> p h c", h=d.shape[1])
                    ins = dve.tensor_scalar(d, x, r(t), None, ALU.mult)
                return ins

            def next_gate():
                gates[0] += 1
                dve.wait_ge(gate_ready, gates[0])
                return gate[(gates[0] - 1) % 2]

            aux_filled(dve, 0)
            dve.tensor_copy(gains[:, :], bank(0, C_END)).then_inc(aux_free[0], 1)
            aux_taken(dve, 0)
            dve.tensor_tensor(gain_e[:, :], gains[:, C_ATTN:C_ATTN + KD], gains[:, C_FW:C_FW + KD], ALU.mult)
            dve.tensor_scalar(qn_scaled[:, :], gains[:, C_QN:C_QN + 1], SB_D ** -0.5, None, ALU.mult)
            lb_rows = gains[:, C_LB:C_LB + 16].rearrange("p (l h) -> p l h", l=2)
            link(dve.tensor_tensor(lb[:, 2, :], lb_rows[:, 0, :], lb_rows[:, 1, :], ALU.max))
            dve.tensor_tensor(lb[:, 0:2, :], lb_rows, lb[:, 2:3, :].to_broadcast([P, 2, 8]), ALU.subtract).then_inc(sem("lb_in"), 1)

            def lower_bounds():
                dve.wait_ge(sem("lb_exp"), 1)
                link(dve.tensor_tensor(lb[:, 0, :], lb[:, 2, :], lb[:, 3, :], ALU.add))
                link(dve.reciprocal(lb[:, 1, :], lb[:, 0, :]))
                link(dve.tensor_tensor(lb[:, 0, :], lb[:, 2, :], lb[:, 1, :], ALU.mult))
                link(dve.tensor_scalar(lb[:, 1, :], lb[:, 0, :], -1.0, 1.0, ALU.mult, ALU.add))

            def hg_forget(half):
                aux_taken(dve, AUX[("tr", 3 * half, 1)])
                for h in range(4):
                    c = slice(h * S, (h + 1) * S)
                    e = half * 4 + h
                    ins = dve.tensor_scalar(Eb[0][:, c], Eb[1][:, c], lb[:, 1, e:e + 1], lb[:, 0, e:e + 1], ALU.mult, ALU.add)
                ins.then_inc(sem("hg_f"), 1)

            def hg_cumsum(half):
                dve.wait_ge(sem("hg_logf"), half + 1)
                for h in range(4):
                    e = half * 4 + h
                    c = slice(h * S, (h + 1) * S)
                    ins = dve.tensor_scalar(kF[:, c], kF[:, c], lb[:, 1, e:e + 1], None, ALU.mult)
                ins.then_inc(sem("hg_k"), 1)
                for j in range(8):
                    c = slice(j * P, (j + 1) * P)
                    ins = dve.tensor_tensor_scan(bF[:, c], ones[:, 0:P], Eb[1][:, c], 0.0, ALU.mult, ALU.add)
                link(ins)

            def hg_queries(half):
                for i in range(2):
                    u = AUX[("tr", 3 * half + 1, i)]
                    aux_filled(dve, u)
                    dve.tensor_copy(qF[:, i * 512:(i + 1) * 512], bank(u)).then_inc(aux_free[u % 4], 1)

            def hg_diagonal(half):
                for i in range(2):
                    u = AUX[("diag", half, i)]
                    aux_filled(dve, u)
                    dve.tensor_tensor(Am[:, 4 * i:4 * i + 4, :], bank(u).rearrange("p (g t) -> p g t", g=4),
                                      ident[:, :].unsqueeze(1).to_broadcast([P, 4, P]), ALU.mult).then_inc(aux_free[u % 4], 1)

            def halves(x, s):
                return x[:, :].rearrange("p (n u s) -> p n u s", u=2, s=s)

            def hg_sub(half, n):
                s = LEVELS[n]
                b, nb = halves(bF, s), 512 // s
                mid = b[:, :, 0, s - 1:s].to_broadcast([P, nb, s])
                e = Eb[n % 2][:, :].rearrange("p (x n s) -> p x n s", x=2, s=s)
                if n > 0:
                    dve.tensor_tensor(e[:, 0], b[:, :, 1, :], mid, ALU.subtract)
                dve.tensor_tensor(e[:, 1], mid, b[:, :, 0, :], ALU.subtract).then_inc(sem("hg_sub"), 1)

            def hg_mul(half, n):
                s = LEVELS[n]
                dve.wait_ge(sem("hg_exp"), half * 8 + n + 1)
                if n >= 2:
                    aux_filled(dve, AUX[("level", half, n - 2)])
                e = Eb[n % 2][:, :].rearrange("p (x n s) -> p x n s", x=2, s=s)
                dve.tensor_tensor(Qp[n % 2][:, :].rearrange("p (n s) -> p n s", s=s), halves(qF, s)[:, :, 1, :], e[:, 0], ALU.mult)
                dve.tensor_tensor(halves(Kp[n % 2], s)[:, :, 0, :], halves(kF, s)[:, :, 0, :], e[:, 1], ALU.mult)\
                    .then_inc(sem("hg_mul"), 1)

            def hg_take(half, n):
                s = LEVELS[n]
                u = AUX[("level", half, n)]
                aux_filled(dve, u)
                if n == 0:
                    ins = dve.tensor_copy(A01[:, :, :], bank(u).rearrange("p (h t) -> p h t", h=4))
                else:
                    aux_taken(dve, AUX[("diag", half, 1) if n == 1 else ("level", half, n - 1)])
                    nb = 64 // s
                    dst = Am[:, :, :].rearrange("p g (n u s) -> p g n u s", u=2, s=s)[:, :, :, 1, :]
                    m = lmask[:, n - 1, :].bitcast(I32).rearrange("p (n s) -> p n s", s=s).unsqueeze(1).to_broadcast([P, 8, nb, s])
                    ins = dve.copy_predicated(dst, m, bank(u).rearrange("p (g n s) -> p g n s", g=8, s=s))
                ins.then_inc(aux_free[u % 4], 1)

            def hg_output(half):
                aux_filled(dve, AUX[("pv", half, 1)])
                for t in range(T):
                    u = AUX[("pv", half, t)]
                    dve.tensor_copy(ob[:, t, half * 512:(half + 1) * 512], bank(u)).then_inc(aux_free[u % 4], 1)
                for t in range(T):
                    aux_taken(dve, AUX[("pv", half, t)])
                dve.sem_inc(sem("hg_out"), 1)

            def ml_conv(s):
                for i in range(2):
                    u = AUX[("tr", s, i)]
                    aux_filled(dve, u)
                    for tap in range(ML_TAPS - 1, -1, -1):
                        back = ML_TAPS - 1 - tap
                        for c in range(2):
                            ch = 4 * (s - 7) + 2 * i + c
                            x, y = bank(u)[:, c * S:(c + 1) * S], qk[:, ch, :]
                            w = gains[:, C_CONVW + tap * 8 + ch:C_CONVW + tap * 8 + ch + 1]
                            if back == 0:
                                ins = dve.tensor_scalar(y, x, w, gains[:, C_CONVB + ch:C_CONVB + ch + 1], ALU.mult, ALU.add)
                            else:
                                ins = dve.scalar_tensor_tensor(out=y[:, back:S], in0=x[:, 0:S - back], scalar=w,
                                                               in1=y[:, back:S], op0=ALU.mult, op1=ALU.add)
                            if tap > 0 and c == 1:
                                link(ins)
                    ins.then_inc(aux_free[u % 4], 1)
                    aux_taken(dve, u)
                dve.sem_inc(sem("ml_conv"), 1)

            def ml_gates_out():
                u = AUX[("gates", 0)]
                aux_filled(dve, u)
                dve.tensor_copy(gates_ch[:, :], aux[0:16, u % 4, 0:S]).then_inc(aux_free[u % 4], 1)

            def ml_gates():
                u = AUX[("gatesT", 0)]
                aux_filled(dve, u)
                dve.wait_ge(sem("gbias_loaded"), 32)
                for part in range(2):
                    for t in range(T):
                        x = bank(u)[:, t * 16 + part * 8:t * 16 + part * 8 + 8]
                        ins = dve.scalar_tensor_tensor(out=gtok[:, t, :], in0=x, scalar=r_tok("x", t),
                                                       in1=gtok[:, t, :] if part else gbias[:, :], op0=ALU.mult, op1=ALU.add)
                    if part == 0:
                        link(ins)
                ins.then_inc(aux_free[u % 4], 1)
                aux_taken(dve, u)
                f = gtok[:, :, 4:8]
                dve.scalar_tensor_tensor(out=gtmp[:, :, :], in0=f, scalar=-1.0, in1=f, op0=ALU.mult, op1=ALU.min)\
                    .then_inc(sem("ml_nf"), 1)

            def ml_logf():
                f = gtok[:, :, 4:8]
                dve.wait_ge(sem("ml_ln"), 1)
                dve.scalar_tensor_tensor(out=f, in0=f, scalar=0.0, in1=gtmp[:, :, :], op0=ALU.min, op1=ALU.subtract)\
                    .then_inc(sem("ml_lf"), 1)

            def ml_rows():
                u = AUX[("gtr", 0)]
                aux_filled(dve, u)
                gi, lf = aux[0:4, u % 4, 0:S], aux[0:4, u % 4, S:2 * S]
                link(dve.tensor_tensor_scan(hrow[:, 0, :], ones[0:4, :], lf, 0.0, ALU.mult, ALU.add))
                dve.tensor_tensor(hrow[:, 1, :], gi, hrow[:, 0, :], ALU.subtract).then_inc(aux_free[u % 4], 1)
                aux_taken(dve, u)
                link(dve.tensor_tensor_scan(hrow[:, 2, :], ones[0:4, :], hrow[:, 1, :], 0.0, ALU.mult, ALU.max))
                dve.tensor_scalar(hrow[:, 3, :], hrow[:, 2, :], -1.0, None, ALU.mult)
                dve.tensor_tensor(hrow[:, 4, :], hrow[:, 0, :], hrow[:, 2, :], ALU.add).then_inc(sem("ml_rows"), 1)

            def ml_weights():
                u = AUX[("atr", 0)]
                aux_filled(dve, u)
                dve.tensor_copy(acol[:, :], bank(u, 16)).then_inc(aux_free[u % 4], 1)
                aux_taken(dve, u)
                for i in range(2):
                    u = AUX[("bc", i)]
                    aux_filled(dve, u)
                    for j in range(2):
                        h = 2 * i + j
                        x = bank(u)[:, j * S:(j + 1) * S]
                        dve.tensor_scalar(Wd[:, h, 0:S], x, acol[:, h:h + 1], 0.0, ALU.add, ALU.min)
                        ins = dve.tensor_scalar(Wd[:, h, S:S + P], x[:, P:S], acol[:, 4 + h:5 + h], 0.0, ALU.add, ALU.min)
                    ins.then_inc(aux_free[u % 4], 1)
                aux_taken(dve, AUX[("bc", 1)])
                dve.sem_inc(sem("ml_w_in"), 1)

            def diagonal_blocks(x):
                return x[:, :, :].rearrange("p h (b t) -> p h b t", b=3)[:, :, 0:3:2, :]

            def ml_mask():
                dve.wait_ge(sem("ml_w_exp"), 1)
                d = diagonal_blocks(Wd)
                link(dve.tensor_tensor(d, d, causal[:, :].unsqueeze(1).unsqueeze(1).to_broadcast([P, 4, 2, P]), ALU.mult))
                dve.memset(vml[:, :, :, ML_DV:ML_DV + 2], 1.0)

            def ml_scores():
                for h in range(4):
                    u = AUX[("st", h)]
                    aux_filled(dve, u)
                    dve.scalar_tensor_tensor(out=Wd[:, h, :], in0=bank(u, 384), scalar=ML_DQK ** -0.5, in1=Wd[:, h, :],
                                             op0=ALU.mult, op1=ALU.mult).then_inc(aux_free[u % 4], 1)

            def ml_output(h):
                for t in range(T):
                    u = AUX[("mpv", h, t)]
                    aux_filled(dve, u)
                    d = den[:, h * 2 + t, :]
                    dn = bank(u)[:, ML_DV:ML_DV + 1]
                    link(dve.tensor_scalar(d[:, 0:1], dn, -1.0, acol[:, 8 + t * 4 + h:9 + t * 4 + h], ALU.mult, ALU.max))
                    link(dve.tensor_tensor(d[:, 0:1], d[:, 0:1], dn, ALU.max))
                    link(dve.reciprocal(d[:, 1:2], d[:, 0:1]))
                    dve.tensor_scalar(hA[:, t, h * ML_DV:(h + 1) * ML_DV], bank(u, ML_DV), d[:, 1:2], None, ALU.mult)\
                        .then_inc(aux_free[u % 4], 1)
                if h == 3:
                    for hh in range(2, 4):
                        for t in range(T):
                            aux_taken(dve, AUX[("mpv", hh, t)])
                    dve.sem_inc(sem("ml_h"), 1)

            def per_head(name):
                return rstd[:, SLOT[name], :].rearrange("p (t h) -> p t h", t=T)

            def a_evacuate(s):
                n = FIRST["A"] + s
                if s == 0:
                    powered(dve, "x")
                r = lambda t: r_tok("x", t)
                if s in A_TRANSPOSED:
                    scaled(n, gate[s % 2], r).then_inc(acc_free[n % 2], 1)
                elif s in (2, 5):
                    h = (s - 2) // 3
                    scaled(n, ob[:, :, h * 512:(h + 1) * 512], r).then_inc(acc_free[n % 2], 1)
                elif s in (9, 10):
                    scaled(n, vml[:, :, 2 * (s - 9):2 * (s - 8), 0:ML_DV], r).then_inc(acc_free[n % 2], 1)
                else:
                    x, half = (ob, s // 8) if s < 12 else (hA, s % 2)
                    y = x[:, :, half * COLS:(half + 1) * COLS]
                    link(dve.tensor_tensor(y, y, next_gate()[:, :, :], ALU.mult))
                    dve.sem_inc(acc_free[n % 2], 1)
                    if s < 12:
                        dve.sem_inc(sem("yb_ready"), 1)
                    if s >= 14:
                        dve.sem_inc(sem("ya_ready"), 1)

            for s in range(16):
                for p in range(8):
                    split_lo(SLABS[FIRST["A"] + s][0] + p)
                    w = s * 8 + p
                    if s == 0:
                        lo_split(AUX[("xT", p)], actA, 2 * p, gains[:, C_NORM:C_NORM + KD])
                        if p == 4:
                            lower_bounds()
                    if (s, p) == (1, 0):
                        dve.wait_ge(sem("ss_x"), 1)
                        row_variance("x")
                    if (s, p) == (1, 7):
                        dve.wait_ge(sem("gw_hi"), 1)
                        dve.tensor_tensor(gw_hi_lo[:, :, 8:16], gw[:, :, :], gw_hi_lo[:, :, 0:8].bitcast(F32), ALU.subtract)\
                            .then_inc(sem("gw_lo"), 1)
                    if (s, p) == (2, 0):
                        for n in range(2):
                            lo_split(AUX[("p" if n == 0 else "p2", 0)], pT[n], 0)
                        dve.wait_ge(sem("consts_ready"), 1)
                        dve.memset(Kp[0][:, :], 0.0)
                        dve.memset(Kp[1][:, :], 0.0)
                    for half, L0 in enumerate(HG_START):
                        if w == L0 - 7:
                            hg_forget(half)
                        if w == L0 - 5:
                            hg_cumsum(half)
                        if w == L0 - 1:
                            hg_queries(half)
                        if w == L0 + 1:
                            hg_diagonal(half)
                        n, odd = divmod(w - L0, 2)
                        if not odd:
                            if 0 <= n - 1 < 8:
                                hg_mul(half, n - 1)
                            if 0 <= n < 8:
                                hg_sub(half, n)
                        if odd and 0 <= n - 2 < 8:
                            hg_take(half, n - 2)
                        if w == L0 + 22:
                            hg_output(half)
                        if w == L0 + 25:
                            dve.wait_ge(sem("ss_hB"), half + 1)
                            variance(f"hB{half}", HG_E)
                        if w == L0 + 28:
                            powered(dve, f"hB{half}")
                            x = ob[:, :, half * 512:(half + 1) * 512].rearrange("p t (h c) -> p t h c", h=4)
                            link(dve.tensor_tensor(x, x, per_head(f"hB{half}").unsqueeze(3).to_broadcast([P, T, 4, P]), ALU.mult))
                    if p == 3 and s > 0:
                        a_evacuate(s - 1)
                    if (s, p) in ((9, 0), (9, 6)):
                        ml_conv(7 + p // 6)
                    if (s, p) == (10, 0):
                        ml_gates_out()
                    if (s, p) == (10, 3):
                        ml_gates()
                    if (s, p) == (10, 6):
                        ml_logf()
                    if (s, p) == (11, 0):
                        ml_rows()
                    if (s, p) == (11, 3):
                        ml_weights()
                    if (s, p) == (11, 6):
                        ml_mask()
                    if (s, p) == (12, 0):
                        ml_scores()
                    if s == 12 and 3 <= p <= 6:
                        ml_output(p - 3)
                    if (s, p) == (13, 1):
                        dve.wait_ge(sem("ss_hA"), 1)
                        variance("hA", ML_DV)
                    if (s, p) == (13, 2):
                        powered(dve, "hA")
                        x = hA[:, :, :].rearrange("p t (h c) -> p t h c", h=4)
                        link(dve.tensor_tensor(x, x, per_head("hA").unsqueeze(3).to_broadcast([P, T, 4, ML_DV]), ALU.mult))
                    if (s, p) == (15, 0):
                        for i in range(4, 8):
                            lo_split(AUX[("yT", i)], actB, 2 * i, gains[:, C_MIX:C_MIX + KD])
                    if (s, p) == (15, 6):
                        for i in range(2):
                            lo_split(AUX[("yT", i)], actB, 2 * i, gains[:, C_MIX:C_MIX + KD])

            def add_slab(n, s):
                slab_made(dve, n)
                x = resid[:, :, s * COLS:(s + 1) * COLS]
                dve.tensor_tensor(x, x, acc2(n), ALU.add).then_inc(acc_free[n % 2], 1)
                slab_taken(dve, n)
                dve.sem_inc(sem("h_added"), 1)

            for s in range(4):
                for p in range(8):
                    split_lo(SLABS[FIRST["C"] + s][0] + p)
                    if s == 0 and p == 3:
                        a_evacuate(15)
                    if s == 0 and p == 5:
                        for i in range(2, 4):
                            lo_split(AUX[("yT", i)], actB, 2 * i, gains[:, C_MIX:C_MIX + KD])
                    if s > 0 and p == 3:
                        add_slab(FIRST["C"] + s - 1, s - 1)
                    if s > 0 and p == 5:
                        for i in range(2):
                            lo_split(AUX[("hD", 2 * s - 2 + i)], actA, 4 * s - 4 + 2 * i, gains[:, C_PE:C_PE + KD])

            def d_gate(s):
                g = next_gate()
                n = FIRST["D"] + 2 * s + 1
                dve.sem_inc(acc_free[n % 2], 1)
                link(dve.tensor_tensor(g[:, :, :], g[:, :, :], eb[s % 2][:, :, :], ALU.mult))
                x = resid[:, :, s * COLS:(s + 1) * COLS]
                dve.tensor_tensor(x, x, g[:, :, :], ALU.add).then_inc(sem("h_gated"), 1)

            def d_final(s):
                dve.wait_ge(sem("ss_f1"), s + 1)
                aux_filled(dve, AUX[("hE", 2 * s + 1)])
                x = resid[:, :, s * COLS:(s + 1) * COLS]
                dve.tensor_tensor(x, x, fw[:, s * COLS:(s + 1) * COLS].unsqueeze(1).to_broadcast([P, T, COLS]), ALU.mult)\
                    .then_inc(sem("h_final"), 1)

            for s in range(4):
                n = FIRST["D"] + 2 * s
                split_lo(SLABS[n][0])
                for p in range(8):
                    split_lo(SLABS[n + 1][0] + p)
                    if s == 0 and p == 2:
                        add_slab(FIRST["C"] + 3, 3)
                    if s == 0 and p == 5:
                        for i in range(6, 8):
                            lo_split(AUX[("hD", i)], actA, 2 * i, gains[:, C_PE:C_PE + KD])
                    if s == 0 and p == 6:
                        dve.wait_ge(sem("ss_h1"), 1)
                        row_variance("h1")
                        dve.wait_ge(sem("fw_loaded"), 16)
                    if s > 0 and p == 1:
                        d_gate(s - 1)
                    if s > 0 and p == 6:
                        for i in range(2):
                            lo_split(AUX[("hE", 2 * s - 2 + i)], actB, 4 * s - 4 + 2 * i, gain_e)
                        d_final(s - 1)
                    if p == 3:
                        slab_made(dve, n)
                        dve.tensor_copy(eb[s % 2][:, :, :], acc2(n)).then_inc(acc_free[n % 2], 1)
                        slab_taken(dve, n)

            def rE(t):
                return r_e[:, t:t + 1]

            def qk_normalise(s):
                dve.wait_ge(sem("ss_qk"), s + 1)
                variance(f"qk{s}", SB_D)

            def qk_scale(s):
                powered(dve, f"qk{s}")
                x = gate[s % 2][:, :, :].rearrange("p t (h c) -> p t h c", h=4)
                dve.tensor_tensor(x, x, per_head(f"qk{s}").unsqueeze(3).to_broadcast([P, T, 4, P]), ALU.mult)\
                    .then_inc(sem("qk_normed"), 1)

            def qk_transposed(s):
                dst, gain = (qT, qn_scaled) if s < 2 else (kT, gains[:, C_KN:C_KN + 1])
                for i in range(2):
                    u = AUX[("tr2", s, i)]
                    aux_filled(dve, u)
                    c = 4 * (s % 2) + 2 * i
                    dve.tensor_scalar(dst[:, c:c + 2, :], bank(u).rearrange("p (h t) -> p h t", h=2), gain[:, 0:1], None, ALU.mult)\
                        .then_inc(aux_free[u % 4], 1)

            def att_take(b):
                for j in range(4):
                    u = AUX[("z", b, j)]
                    aux_filled(dve, u)
                    dve.tensor_copy(zt[:, j, :], bank(u, 384)).then_inc(aux_free[u % 4], 1)
                for j in range(4):
                    aux_taken(dve, AUX[("z", b, j)])
                dve.sem_inc(sem("att_z"), 1)

            def strict_blocks(x):
                d = diagonal_blocks(x)
                return dve.tensor_tensor(d, d, strict[:, :].unsqueeze(1).unsqueeze(1).to_broadcast([P, 4, 2, P]), ALU.mult)

            def att_logs(b):
                dve.wait_ge(sem("att_ln"), b + 1)
                link(dve.scalar_tensor_tensor(out=Lp[:, :, :], in0=zt[:, :, :], scalar=0.0, in1=ab[:, :, :], op0=ALU.max, op1=ALU.add))
                strict_blocks(Lp).then_inc(sem("att_l"), 1)
                link(dve.scalar_tensor_tensor(out=zt[:, :, :], in0=zt[:, :, :], scalar=0.0, in1=ab[:, :, :], op0=ALU.min,
                                              op1=ALU.subtract))

            def att_arg(b):
                for j in range(4):
                    u = AUX[("tail", b, j)]
                    aux_filled(dve, u)
                    dve.tensor_tensor(zt[:, j, :], zt[:, j, :], bank(u, 384), ALU.subtract).then_inc(aux_free[u % 4], 1)
                for j in range(4):
                    aux_taken(dve, AUX[("tail", b, j)])
                dve.sem_inc(sem("att_arg"), 1)

            def att_mask(b):
                dve.wait_ge(sem("att_w"), b + 1)
                strict_blocks(zt).then_inc(sem("att_masked"), 1)

            def att_output(b):
                aux_filled(dve, AUX[("att", b, 1)])
                for t in range(T):
                    u = AUX[("att", b, t)]
                    dve.tensor_copy(vA[:, t, b * 512:(b + 1) * 512], bank(u)).then_inc(aux_free[u % 4], 1)

            def vs_scale(half):
                powered(dve, f"s{half}")
                x = vs[:, :, half * 512:(half + 1) * 512].rearrange("p t (h c) -> p t h c", h=4)
                dve.tensor_tensor(x, x, per_head(f"s{half}").unsqueeze(3).to_broadcast([P, T, 4, P]), ALU.mult)\
                    .then_inc(sem("vs_ready"), 1)

            def spatial_gate(half):
                dve.wait_ge(sem("gbc_loaded"), 16)
                for i in range(2):
                    u = AUX[("sgu", 2 * half + i)]
                    aux_filled(dve, u)
                    g = 4 * half + 2 * i
                    t4 = ab[:, 0:2, 0:S].rearrange("p g (t c) -> p g t c", t=T)
                    for j in range(2):
                        ins = dve.tensor_tensor(t4[:, j], bank(u)[:, j * S:(j + 1) * S].rearrange("p (t c) -> p t c", t=T),
                                                gbc[:, (g + j) * P:(g + j + 1) * P].unsqueeze(1).to_broadcast([P, T, P]), ALU.mult)
                    ins.then_inc(aux_free[u % 4], 1)
                    aux_taken(dve, u)
                    for j in range(2):
                        x = u2[:, :, (g + j) * P:(g + j + 1) * P]
                        ins = dve.scalar_tensor_tensor(out=x, in0=t4[:, j], scalar=gains[:, C_BS + g + j:C_BS + g + j + 1], in1=x,
                                                       op0=ALU.add, op1=ALU.mult)
                    if i == 0:
                        link(ins)
                ins.then_inc(sem("ya2_ready"), 1)

            for s in range(10):
                n = FIRST["E1"] + s
                for p in range(8):
                    split_lo(SLABS[n][0] + p)
                    w = s * 8 + p
                    if s == 0:
                        if p == 2:
                            d_gate(3)
                        if p == 5:
                            for i in range(6, 8):
                                lo_split(AUX[("hE", i)], actB, 2 * i, gain_e)
                        if p == 6:
                            d_final(3)
                            dve.wait_ge(sem("h_final"), 4)
                            dve.sem_inc(sem("block1_done"), 1)
                        if p == 7:
                            dve.wait_ge(sem("ss_f1"), 4)
                            row_variance("f1")
                    if (s, p) == (1, 0):
                        dve.wait_ge(sem("ss_f2"), 4)
                        powered(dve, "f1")
                        i, j = SLOT["f1"], SLOT["f2"]
                        link(dve.tensor_reduce(var[:, j, 4:6], ss[:, j, :].rearrange("p (t c) -> p t c", t=T), AX.X, ALU.add))
                        for _ in range(2):
                            link(dve.tensor_tensor(var[:, j, 4:6], var[:, j, 4:6], rstd[:, i, 0:T], ALU.mult))
                        variance("f2", D, var[:, j, 4:6])
                    if (s, p) == (1, 1):
                        powered(dve, "f2")
                        dve.tensor_tensor(r_e[:, :], rstd[:, SLOT["f1"], 0:T], rstd[:, SLOT["f2"], 0:T], ALU.mult)\
                            .then_inc(sem("r_e_ready"), 1)
                        dve.wait_ge(sem("r_e_ready"), 1)
                    if 1 <= s <= 4:
                        if p == 3:
                            scaled(n - 1, gate[(s - 1) % 2], rE).then_inc(acc_free[(n - 1) % 2], 1)
                            slab_taken(dve, n - 1)
                            dve.sem_inc(sem("qk_tok"), 1)
                        if p == 5:
                            qk_normalise(s - 1)
                        if p == 6:
                            qk_scale(s - 1)
                    if 2 <= s <= 5 and p == 2:
                        qk_transposed(s - 2)
                    if (s, p) == (2, 4):
                        for i in range(2):
                            u = AUX[("ws", i)]
                            aux_filled(dve, u)
                            dve.tensor_copy(wsT[:, 4 * i:4 * i + 4, :], bank(u).rearrange("p (g t) -> p g t", g=4))\
                                .then_inc(aux_free[u % 4], 1)
                    if s == 2 and p in (5, 6):
                        t = p - 5
                        link(dve.tensor_scalar(resid[:, t, :], resid[:, t, :], r_tok("f1", t), None, ALU.mult))
                    if s in (5, 6) and p == 3:
                        scaled(n - 1, vA[:, :, (s - 5) * 512:(s - 4) * 512], rE).then_inc(acc_free[(n - 1) % 2], 1)
                    for b, z0 in enumerate(ATT_START):
                        if w == z0 + 5:
                            att_take(b)
                        if w == z0 + 9:
                            att_logs(b)
                        if w == z0 + 12:
                            att_arg(b)
                        if w == z0 + 15:
                            att_mask(b)
                        if w == z0 + 18:
                            att_output(b)
                    if s in (7, 8) and p == 5:
                        dve.wait_ge(sem("ss_s"), s - 6)
                        variance(f"s{s - 7}", P)
                    if s in (7, 8) and p == 7:
                        vs_scale(s - 7)
                    if (s, p) == (9, 4):
                        slab_taken(dve, n - 1)
                        spatial_gate(0)
                    if (s, p) == (9, 7):
                        for i in range(2):
                            lo_split(AUX[("yaT", i)], actA, 2 * i)

            pair_gate = [None]
            for ph in ("E2", "E3"):
                for s in range(8):
                    n = FIRST[ph] + s
                    for p in range(SLABS[n][1]):
                        split_lo(SLABS[n][0] + p)
                        if ph == "E2" and s == 0:
                            if p == 4:
                                slab_taken(dve, n - 1)
                                spatial_gate(1)
                            if p == 6:
                                for i in range(2, 4):
                                    lo_split(AUX[("yaT", i)], actA, 2 * i)
                            if p == 7:
                                for i in range(4):
                                    lo_split(AUX[("ybT", i)], actA, 8 + 2 * i)
                        if p == 3 and s % 2 == 1:
                            pair_gate[0] = next_gate()
                            dve.sem_inc(acc_free[(n - 1) % 2], 1)
                        if p == 3 and s % 2 == 0 and (s > 0 or ph == "E3"):
                            merge_phase2 = ph == "E3" and s > 0
                            col = (s // 2 - 1) % 4
                            x = merged[:, :, col * COLS:(col + 1) * COLS]
                            slab_made(dve, n - 1)
                            if not merge_phase2:
                                dve.tensor_tensor(x, pair_gate[0][:, :, :], acc2(n - 1), ALU.mult).then_inc(acc_free[(n - 1) % 2], 1)
                                slab_taken(dve, n - 1)
                            else:
                                gt = pair_gate[0][:, :, :]
                                dve.tensor_tensor(gt, gt, acc2(n - 1), ALU.mult).then_inc(acc_free[(n - 1) % 2], 1)
                                slab_taken(dve, n - 1)
                                dve.tensor_tensor(x, x, gt, ALU.add).then_inc(sem("merged_ready"), 1)
                        if ph == "E3" and s >= 2 and s % 2 == 0 and p == 6:
                            for i in range(2):
                                lo_split(AUX[("mT", s - 2 + i)], actF, 2 * (s - 2 + i))

            for s in range(4):
                n = FIRST["G"] + s
                for p in range(8):
                    split_lo(SLABS[n][0] + p)
                    if s == 0 and p == 3:
                        gt = pair_gate[0][:, :, :]
                        x = merged[:, :, 3 * COLS:4 * COLS]
                        slab_made(dve, n - 1)
                        dve.tensor_tensor(gt, gt, acc2(n - 1), ALU.mult).then_inc(acc_free[(n - 1) % 2], 1)
                        slab_taken(dve, n - 1)
                        dve.tensor_tensor(x, x, gt, ALU.add).then_inc(sem("merged_ready"), 1)
                    if s == 0 and p == 5:
                        for i in range(6, 8):
                            lo_split(AUX[("mT", i)], actF, 2 * i)
                    if s > 0 and p == 3:
                        add_slab(n - 1, s - 1)
                    if s > 0 and p == 5:
                        for i in range(2):
                            lo_split(AUX[("hH", 2 * s - 2 + i)], actA, 4 * s - 4 + 2 * i, gains[:, C_FFN:C_FFN + KD])

            def take_gate(n):
                pair_gate[0] = next_gate()
                dve.sem_inc(acc_free[n % 2], 1)

            def hidden(n, j):
                slab_made(dve, n)
                for t in range(T):
                    ins = dve.scalar_tensor_tensor(out=hid[:, t, :], in0=acc2(n)[:, t, :], scalar=r_tok("ffn", t),
                                                   in1=pair_gate[0][:, t, :], op0=ALU.mult, op1=ALU.mult)
                ins.then_inc(acc_free[n % 2], 1)
                slab_taken(dve, n)
                dve.sem_inc(sem("hid_ready"), 1)

            for part, (f0, width) in enumerate(FFN_PARTS):
                nh = width // COLS
                for s in range(2 * nh):
                    n = FIRST[f"H{part}"] + s
                    for p in range(8):
                        split_lo(SLABS[n][0] + p)
                        if s == 0 and p == 3:
                            add_slab(n - 1, 3)
                        if s == 0 and part == 0:
                            if p == 5:
                                for i in range(6, 8):
                                    lo_split(AUX[("hH", i)], actA, 2 * i, gains[:, C_FFN:C_FFN + KD])
                            if p == 6:
                                dve.wait_ge(sem("ss_ffn"), 1)
                                row_variance("ffn")
                        if s % 2 == 1 and p == 3:
                            take_gate(n - 1)
                        if s > 0 and s % 2 == 0 and p == 3:
                            hidden(n - 1, s // 2 - 1)
                        if s > 0 and s % 2 == 0 and p == 6:
                            for c in range(4):
                                lo_split(AUX[("hid", part, 2 * s - 4 + c)], actF, 2 * s - 4 + c, n=1)
                for s in range(4):
                    n = FIRST[f"O{part}"] + s
                    for p in range(SLABS[n][1]):
                        split_lo(SLABS[n][0] + p)
                        if s == 0 and p == 3:
                            hidden(n - 1, nh - 1)
                        if s == 0 and p == 4:
                            for c in range(4):
                                lo_split(AUX[("hid", part, 4 * nh - 4 + c)], actF, 4 * nh - 4 + c, n=1)
                        if s > 0 and p == 3:
                            add_slab(n - 1, s - 1)
                        if part == 2 and s > 0 and p == 5:
                            for i in range(2):
                                lo_split(AUX[("hJ", 2 * s - 2 + i)], actB, 4 * s - 4 + 2 * i, gains[:, C_PLE:C_PLE + KD])

            def j_gate(s):
                g = next_gate()
                n = FIRST["J"] + 2 * s + 1
                dve.sem_inc(acc_free[n % 2], 1)
                link(dve.tensor_tensor(g[:, :, :], g[:, :, :], merged[:, :, (s % 2) * COLS:(s % 2 + 1) * COLS], ALU.mult))
                x = resid[:, :, s * COLS:(s + 1) * COLS]
                dve.tensor_tensor(x, x, g[:, :, :], ALU.add).then_inc(sem("out_ready"), 1)

            for s in range(4):
                n = FIRST["J"] + 2 * s
                split_lo(SLABS[n][0])
                for p in range(8):
                    split_lo(SLABS[n + 1][0] + p)
                    if s == 0 and p == 2:
                        add_slab(n - 1, 3)
                    if s == 0 and p == 5:
                        for i in range(6, 8):
                            lo_split(AUX[("hJ", i)], actB, 2 * i, gains[:, C_PLE:C_PLE + KD])
                    if s == 0 and p == 6:
                        dve.wait_ge(sem("ss_ple"), 1)
                        row_variance("ple")
                    if s > 0 and p == 1:
                        j_gate(s - 1)
                    if p == 3:
                        slab_made(dve, n)
                        dve.tensor_copy(merged[:, :, (s % 2) * COLS:(s % 2 + 1) * COLS], acc2(n)).then_inc(acc_free[n % 2], 1)
                        slab_taken(dve, n)
            j_gate(3)


_INS = ["x", "p", "norm_w", "w_in", "conv_w", "conv_b", "ml_b_i", "ml_b_f", "ml_norm_w", "hg_lb", "hg_norm_w", "w_out",
        "pe_norm_w", "w_pg", "w_pe", "final_norm_w", "p_2", "attn_norm_g_2", "w_in_2", "sgu_norm_g_2", "w_s_2", "b_s_2",
        "q_norm_g_2", "k_norm_g_2", "w_up_a_2", "w_up_b_2", "w_o_2", "ffn_norm_g_2", "w_ffn_in_2", "w_ffn_out_2",
        "ple_norm_g_2", "w_ple_gate_2", "w_ple_2"]


def kernel(**inputs):
    import numpy as _np
    import concourse.bacc as _bacc
    from concourse.bass_utils import run_bass_kernel_spmd as _run

    nc = _bacc.Bacc("TRN2", target_bir_lowering=False, num_devices=1)
    arrays, aps = {}, {}
    for name in _INS:
        a = _np.ascontiguousarray(inputs[name])
        arrays[f"in_{name}"] = a
        aps[name] = nc.dram_tensor(f"in_{name}", a.shape, mybir.dt.from_np(a.dtype), kind="ExternalInput").ap()
    out = nc.dram_tensor("out_0", (1, S, D), F32, kind="ExternalOutput").ap()
    two_blocks_kernel(nc, aps, out)
    r = _run(nc, [arrays], core_ids=[0])
    return r.results[0]["out_0"]
```

```python
from contextlib import ExitStack

import concourse.bass as bass
from concourse import mybir

F32 = mybir.dt.float32
F32R = mybir.dt.float32r
I32 = mybir.dt.int32
ACT = mybir.ActivationFunctionType
ALU = mybir.AluOpType
AX = mybir.AxisListType

P = 128
D = 2048
KD = D // P
S = 256
T = S // P
COLS = 512
PK = 2
RAW = 8
RING = 4
EPS = 1e-6

ML_HEADS, ML_DQK, ML_DV, ML_TAPS = 4, 128, 256, 4
ML_W = ML_HEADS * ML_DV
HG_E = 128
SB_D = 128
PE_DIM = 256
FFN = 5632

MQ, MK, MV, MO, MZ, MI = 0, 512, 1024, 2048, 3072, 4096
HQ, HF, HI, HG = 4104, 5128, 6152, 7176
U2, S2, Q2, K2, V2, GA2, GB2 = 0, 1024, 2048, 3072, 4096, 5120, 7168

A_COLS = [HF, HQ, HI, HF + 512, HQ + 512, HI + 512, HG, MQ, MK, MV, MV + 512, HG + 512, MZ, MZ + 512, MO, MO + 512]
E1_COLS = [Q2, Q2 + 512, K2, K2 + 512, V2, V2 + 512, S2, S2 + 512, U2, U2 + 512]
HIDDEN = FFN // COLS
ROUND = 24

C_NORM, C_PE, C_ATTN, C_FFN, C_PLE, C_LB, C_CONVW = 0, 16, 32, 48, 64, 80, 96
C_CONVB, C_QN, C_KN, C_BS, C_MIX, C_FW, C_END = 128, 136, 137, 138, 146, 162, 178

LEVELS = [128 >> n for n in range(8)]
A_TRANSPOSED = (0, 1, 3, 4, 7, 8)
A_GATED = (6, 11, 12, 13, 14, 15)
HG_START = (23, 49)
ATT_START = (35, 55)


def plan():
    phases = [("A", [8] * 16), ("C", [8] * 4), ("DP", [1] * 4), ("D", [8] * 4), ("E1", [8] * 10),
              ("E2", [8, 4, 8, 4] * 4), ("G", [8] * 4),
              ("F0", [8, 8]), ("F", [8, 2, 2, 2, 2, 8] * (HIDDEN - 1)), ("JP", [1] * 4), ("FT", [2] * 4), ("J", [8] * 4)]
    slabs, first, g = [], {}, 0
    for name, counts in phases:
        first[name] = len(slabs)
        for n in counts:
            slabs.append((g, n))
            g += n
    return slabs, first


def plan_aux():
    names = [("gain0", 0)] + [("xT", i) for i in range(8)] + [("gains", 0)]

    def two(name, *key):
        names.extend((name, *key, i) for i in range(2))

    two("tr", 0)
    names.extend([("p", 0), ("p2", 0)])
    two("tr", 1); two("diag", 0)
    names.extend(("level", 0, n) for n in range(6))
    two("tr", 3)
    names.extend(("level", 0, n) for n in range(6, 8))
    two("pv", 0); two("tr", 4); two("diag", 1)
    names.extend(("level", 1, n) for n in range(8))
    two("tr", 7); two("pv", 1); two("tr", 8)
    names.extend([("gates", 0), ("gatesT", 0), ("gtr", 0), ("atr", 0), ("bc", 0), ("bc", 1)])
    names.extend(("st", h) for h in range(4))
    names.extend(("mpv", h, t) for h in range(4) for t in range(2))
    names.extend(("yT", i) for i in (4, 5, 6, 7, 0, 1, 2, 3))
    names.extend(("hD", i) for i in range(8))
    names.extend(("hE", i) for i in range(8))
    two("tr2", 0); two("ws"); two("tr2", 1); two("tr2", 2)
    for b in range(2):
        names.extend(("z", b, h) for h in range(4))
        if b == 0:
            two("tr2", 3)
        names.extend(("tail", b, h) for h in range(4))
        two("att", b)
    names.extend([("sgu", 0), ("sgu", 1), ("yaT", 0), ("yaT", 1), ("sgu", 2), ("sgu", 3), ("yaT", 2), ("yaT", 3)])
    names.extend(("ybT", i) for i in range(4))
    names.extend(("mT", s, c) for s in range(4) for c in range(4))
    names.extend(("hH", i) for i in range(8))
    names.extend(("hid", j, c) for j in range(HIDDEN) for c in range(4))
    names.extend(("hJ", i) for i in range(8))
    assert len(set(names)) == len(names)
    return {n: i for i, n in enumerate(names)}


def two_blocks_kernel(nc, A, out):
    SLABS, FIRST = plan()
    AUX = plan_aux()
    ctx = ExitStack()
    with ctx:
        def sb(name, shape, dt=F32, at=None):
            return (at or ctx).enter_context(nc.sbuf_tensor(name, shape, dt))

        sems = {}

        def sem(name):
            if name not in sems:
                sems[name] = ctx.enter_context(nc.semaphore(name))
            return sems[name]

        raw = sb("raw", [P, RAW, PK, COLS])
        whi = sb("whi", [P, RING, PK, COLS], F32R)
        wlo = sb("wlo", [P, RING, PK, COLS], F32R)
        resid = sb("resid", [P, T, D])
        ra = ExitStack()
        actA = [sb(f"actA_{x}", [P, KD, S], F32R, at=ra) for x in ("hi", "lo")]
        ra.close()
        qT = sb("qT", [P, 8, S])
        kT = sb("kT", [P, 8, S])
        zt = sb("att_z", [P, 4, 384])
        Lp = sb("att_l", [P, 4, 384])
        wsT = sb("wsT", [P, 8, P])
        rs = ExitStack()
        stage1 = sb("stage1", [P, P], at=rs)
        stage2 = sb("stage2", [C_END - P, P], at=rs)
        ptok = [sb(f"ptok{n}", [P, T, PE_DIM], at=rs) for n in range(2)]
        rs.close()
        rh = ExitStack()
        bF = sb("hg_b", [P, 1024], at=rh)
        qF = sb("hg_q", [P, 1024], at=rh)
        kF = sb("hg_k", [P, 1024], at=rh)
        Eb = [sb(f"hg_e{i}", [P, 1024], at=rh) for i in range(2)]
        Qp = [sb(f"hg_qd{i}", [P, 512], at=rh) for i in range(2)]
        Am = sb("hg_a", [P, 8, P], at=rh)
        A01 = sb("hg_a01", [P, 4, P], at=rh)
        rh.close()
        rm = ExitStack()
        qk = sb("ml_qk", [P, 8, S], at=rm)
        hrow = sb("hrow", [4, 6, S], at=rm)
        Wd = sb("ml_w", [P, 4, 384], at=rm)
        vml = sb("ml_v", [P, T, 4, ML_DV + 2], at=rm)
        rm.close()
        actB = [sb(f"actB_{x}", [P, KD, S], F32R) for x in ("hi", "lo")]
        gate = [sb(f"gate{i}", [P, T, COLS]) for i in range(2)]
        pT = [[sb(f"p{n}T_{x}", [P, PK, S], F32R) for x in ("hi", "lo")] for n in range(2)]
        gains = sb("gains", [P, C_END])
        gain_e = sb("gain_e", [P, KD])
        lb = sb("lb", [P, 4, 8])
        qn_scaled = sb("qn_scaled", [P, 1])
        ident = sb("ident", [P, P])
        ones = sb("ones", [P, S])
        causal = sb("causal", [P, P])
        strict = sb("strict", [P, P])
        later = sb("later", [P, P])
        lmask = sb("lmask", [P, 7, 64])
        minus_half = sb("minus_half", [P, 16])
        junk = sb("junk", [P, COLS])
        ss = sb("ss", [P, 16, 8])
        var = sb("var", [P, 16, 8])
        rstd = sb("rstd", [P, 16, 8])
        r_e = sb("r_e", [P, T])
        r1 = ExitStack()
        ob = sb("hg_v", [P, T, 1024], at=r1)
        gw = sb("gw", [P, KD, 8], at=r1)
        gw_hi_lo = sb("gw_hi_lo", [P, KD, 16], F32R, at=r1)
        gates_ch = sb("gates_ch", [16, S], at=r1)
        gbias = sb("gbias", [P, 8], at=r1)
        sel = sb("sel", [4, 4, P], at=r1)
        gtok = sb("gtok", [P, T, 8], at=r1)
        gtmp = sb("gtmp", [P, T, 4], at=r1)
        acol = sb("acol", [P, 16], at=r1)
        den = sb("den", [P, 8, 2], at=r1)
        rh = ExitStack()
        Kp = [sb(f"hg_kd{i}", [P, 1024], at=rh) for i in range(2)]
        rh.close()
        hA = sb("ml_h", [P, T, ML_W], at=r1)
        r1.close()
        rd = ExitStack()
        ple = sb("ple", [P, T, D], at=rd)
        fw = sb("final_gain", [P, D], at=rd)
        rd.close()
        r2 = ExitStack()
        vA = sb("att_v", [P, T, 1024], at=r2)
        ab = sb("att_ab", [P, 4, 384], at=r2)
        gbc = sb("sgu_gain", [P, 1024], at=r2)
        u2 = sb("sgu_u", [P, T, 1024], at=r2)
        vs = sb("sgu_v", [P, T, 1024], at=r2)
        r2.close()
        rf = ExitStack()
        ple2 = sb("ple2", [P, T, D], at=rf)
        hidT = [sb(f"hidT_{x}", [P, 4, S], F32R, at=rf) for x in ("hi", "lo")]
        hid = sb("hid", [P, T, COLS], at=rf)
        rf.close()
        actM = [sb(f"actM_{x}", [P, KD, S], F32R) for x in ("hi", "lo")]
        merged = sb("merged", [P, T, COLS])
        wsr = zt[:, :, :].rearrange("p a b -> p (a b)")[:, 0:1024].rearrange("p (g s) -> p g s", g=8)

        acc = ctx.enter_context(nc.psum_tensor("acc", [P, 4, COLS], F32))
        aux = ctx.enter_context(nc.psum_tensor("aux", [P, 4, COLS], F32))

        first_loaded = [sem(f"first_loaded{i}") for i in range(RAW)]
        raw_loaded = [sem(f"raw_loaded{i}") for i in range(RAW // 2)]
        hi_ready, lo_ready, piece_used = sem("hi_ready"), sem("lo_ready"), sem("piece_used")
        acc_free = [sem(f"acc_free{i}") for i in range(2)]
        aux_full = sem("aux_full")
        aux_free = [sem(f"aux_free{i}") for i in range(4)]
        split_hi_done = sem("split_hi_done")
        gate_ready = sem("gate_ready")
        pow_in, pow_out = sem("pow_in"), sem("pow_out")

        def view(w):
            return w.rearrange("(k p) n -> p k n", p=P)

        def aux_filled(eng, u, i=0):
            eng.wait_ge(aux_full, u + 1 + i * 4)

        def aux_taken(eng, u, i=0):
            eng.wait_ge(aux_free[u % 4], u // 4 + 1 + i)

        def slab_made(eng, n, i=0):
            eng.wait_ge(piece_used, sum(SLABS[n]) + i * ROUND)

        def slab_taken(eng, n, i=0):
            eng.wait_ge(acc_free[n % 2], n // 2 + 1 + i)

        SHORT = {SLABS[FIRST[name] + q][0] for name in ("DP", "JP") for q in range(4)}

        def raw_piece(g):
            if g not in SHORT:
                return raw[:, g % RAW]
            pair = raw[:, g % RAW // 2 * 2:g % RAW // 2 * 2 + 2].rearrange("p q k c -> p (q k c)")
            return pair.rearrange("p (k q c) -> p q k c", k=PK, q=2)[:, g % 2]

        def pieces(n, count):
            return [(SLABS[s][0] + p, s, p) for s in range(n, n + count) for p in range(SLABS[s][1])]

        def bank(u, n=COLS):
            return aux[:, u % 4, 0:n]

        def acc2(n):
            return acc[:, 2 * (n % 2):2 * (n % 2) + 2, :]

        POWS = [("x", T), ("hB0", 8), ("hB1", 8), ("hA", 8), ("h1", T), ("f1", T), ("f2", T), ("qk0", 8), ("qk1", 8),
                ("qk2", 8), ("qk3", 8), ("s0", 8), ("s1", 8), ("ffn", T), ("ple", T)]
        SLOT = {n: i for i, (n, _) in enumerate(POWS)}

        def r_tok(name, t):
            return rstd[:, SLOT[name], t:t + 1]

        def powered(eng, name):
            eng.wait_ge(pow_out, SLOT[name] + 1)

        block = ctx.enter_context(nc.Block())

        @block.sync
        def _(sp):
            piece = [0]

            def load(src, i=0):
                g = piece[0]
                piece[0] += 2
                sp.wait_ge(lo_ready, g - RAW + 2 + i * ROUND)
                dst = raw[:, g % RAW:g % RAW + 2].rearrange("p q k c -> p (q k c)")
                sp.dma_start(dst.rearrange("p (k c) -> p k c", k=src.shape[1]), src).then_inc(raw_loaded[g // 2 % (RAW // 2)], 16)

            def load_slab(w, c, n=8, k0=0, i=0):
                for p in range(0, n, 2):
                    load(view(w)[:, bass.ds(k0 + p * PK, 2 * PK), bass.ds(c, COLS)], i)

            def load_short(w, c):
                load(view(w)[:, :, c:c + 2 * COLS])

            def load_first(n):
                for g in range(piece[0], piece[0] + n):
                    sp.dma_start(raw[:, g], view(A["w_in"][0])[:, g * PK:(g + 1) * PK, A_COLS[0]:A_COLS[0] + COLS])\
                        .then_inc(first_loaded[g], 16)
                piece[0] += n

            def load_x(c):
                sp.dma_start(resid[:, :, c * COLS:(c + 1) * COLS],
                             A["x"][0].rearrange("(t p) c -> p t c", p=P)[:, :, c * COLS:(c + 1) * COLS])\
                    .then_inc(sem(f"x_loaded{c}"), 16)

            sp.dma_start(stage1[C_NORM:C_NORM + KD, :], A["norm_w"].rearrange("a (r c) -> (a r) c", c=P))\
                .then_inc(sem("norm_loaded"), 16)
            load_x(0)
            load_first(2)
            load_x(1)
            load_first(2)
            load_x(2)
            load_x(3)
            load_first(4)

            rows = [(stage1, C_PE, A["pe_norm_w"]), (stage1, C_ATTN, A["attn_norm_g_2"]),
                    (stage1, C_FFN, A["ffn_norm_g_2"]), (stage1, C_PLE, A["ple_norm_g_2"]), (stage1, C_LB, A["hg_lb"]),
                    (stage1, C_CONVW, A["conv_w"][0]), (stage2, C_CONVB, A["conv_b"]), (stage2, C_QN, A["q_norm_g_2"]),
                    (stage2, C_KN, A["k_norm_g_2"]), (stage2, C_BS, A["b_s_2"][0]), (stage2, C_MIX, A["ml_norm_w"]),
                    (stage2, C_MIX + 8, A["hg_norm_w"])]
            for dst, c, src in rows:
                c -= 0 if dst is stage1 else P
                flat = src.rearrange("a (r c) -> (a r) c", c=P)
                sp.dma_start(dst[c:c + flat.shape[0], :], flat).then_inc(sem("small_loaded"), 16)
            sp.dma_start(stage2[C_FW - P:C_END - P, :], A["final_norm_w"].rearrange("(r c) -> r c", c=P))\
                .then_inc(sem("small_loaded"), 16)
            for n, name in enumerate(("p", "p_2")):
                sp.dma_start(ptok[n][:, :, :], A[name][0, 0].rearrange("(t p) c -> p t c", p=P)).then_inc(sem("p_loaded"), 16)
            sp.dma_start(gw[:, :, :], view(A["w_in"][0])[:, :, MI:MI + 8]).then_inc(sem("gw_loaded"), 16)
            sp.dma_start(gbias[:, 0:4], A["ml_b_i"][0].partition_broadcast(P)).then_inc(sem("gbias_loaded"), 16)
            sp.dma_start(gbias[:, 4:8], A["ml_b_f"][0].partition_broadcast(P)).then_inc(sem("gbias_loaded"), 16)
            load_slab(A["w_in"][0], A_COLS[1])
            for c in A_COLS[2:]:
                load_slab(A["w_in"][0], c)
            for s in range(4):
                load_slab(A["w_out"][0], s * COLS, 4, KD // 2)
                load_slab(A["w_out"][0], s * COLS, 4)
            sp.wait_ge(sem("h_added"), 1)
            sp.dma_start(fw[:, :], A["final_norm_w"].partition_broadcast(P)).then_inc(sem("fw_loaded"), 16)
            for s in range(0, 4, 2):
                load_short(A["w_pe"][0], s * COLS)
            for s in range(4):
                load_slab(A["w_pg"][0], s * COLS)
            for n, c in enumerate(E1_COLS):
                load_slab(A["w_in_2"][0], c)
                if n == 1:
                    sp.wait_ge(sem("block1_done"), 1)
                    sp.dma_start(wsr, A["w_s_2"][0].rearrange("g t s -> t g s")).then_inc(sem("ws_loaded"), 16)
                    sp.dma_start(gbc[:, :], A["sgu_norm_g_2"][0].rearrange("g c -> (g c)").partition_broadcast(P))\
                        .then_inc(sem("gbc_loaded"), 16)

            def load_merge(c, i):
                for c0, w_up in ((GA2, "w_up_a_2"), (GB2, "w_up_b_2")):
                    load_slab(A["w_in_2"][0], c0 + c, 8, 0, i)
                    load_slab(A[w_up][0], c, 4, 0, i)

            load_merge(0, 0)
            with sp.Fori(0, D // COLS - 1) as i:
                load_merge(COLS + i * COLS, i)
            piece[0] += 2 * ROUND
            for s in range(4):
                load_slab(A["w_o_2"][0], s * COLS)
            load_slab(A["w_ffn_in_2"][0], 0)
            load_slab(A["w_ffn_in_2"][0], FFN)
            with sp.Fori(0, HIDDEN - 1) as i:
                load_slab(A["w_ffn_in_2"][0], COLS + i * COLS, 8, 0, i)
                for s in range(4):
                    load_slab(A["w_ffn_out_2"][0], s * COLS, 2, 4 * i, i)
                load_slab(A["w_ffn_in_2"][0], FFN + COLS + i * COLS, 8, 0, i)
            piece[0] += (HIDDEN - 2) * ROUND
            for s in range(0, 4, 2):
                load_short(A["w_ple_2"][0], s * COLS)
            for s in range(4):
                load_slab(A["w_ffn_out_2"][0], s * COLS, 2, 4 * (HIDDEN - 1))
            for s in range(4):
                load_slab(A["w_ple_gate_2"][0], s * COLS)
            for s in range(4):
                for t in range(T):
                    sp.wait_ge(sem("out_ready"), s + 1 + (t if s == 3 else 0))
                    sp.dma_start(out[0, t * P:(t + 1) * P, s * COLS:(s + 1) * COLS],
                                 resid[:, t, s * COLS:(s + 1) * COLS]).then_inc(sem("stored"), 16)
            sp.wait_ge(sem("stored"), 16 * 4 * T)

        @block.gpsimd
        def _(pool):
            made = [0]

            def link(ins):
                made[0] += 1
                ins.then_inc(sem("pool_step"), 1)

            def settle():
                pool.wait_ge(sem("pool_step"), made[0])

            link(pool.memset(ident[:, :], 0.0))
            settle()
            link(pool.affine_select(out=ident[:, :], in_=ident[:, :], compare_op=ALU.not_equal, fill=1.0, base=0,
                                    pattern=[[-1, P]], channel_multiplier=1))
            settle()
            pool.sem_inc(sem("ident_ready"), 1)
            link(pool.memset(ones[:, :], 1.0))
            link(pool.memset(lmask[:, :, :], 1.0))
            link(pool.memset(sel[:, :, :], 0.0))
            settle()
            link(pool.affine_select(out=causal[:, :], in_=ones[:, 0:P], compare_op=ALU.is_ge, fill=0.0, base=0,
                                    pattern=[[1, P]], channel_multiplier=-1))
            link(pool.affine_select(out=strict[:, :], in_=ones[:, 0:P], compare_op=ALU.is_gt, fill=0.0, base=0,
                                    pattern=[[1, P]], channel_multiplier=-1))
            link(pool.affine_select(out=later[:, :], in_=ones[:, 0:P], compare_op=ALU.is_gt, fill=0.0, base=0,
                                    pattern=[[-1, P]], channel_multiplier=1))
            link(pool.affine_select(out=sel[:, :, :], in_=sel[:, :, :], compare_op=ALU.not_equal, fill=1.0, base=0,
                                    pattern=[[-1, 4], [0, P]], channel_multiplier=1))
            for n, s in enumerate(LEVELS[1:]):
                m = lmask[:, n, :].rearrange("p (n s) -> p n s", s=s)
                link(pool.affine_select(out=m, in_=m, compare_op=ALU.is_ge, fill=0.0, base=0,
                                        pattern=[[-2 * s, 64 // s], [0, s]], channel_multiplier=1))
            settle()
            for n, s in enumerate(LEVELS[1:]):
                m = lmask[:, n, :].rearrange("p (n s) -> p n s", s=s)
                link(pool.affine_select(out=m, in_=m, compare_op=ALU.is_ge, fill=0.0, base=s - 1,
                                        pattern=[[2 * s, 64 // s], [0, s]], channel_multiplier=-1))
            link(pool.memset(minus_half[:, :], -0.5))
            settle()
            pool.sem_inc(sem("consts_ready"), 1)
            for i, (name, n) in enumerate(POWS):
                if name == "qk0":
                    pool.wait_ge(sem("ws_loaded"), 16)
                    pool.affine_select(out=wsr, in_=wsr, compare_op=ALU.is_ge, fill=0.0, base=0,
                                       pattern=[[0, 8], [-1, P]], channel_multiplier=1).then_inc(sem("ws_masked"), 1)
                pool.wait_ge(pow_in, i + 1)
                pool.tensor_tensor(rstd[:, i, 0:n], var[:, i, 0:n], minus_half[:, 0:n], ALU.pow).then_inc(pow_out, 1)

        @block.scalar
        def _(act):
            steps = [0]
            gates = [0]

            def link(ins):
                steps[0] += 1
                ins.then_inc(sem("act_step"), 1)
                act.wait_ge(sem("act_step"), steps[0])

            def split_hi(g, i=0):
                if g < RAW:
                    act.wait_ge(first_loaded[g], 16)
                else:
                    act.wait_ge(raw_loaded[g // 2 % (RAW // 2)], 16 * (g // RAW) + i * (16 * ROUND // RAW))
                if g >= RING:
                    act.wait_ge(piece_used, g - RING + 1 + i * ROUND)
                act.activation(whi[:, g % RING], raw_piece(g), ACT.Copy).then_inc(hi_ready, 1)

            def act_split(u, dst, c0, gain=None, n=2):
                aux_filled(act, u)
                for c in range(n):
                    ins = act.activation(dst[0][:, c0 + c, :], bank(u)[:, c * S:(c + 1) * S], ACT.Copy,
                                         scale=1.0 if gain is None else gain[:, c0 + c:c0 + c + 1])
                ins.then_inc(split_hi_done, 1)

            def four_hi(dst):
                act.activation(dst, aux[:, :, 0:S], ACT.Copy).then_inc(split_hi_done, 1)

            def squares(src, dst):
                link(act.activation(junk[:, 0:src.shape[-1]], src, ACT.Square, accum_out=dst))

            def gated(n, func, r, buf=None, i=0):
                slab_made(act, n, i)
                powered(act, r) if r in SLOT else act.wait_ge(sem("r_e_ready"), 1)
                buf = gate[gates[0] % 2] if buf is None else buf
                gates[0] += 1
                for t in range(T):
                    scale = r_tok(r, t) if r in SLOT else r_e[:, t:t + 1]
                    ins = act.activation(buf[:, t, :], acc2(n)[:, t, :], func, scale=scale)
                ins.then_inc(gate_ready, 1)

            def gelu(n, dst):
                slab_made(act, n)
                act.wait_ge(sem("r_e_ready"), 1)
                for t in range(T):
                    ins = act.activation(dst[:, t, :], acc2(n)[:, t, :], ACT.Gelu_apprx_tanh, scale=r_e[:, t:t + 1])
                ins.then_inc(acc_free[n % 2], 1)

            def resid_squares(s, name, signal, count):
                act.wait_ge(sem(signal), count)
                for t in range(T):
                    squares(resid[:, t, s * COLS:(s + 1) * COLS], ss[:, SLOT[name], t * 4 + s:t * 4 + s + 1])
                act.sem_inc(sem("ss_" + name), 1)

            act.wait_ge(sem("ident_ready"), 1)
            link(act.activation(junk[:, 0:P], ident[:, :], ACT.Square))

            for s in range(16):
                for p in range(8):
                    w = s * 8 + p
                    if w == 0:
                        aux_taken(act, AUX[("gain0", 0)])
                    if w < 2:
                        act_split(AUX[("xT", p)], actA, 2 * p, gains[:, C_NORM:C_NORM + KD])
                    split_hi(SLABS[FIRST["A"] + s][0] + p)
                    if 2 <= w < 8:
                        act_split(AUX[("xT", p)], actA, 2 * p, gains[:, C_NORM:C_NORM + KD])
                    if s == 0:
                        if p >= 4:
                            c = p - 4
                            for t in range(T):
                                squares(resid[:, t, c * COLS:(c + 1) * COLS], ss[:, SLOT["x"], t * 4 + c:t * 4 + c + 1])
                        if p == 7:
                            act.sem_inc(sem("ss_x"), 1)
                    if (s, p) == (1, 5):
                        act.wait_ge(sem("lb_in"), 1)
                        act.activation(lb[:, 2:4, :], lb[:, 0:2, :], ACT.Exp).then_inc(sem("lb_exp"), 1)
                    if (s, p) == (1, 6):
                        act.wait_ge(sem("gw_loaded"), 16)
                        act.activation(gw_hi_lo[:, :, 0:8], gw[:, :, :], ACT.Copy).then_inc(sem("gw_hi"), 1)
                    if (s, p) == (2, 0):
                        for n in range(2):
                            act_split(AUX[("p" if n == 0 else "p2", 0)], pT[n], 0)
                    for half, L0 in enumerate(HG_START):
                        if w == L0 - 8:
                            if half == 1:
                                act.wait_ge(sem("hg_mul"), 8)
                            for i in range(2):
                                u = AUX[("tr", 3 * half, i)]
                                aux_filled(act, u)
                                act.activation(Eb[1][:, i * 512:(i + 1) * 512], bank(u), ACT.Sigmoid)
                                act.activation(kF[:, i * 512:(i + 1) * 512], bank(u), ACT.Sigmoid, scale=-1.0)\
                                    .then_inc(aux_free[u % 4], 1)
                        if w == L0 - 6:
                            act.wait_ge(sem("hg_f"), half + 1)
                            act.activation(Eb[1][:, :], Eb[0][:, :], ACT.Ln).then_inc(sem("hg_logf"), 1)
                        n, odd = divmod(w - L0, 2)
                        if 0 <= n < 8 and odd:
                            act.wait_ge(sem("hg_sub"), half * 8 + n + 1)
                            if n == 0:
                                act.activation(Eb[0][:, 0:512].rearrange("p (h t) -> p h t", h=4),
                                               bF[:, :].rearrange("p (h u t) -> p h u t", h=4, u=2)[:, :, 1, :], ACT.Exp)
                                act.activation(Eb[0][:, 512:1024], Eb[0][:, 512:1024], ACT.Exp).then_inc(sem("hg_exp"), 1)
                            else:
                                act.activation(Eb[n % 2][:, :], Eb[n % 2][:, :], ACT.Exp).then_inc(sem("hg_exp"), 1)
                        if w == L0 + 24:
                            act.wait_ge(sem("hg_out"), half + 1)
                            for t in range(T):
                                for h in range(4):
                                    c = (half * 4 + h) * P
                                    squares(ob[:, t, c:c + P], ss[:, SLOT[f"hB{half}"], t * 4 + h:t * 4 + h + 1])
                            act.sem_inc(sem("ss_hB"), 1)
                    if (s, p) in ((9, 3), (10, 1)):
                        act.wait_ge(sem("ml_conv"), s - 8)
                        x = qk[:, 4 * (s - 9):4 * (s - 8), :]
                        act.activation(x, x, ACT.Silu).then_inc(sem("ml_qk"), 1)
                    if (s, p) == (10, 5):
                        act.wait_ge(sem("ml_nf"), 1)
                        link(act.activation(gtmp[:, :, :], gtmp[:, :, :], ACT.Exp))
                        act.activation(gtmp[:, :, :], gtmp[:, :, :], ACT.Ln, bias=1.0).then_inc(sem("ml_ln"), 1)
                    if (s, p) == (11, 1):
                        act.wait_ge(sem("ml_rows"), 1)
                        act.activation(hrow[:, 5, :], hrow[:, 4, :], ACT.Exp, scale=-1.0).then_inc(sem("ml_em"), 1)
                    if (s, p) == (11, 5):
                        act.wait_ge(sem("ml_w_in"), 1)
                        act.activation(Wd[:, :, :], Wd[:, :, :], ACT.Exp).then_inc(sem("ml_w_exp"), 1)
                    if (s, p) == (12, 7):
                        act.wait_ge(sem("ml_h"), 1)
                        for t in range(T):
                            for h in range(4):
                                squares(hA[:, t, h * ML_DV:(h + 1) * ML_DV], ss[:, SLOT["hA"], t * 4 + h:t * 4 + h + 1])
                        act.sem_inc(sem("ss_hA"), 1)
                    if p == 3 and s - 1 in A_GATED:
                        gated(FIRST["A"] + s - 1, ACT.Sigmoid if s - 1 >= 14 else ACT.Silu, "x")
                    if (s, p) == (15, 0):
                        for i in range(4, 8):
                            act_split(AUX[("yT", i)], actB, 2 * i, gains[:, C_MIX:C_MIX + KD])
                    if (s, p) == (15, 6):
                        for i in range(2):
                            act_split(AUX[("yT", i)], actB, 2 * i, gains[:, C_MIX:C_MIX + KD])

            for s in range(4):
                for p in range(8):
                    split_hi(SLABS[FIRST["C"] + s][0] + p)
                    if s == 0 and p == 3:
                        gated(FIRST["A"] + 15, ACT.Sigmoid, "x")
                    if s == 0 and p == 5:
                        for i in range(2, 4):
                            act_split(AUX[("yT", i)], actB, 2 * i, gains[:, C_MIX:C_MIX + KD])
                    if s > 0 and p == 4:
                        resid_squares(s - 1, "h1", "h_added", s)
                    if s > 0 and p == 5:
                        for i in range(2):
                            act_split(AUX[("hD", 2 * s - 2 + i)], actA, 4 * s - 4 + 2 * i, gains[:, C_PE:C_PE + KD])

            for q in range(4):
                split_hi(SLABS[FIRST["DP"] + q][0])
            for s in range(4):
                for p in range(8):
                    split_hi(SLABS[FIRST["D"] + s][0] + p)
                    if s == 0 and p == 0:
                        resid_squares(3, "h1", "h_added", 4)
                    if s == 0 and p == 1:
                        for i in range(6, 8):
                            act_split(AUX[("hD", i)], actA, 2 * i, gains[:, C_PE:C_PE + KD])
                    if s > 1 and p == 1:
                        resid_squares(s - 2, "f2", "h_final", s - 1)
                    if s > 0 and p == 3:
                        gated(FIRST["D"] + s - 1, ACT.Sigmoid, "h1")
                    if s > 0 and p == 5:
                        resid_squares(s - 1, "f1", "h_gated", s)
                    if s > 0 and p == 7:
                        for i in range(2):
                            act_split(AUX[("hE", 2 * s - 2 + i)], actB, 4 * s - 4 + 2 * i, gain_e)

            for s in range(10):
                for p in range(8):
                    n = FIRST["E1"] + s
                    split_hi(SLABS[n][0] + p)
                    w = s * 8 + p
                    if s == 0:
                        if p == 1:
                            resid_squares(2, "f2", "h_final", 3)
                        if p == 3:
                            gated(n - 1, ACT.Sigmoid, "h1")
                        if p == 5:
                            resid_squares(3, "f1", "h_gated", 4)
                        if p == 7:
                            for i in range(6, 8):
                                act_split(AUX[("hE", i)], actB, 2 * i, gain_e)
                    if (s, p) == (1, 0):
                        resid_squares(3, "f2", "h_final", 4)
                    if 1 <= s <= 4 and p == 4:
                        act.wait_ge(sem("qk_tok"), s)
                        for t in range(T):
                            for h in range(4):
                                squares(gate[(s - 1) % 2][:, t, h * P:(h + 1) * P],
                                        ss[:, SLOT[f"qk{s - 1}"], t * 4 + h:t * 4 + h + 1])
                        act.sem_inc(sem("ss_qk"), 1)
                    for b, z0 in enumerate(ATT_START):
                        if w == z0 + 6:
                            act.wait_ge(sem("att_z"), b + 1)
                            link(act.activation(ab[:, :, :], zt[:, :, :], ACT.Abs))
                            link(act.activation(ab[:, :, :], ab[:, :, :], ACT.Exp, scale=-1.0))
                        if w == z0 + 7:
                            act.activation(ab[:, :, :], ab[:, :, :], ACT.Ln, bias=1.0).then_inc(sem("att_ln"), 1)
                        if w == z0 + 16:
                            act.wait_ge(sem("att_arg"), b + 1)
                            act.activation(zt[:, :, :], zt[:, :, :], ACT.Exp).then_inc(sem("att_w"), 1)
                    if s in (7, 8) and p == 3:
                        gelu(n - 1, vs[:, :, (s - 7) * COLS:(s - 6) * COLS])
                    if s == 9 and p == 3:
                        gelu(n - 1, u2[:, :, 0:COLS])
                    if s in (7, 8) and p == 4:
                        slab_taken(act, n - 1)
                        for t in range(T):
                            for h in range(4):
                                c = ((s - 7) * 4 + h) * P
                                squares(vs[:, t, c:c + P], ss[:, SLOT[f"s{s - 7}"], t * 4 + h:t * 4 + h + 1])
                        act.sem_inc(sem("ss_s"), 1)
                    if s == 9 and p == 7:
                        for i in range(2):
                            act_split(AUX[("yaT", i)], actA, 2 * i)

            def merge_round(n, i, first):
                for t, (g, _, _) in enumerate(pieces(n, 4)):
                    if t == 6 and not first:
                        aux_filled(act, AUX[("mT", 0, 3)], i)
                    split_hi(g, i)
                    if first and t == 3:
                        gelu(n - 1, u2[:, :, COLS:2 * COLS])
                    if first and t == 6:
                        for j in range(2, 4):
                            act_split(AUX[("yaT", j)], actA, 2 * j)
                    if first and t == 7:
                        for j in range(4):
                            act_split(AUX[("ybT", j)], actA, 8 + 2 * j)
                    if not first and t == 6:
                        four_hi(actM[0][:, bass.ds(4 * i, 4), :])
                    if t == 11:
                        gated(n, ACT.Sigmoid, "r_e", gate[0], i)
                    if t == 23:
                        gated(n + 2, ACT.Sigmoid, "r_e", gate[1], i)

            merge_round(FIRST["E2"], 0, True)
            with act.Fori(0, D // COLS - 1) as i:
                merge_round(FIRST["E2"] + 4, i, False)

            for s in range(4):
                for p in range(8):
                    split_hi(SLABS[FIRST["G"] + s][0] + p)
                    if s == 0 and p == 5:
                        aux_filled(act, AUX[("mT", 3, 3)])
                        four_hi(actM[0][:, 12:16, :])
                    if s > 0 and p == 4:
                        resid_squares(s - 1, "ffn", "h_added", 4 + s)
                    if s > 0 and p == 5:
                        for i in range(2):
                            act_split(AUX[("hH", 2 * s - 2 + i)], actA, 4 * s - 4 + 2 * i, gains[:, C_FFN:C_FFN + KD])

            for t, (g, s, p) in enumerate(pieces(FIRST["F0"], 2)):
                split_hi(g)
                if t == 4:
                    resid_squares(3, "ffn", "h_added", 8)
                if t == 5:
                    for i in range(6, 8):
                        act_split(AUX[("hH", i)], actA, 2 * i, gains[:, C_FFN:C_FFN + KD])
                if t == 11:
                    gated(FIRST["F0"], ACT.Silu, "ffn", gate[0])
            with act.Fori(0, HIDDEN - 1) as i:
                for t, (g, s, p) in enumerate(pieces(FIRST["F"], 6)):
                    split_hi(g, i)
                    if t == 6:
                        aux_filled(act, AUX[("hid", 0, 3)], i)
                        four_hi(hidT[0][:, :, :])
                    if t == 11:
                        act.wait_ge(sem("hid_ready"), i + 1)
                        gated(FIRST["F"], ACT.Silu, "ffn", gate[0], i)

            for t, (g, s, p) in enumerate(pieces(FIRST["JP"], 12)):
                split_hi(g)
                if t == 4:
                    aux_filled(act, AUX[("hid", HIDDEN - 1, 3)])
                    four_hi(hidT[0][:, :, :])
                for q in range(4):
                    if t == 9 + 2 * q:
                        resid_squares(q, "ple", "h_added", 9 + q)
                    if t == 11 + 2 * q:
                        for i in range(2):
                            act_split(AUX[("hJ", 2 * q + i)], actB, 4 * q + 2 * i, gains[:, C_PLE:C_PLE + KD])
                if t >= 20 and p == 3:
                    q = s - FIRST["J"] - 1
                    if q >= 1:
                        act.wait_ge(sem("out_ready"), q)
                    gated(s - 1, ACT.Sigmoid, "ple", gate[q % 2])
            act.wait_ge(sem("out_ready"), 2)
            for t in range(T):
                act.wait_ge(sem("last_tile"), t + 1)
                act.activation(gate[1][:, t, :], acc2(FIRST["J"] + 3)[:, t, :], ACT.Sigmoid, scale=r_tok("ple", t))\
                    .then_inc(sem("last_gate"), 1)

        @block.tensor
        def _(pe):
            def four_chunks(u, src, i=0):
                for j in range(u, u + 4):
                    c = j % 4
                    aux_taken(pe, j - 4, i)
                    for t in range(T):
                        ins = pe.transpose(bank(j)[:, t * P:(t + 1) * P], src[:, t, c * P:(c + 1) * P], ident[:, :])
                    ins.then_inc(aux_full, 1)

            def transposes(name, src, c0, n=2):
                u = AUX[name]
                free(u)
                for c in range(n):
                    for t in range(T):
                        ins = pe.transpose(bank(u)[:, c * S + t * P:c * S + (t + 1) * P],
                                           src[:, t, (c0 + c) * P:(c0 + c + 1) * P], ident[:, :])
                ins.then_inc(aux_full, 1)

            def free(u):
                if u >= 4:
                    aux_taken(pe, u - 4)

            def piece(n, p, act, k, last, i=0, slabs=0):
                g = SLABS[n][0] + p
                if p == 0 and n >= 2:
                    slab_taken(pe, n - 2, i * (slabs // 2))
                pe.wait_ge(hi_ready, g + 1 + i * ROUND)
                for c in range(PK):
                    for t in range(T):
                        for x in range(2):
                            pe.matmul(acc2(n)[:, t, :], act[x][:, k + c, t * P:(t + 1) * P], whi[:, g % RING, c, :],
                                      start=(p == 0 and c == 0 and x == 0), stop=False)
                pe.wait_ge(lo_ready, g + 1 + i * ROUND)
                for c in range(PK):
                    for t in range(T):
                        ins = pe.matmul(acc2(n)[:, t, :], act[0][:, k + c, t * P:(t + 1) * P], wlo[:, g % RING, c, :],
                                        start=False, stop=(last and c == PK - 1))
                ins.then_inc(piece_used, 1)

            def last_piece(n, p, act, k):
                g = SLABS[n][0] + p
                pe.wait_ge(lo_ready, g + 1)
                for t in range(T):
                    for c in range(PK):
                        for x, w in ((0, whi), (1, whi), (0, wlo)):
                            ins = pe.matmul(acc2(n)[:, t, :], act[x][:, k + c, t * P:(t + 1) * P], w[:, g % RING, c, :],
                                            start=False, stop=(c == PK - 1 and w is wlo))
                    ins.then_inc(sem("last_tile"), 1)

            pe.wait_ge(sem("ident_ready"), 1)
            pe.wait_ge(sem("norm_loaded"), 16)
            pe.transpose(bank(0)[:, 0:KD], stage1[0:KD, :], ident[0:KD, 0:KD]).then_inc(aux_full, 1)

            def transpose_gains():
                u = AUX[("gains", 0)]
                pe.wait_ge(sem("small_loaded"), 16 * 13)
                free(u)
                pe.transpose(bank(u)[:, 0:P], stage1[:, :], ident[:, :])
                pe.transpose(bank(u)[:, P:C_END], stage2[:, :], ident[0:C_END - P, 0:C_END - P]).then_inc(aux_full, 1)

            def transpose_x(i):
                if i % 2 == 0:
                    pe.wait_ge(sem(f"x_loaded{i // 2}"), 16)
                transposes(("xT", i), resid, 2 * i)

            for i in range(2):
                transpose_x(i)

            def tr_slab(s):
                n = FIRST["A"] + s
                slab_taken(pe, n)
                for i in range(2):
                    transposes(("tr", s, i), gate[s % 2], 2 * i)

            def hg_diag(half):
                pe.wait_ge(sem("hg_k"), half + 1)
                aux_taken(pe, AUX[("tr", 3 * half + 1, 1)])
                for i in range(2):
                    u = AUX[("diag", half, i)]
                    free(u)
                    for j in range(4):
                        c = (4 * i + j) * P
                        ins = pe.matmul(bank(u)[:, j * P:(j + 1) * P], kF[:, c:c + P], qF[:, c:c + P], start=True, stop=True)
                    ins.then_inc(aux_full, 1)

            def hg_level(half, n):
                u = AUX[("level", half, n)]
                pe.wait_ge(sem("hg_mul"), half * 8 + n + 1)
                free(u)
                for j in range(4 if n == 0 else 8):
                    m = P if n == 0 else 64
                    c = (2 * j if n == 0 else j) * P
                    ins = pe.matmul(bank(u)[:, j * m:(j + 1) * m], Kp[n % 2][:, c:c + P], Qp[n % 2][:, j * m:(j + 1) * m],
                                    start=True, stop=True)
                ins.then_inc(aux_full, 1)

            def hg_pv(half):
                aux_taken(pe, AUX[("level", half, 7)])
                slab_taken(pe, FIRST["A"] + 2 + 3 * half)
                for t in range(T):
                    u = AUX[("pv", half, t)]
                    free(u)
                    for h in range(4):
                        c = (half * 4 + h) * P
                        o = bank(u)[:, h * P:(h + 1) * P]
                        if t == 1:
                            pe.matmul(o, A01[:, h, :], ob[:, 0, c:c + P], start=True, stop=False)
                        ins = pe.matmul(o, Am[:, 2 * h + t, :], ob[:, t, c:c + P], start=(t == 0), stop=True)
                    ins.then_inc(aux_full, 1)

            def ml_gates():
                u = AUX[("gates", 0)]
                pe.wait_ge(sem("gw_lo"), 1)
                free(u)
                for k in range(KD):
                    pe.matmul(aux[0:16, u % 4, 0:S], gw_hi_lo[:, k, :], actA[0][:, k, :], start=(k == 0), stop=False)
                    ins = pe.matmul(aux[0:8, u % 4, 0:S], gw_hi_lo[:, k, 0:8], actA[1][:, k, :], start=False, stop=(k == KD - 1))
                ins.then_inc(aux_full, 1)

            def ml_gates_by_token():
                u = AUX[("gatesT", 0)]
                aux_taken(pe, AUX[("gates", 0)])
                free(u)
                for t in range(T):
                    ins = pe.transpose(bank(u)[:, t * 16:(t + 1) * 16], gates_ch[:, t * P:(t + 1) * P], ident[0:16, 0:16])
                ins.then_inc(aux_full, 1)

            def ml_gates_tr():
                u = AUX[("gtr", 0)]
                pe.wait_ge(sem("ml_lf"), 1)
                free(u)
                for x in range(2):
                    for t in range(T):
                        ins = pe.transpose(aux[0:4, u % 4, x * S + t * P:x * S + (t + 1) * P], gtok[:, t, 4 * x:4 * x + 4],
                                           ident[:, :])
                ins.then_inc(aux_full, 1)

            def ml_cols():
                u = AUX[("atr", 0)]
                pe.wait_ge(sem("ml_em"), 1)
                free(u)
                for x, row in ((0, 1), (1, 5)):
                    for t in range(T):
                        ins = pe.transpose(bank(u)[:, x * 8 + t * 4:x * 8 + t * 4 + 4], hrow[:, row, t * P:(t + 1) * P],
                                           ident[0:4, 0:4])
                ins.then_inc(aux_full, 1)
                for i in range(2):
                    u = AUX[("bc", i)]
                    free(u)
                    for h in range(2):
                        ins = pe.matmul(bank(u)[:, h * S:(h + 1) * S], sel[:, 2 * i + h, :], hrow[:, 3, :], start=True, stop=True)
                    ins.then_inc(aux_full, 1)

            def ml_scores():
                pe.wait_ge(sem("ml_qk"), 2)
                for h in range(4):
                    u = AUX[("st", h)]
                    free(u)
                    pe.matmul(bank(u)[:, 0:S], qk[:, 4 + h, 0:P], qk[:, h, :], start=True, stop=True)
                    pe.matmul(bank(u)[:, S:S + P], qk[:, 4 + h, P:S], qk[:, h, P:S], start=True, stop=True).then_inc(aux_full, 1)

            def ml_pv(h):
                aux_taken(pe, AUX[("st", h)])
                slab_taken(pe, FIRST["A"] + 9 + h // 2)
                for t in range(T):
                    u = AUX[("mpv", h, t)]
                    free(u)
                    o = bank(u)[:, 0:ML_DV + 1]
                    if t == 0:
                        ins = pe.matmul(o, Wd[:, h, 0:P], vml[:, 0, h, 0:ML_DV + 1], start=True, stop=True)
                    else:
                        pe.matmul(o, Wd[:, h, P:S], vml[:, 0, h, 0:ML_DV + 1], start=True, stop=False)
                        ins = pe.matmul(o, Wd[:, h, S:S + P], vml[:, 1, h, 0:ML_DV + 1], start=False, stop=True)
                    ins.then_inc(aux_full, 1)

            for s in range(16):
                n = FIRST["A"] + s
                for p in range(8):
                    if s == 0:
                        aux_taken(pe, AUX[("xT", p)])
                    piece(n, p, actA, p * PK, p == 7)
                    w = s * 8 + p
                    if s == 0 and p < 6:
                        transpose_x(p + 2)
                    if p == 2 and s - 1 in A_TRANSPOSED:
                        tr_slab(s - 1)
                    if (s, p) == (1, 0):
                        transpose_gains()
                    if (s, p) == (1, 4):
                        pe.wait_ge(sem("p_loaded"), 32)
                        transposes(("p", 0), ptok[0], 0)
                        transposes(("p2", 0), ptok[1], 0)
                    for half, L0 in enumerate(HG_START):
                        if w == L0 - 3:
                            hg_diag(half)
                        n_level, odd = divmod(w - L0, 2)
                        if 0 <= n_level < 8 and not odd:
                            hg_level(half, n_level)
                        if w == L0 + 18:
                            hg_pv(half)
                    if (s, p) == (9, 4):
                        ml_gates()
                    if (s, p) == (9, 7):
                        ml_gates_by_token()
                    if (s, p) == (10, 4):
                        ml_gates_tr()
                    if (s, p) == (10, 7):
                        ml_cols()
                    if (s, p) == (11, 4):
                        ml_scores()
                    for h in range(4):
                        if w == 95 + h:
                            ml_pv(h)
                    if (s, p) == (14, 4):
                        pe.wait_ge(sem("yb_ready"), 2)
                        for i in range(4, 8):
                            transposes(("yT", i), ob, 2 * i - 8)
                    if (s, p) == (15, 2):
                        pe.wait_ge(sem("ya_ready"), 1)
                        for i in range(2):
                            transposes(("yT", i), hA, 2 * i)

            for s in range(4):
                n = FIRST["C"] + s
                for p in range(8):
                    k = (KD // 2 + p * PK) % KD
                    if s == 0:
                        aux_taken(pe, AUX[("yT", k // PK)])
                    piece(n, p, actB, k, p == 7)
                    if s == 0 and p == 1:
                        pe.wait_ge(sem("ya_ready"), 2)
                        for i in range(2, 4):
                            transposes(("yT", i), hA, 2 * i)
                    if s > 0 and p == 1:
                        pe.wait_ge(sem("h_added"), s)
                        for i in range(2):
                            transposes(("hD", 2 * s - 2 + i), resid, 4 * s - 4 + 2 * i)

            for q in range(4):
                piece(FIRST["DP"] + q, 0, pT[0], 0, True)
                if q == 1:
                    pe.wait_ge(sem("h_added"), 4)
                    for i in range(6, 8):
                        transposes(("hD", i), resid, 2 * i)
            for s in range(4):
                n = FIRST["D"] + s
                for p in range(8):
                    if s == 0:
                        aux_taken(pe, AUX[("hD", p)])
                    piece(n, p, actA, p * PK, p == 7)
                    if s > 0 and p == 3:
                        pe.wait_ge(sem("h_gated"), s)
                        for i in range(2):
                            transposes(("hE", 2 * s - 2 + i), resid, 4 * s - 4 + 2 * i)

            def tr2_slab(s):
                pe.wait_ge(sem("qk_normed"), s + 1)
                for i in range(2):
                    transposes(("tr2", s, i), gate[s % 2], 2 * i)

            def spatial_weights():
                pe.wait_ge(sem("ws_masked"), 1)
                for i in range(2):
                    u = AUX[("ws", i)]
                    free(u)
                    for j in range(4):
                        ins = pe.transpose(bank(u)[:, j * P:(j + 1) * P], wsr[:, 4 * i + j, :], ident[:, :])
                    ins.then_inc(aux_full, 1)

            def att_scores(b):
                aux_taken(pe, AUX[("tr2", 1 if b else 0, 1)])
                aux_taken(pe, AUX[("tr2", 3 if b else 2, 1)])
                for j in range(4):
                    u, h = AUX[("z", b, j)], 4 * b + j
                    free(u)
                    pe.matmul(bank(u)[:, 0:S], kT[:, h, 0:P], qT[:, h, :], start=True, stop=True)
                    pe.matmul(bank(u)[:, S:S + P], kT[:, h, P:S], qT[:, h, P:S], start=True, stop=True).then_inc(aux_full, 1)

            def att_tail(b):
                pe.wait_ge(sem("att_l"), b + 1)
                for j in range(4):
                    u = AUX[("tail", b, j)]
                    free(u)
                    o = bank(u)
                    pe.matmul(o[:, 0:S], later[:, :], Lp[:, j, 0:S], start=True, stop=False)
                    pe.matmul(o[:, P:S], ones[:, 0:P], Lp[:, j, S:S + P], start=False, stop=True)
                    pe.matmul(o[:, S:S + P], later[:, :], Lp[:, j, S:S + P], start=True, stop=True).then_inc(aux_full, 1)

            def att_pv(b):
                pe.wait_ge(sem("att_masked"), b + 1)
                slab_taken(pe, FIRST["E1"] + 4 + b)
                for t in range(T):
                    u = AUX[("att", b, t)]
                    free(u)
                    for j in range(4):
                        c = (4 * b + j) * P
                        o = bank(u)[:, j * P:(j + 1) * P]
                        if t == 0:
                            ins = pe.matmul(o, zt[:, j, 0:P], vA[:, 0, c:c + P], start=True, stop=True)
                        else:
                            pe.matmul(o, zt[:, j, P:S], vA[:, 0, c:c + P], start=True, stop=False)
                            ins = pe.matmul(o, zt[:, j, S:S + P], vA[:, 1, c:c + P], start=False, stop=True)
                    ins.then_inc(aux_full, 1)

            def spatial_mix(half):
                pe.wait_ge(sem("vs_ready"), half + 1)
                for i in range(2):
                    u = AUX[("sgu", 2 * half + i)]
                    free(u)
                    for j in range(2):
                        g = 4 * half + 2 * i + j
                        ins = pe.matmul(bank(u)[:, j * S:(j + 1) * S].rearrange("p (t c) -> p t c", t=T), wsT[:, g, :],
                                        vs[:, :, g * P:(g + 1) * P], start=True, stop=True)
                    ins.then_inc(aux_full, 1)

            for s in range(10):
                n = FIRST["E1"] + s
                for p in range(8):
                    if s == 0:
                        aux_taken(pe, AUX[("hE", p)])
                    piece(n, p, actB, p * PK, p == 7)
                    w = s * 8 + p
                    if s == 0 and p == 3:
                        pe.wait_ge(sem("h_gated"), 4)
                        for i in range(6, 8):
                            transposes(("hE", i), resid, 2 * i)
                    if 1 <= s <= 4 and p == (7 if s == 4 else 5):
                        tr2_slab(s - 1)
                    if (s, p) == (2, 1):
                        spatial_weights()
                    for b, z0 in enumerate(ATT_START):
                        if w == z0:
                            att_scores(b)
                        if w == z0 + 10:
                            att_tail(b)
                        if w == z0 + 17:
                            att_pv(b)
                    if (s, p) == (9, 1):
                        spatial_mix(0)
                    if (s, p) == (9, 3):
                        pe.wait_ge(sem("ya2_ready"), 1)
                        for i in range(2):
                            transposes(("yaT", i), u2, 2 * i)

            def merge_round(n0, i, first):
                for t, (_, n, p) in enumerate(pieces(n0, 4)):
                    if n - n0 in (0, 2):
                        piece(n, p, actB, p * PK, p == 7, i, 4)
                    else:
                        if first:
                            aux_taken(pe, AUX[("yaT" if n == n0 + 1 else "ybT", p)])
                        piece(n, p, actA, (0 if n == n0 + 1 else 8) + p * PK, p == 3, i, 4)
                    if first:
                        if t == 0:
                            spatial_mix(1)
                        if t == 3:
                            pe.wait_ge(sem("ya2_ready"), 2)
                            for j in range(2, 4):
                                transposes(("yaT", j), u2, 2 * j)
                        if t == 4:
                            for j in range(4):
                                aux_taken(pe, AUX[("att", j // 2, 1)])
                                transposes(("ybT", j), vA, 2 * j)
                    elif t == 2:
                        pe.wait_ge(sem("merged_ready"), i + 1)
                        four_chunks(AUX[("mT", 0, 0)], merged, i)

            merge_round(FIRST["E2"], 0, True)
            with pe.Fori(0, D // COLS - 1) as i:
                merge_round(FIRST["E2"] + 4, i, False)

            for s in range(4):
                n = FIRST["G"] + s
                for p in range(8):
                    if s == 0:
                        for c in range(PK):
                            aux_taken(pe, AUX[("mT", p // 2, (p % 2) * PK + c)])
                    piece(n, p, actM, p * PK, p == 7)
                    if s == 0 and p == 1:
                        pe.wait_ge(sem("merged_ready"), 4)
                        four_chunks(AUX[("mT", 3, 0)], merged)
                    if s > 0 and p == 1:
                        pe.wait_ge(sem("h_added"), 4 + s)
                        for i in range(2):
                            transposes(("hH", 2 * s - 2 + i), resid, 4 * s - 4 + 2 * i)

            for t, (_, n, p) in enumerate(pieces(FIRST["F0"], 2)):
                if t < 8:
                    aux_taken(pe, AUX[("hH", p)])
                piece(n, p, actA, p * PK, p == 7)
                if t == 1:
                    pe.wait_ge(sem("h_added"), 8)
                    for i in range(6, 8):
                        transposes(("hH", i), resid, 2 * i)
            with pe.Fori(0, HIDDEN - 1) as i:
                n0 = FIRST["F"]
                for t, (_, n, p) in enumerate(pieces(n0, 6)):
                    if n in (n0, n0 + 5):
                        piece(n, p, actA, p * PK, p == 7, i, 6)
                    else:
                        if n == n0 + 1 and p == 0:
                            for c in range(4):
                                aux_taken(pe, AUX[("hid", 0, c)], i)
                        piece(n, p, hidT, p * PK, p == 1, i, 6)
                    if t == 1:
                        pe.wait_ge(sem("hid_ready"), i + 1)
                        four_chunks(AUX[("hid", 0, 0)], hid, i)

            for t, (_, n, p) in enumerate(pieces(FIRST["JP"], 12)):
                if t < 4:
                    piece(n, 0, pT[1], 0, True)
                elif t < 12:
                    if t == 4:
                        for c in range(4):
                            aux_taken(pe, AUX[("hid", HIDDEN - 1, c)])
                    piece(n, p, hidT, p * PK, p == 1)
                elif t < 43:
                    if t < 20:
                        aux_taken(pe, AUX[("hJ", p)])
                    piece(n, p, actB, p * PK, p == 7)
                else:
                    last_piece(n, p, actB, p * PK)
                if t == 0:
                    pe.wait_ge(sem("hid_ready"), HIDDEN)
                    four_chunks(AUX[("hid", HIDDEN - 1, 0)], hid)
                for q in range(4):
                    if t == 7 + 2 * q:
                        pe.wait_ge(sem("h_added"), 9 + q)
                        for i in range(2):
                            transposes(("hJ", 2 * q + i), resid, 4 * q + 2 * i)

        @block.vector
        def _(dve):
            steps = [0]
            gates = [0]

            def link(ins):
                steps[0] += 1
                ins.then_inc(sem("dve_step"), 1)
                dve.wait_ge(sem("dve_step"), steps[0])

            def split_lo(g, i=0):
                dve.wait_ge(hi_ready, g + 1 + i * ROUND)
                dve.tensor_tensor(wlo[:, g % RING], raw_piece(g), whi[:, g % RING].bitcast(F32), ALU.subtract)\
                    .then_inc(lo_ready, 1)

            splits = [0]

            def lo_split(u, dst, c0, gain=None, n=2):
                splits[0] += 1
                dve.wait_ge(split_hi_done, splits[0])
                for c in range(n):
                    x = bank(u)[:, c * S:(c + 1) * S]
                    hi = dst[0][:, c0 + c, :].bitcast(F32)
                    if gain is None:
                        ins = dve.tensor_tensor(dst[1][:, c0 + c, :], x, hi, ALU.subtract)
                    else:
                        ins = dve.scalar_tensor_tensor(out=dst[1][:, c0 + c, :], in0=x, scalar=gain[:, c0 + c:c0 + c + 1],
                                                       in1=hi, op0=ALU.mult, op1=ALU.subtract)
                ins.then_inc(aux_free[u % 4], 1)

            def four_lo(u, dst, i=0):
                splits[0] += 1
                dve.wait_ge(split_hi_done, splits[0] + i)
                dve.tensor_tensor(dst[1], aux[:, :, 0:S], dst[0].bitcast(F32), ALU.subtract).then_inc(aux_free[u % 4], 1)
                aux_taken(dve, u, i)
                for j in range(u + 1, u + 4):
                    dve.sem_inc(aux_free[j % 4], 1)

            def variance(name, width, sums=None):
                i, n = SLOT[name], dict(POWS)[name]
                dve.tensor_scalar(var[:, i, 0:n], ss[:, i, 0:n] if sums is None else sums, 1.0 / width, EPS, ALU.mult, ALU.add)\
                    .then_inc(pow_in, 1)

            def row_variance(name):
                i = SLOT[name]
                link(dve.tensor_reduce(var[:, i, 4:6], ss[:, i, :].rearrange("p (t c) -> p t c", t=T), AX.X, ALU.add))
                variance(name, D, var[:, i, 4:6])

            def scaled(n, dst, r):
                slab_made(dve, n)
                for t in range(T):
                    x = acc2(n)[:, t, :]
                    d = dst[:, t]
                    if len(d.shape) == 3:
                        x = x.rearrange("p (h c) -> p h c", h=d.shape[1])
                    ins = dve.tensor_scalar(d, x, r(t), None, ALU.mult)
                return ins

            def next_gate(i=0):
                gates[0] += 1
                dve.wait_ge(gate_ready, gates[0] + i)
                return gate[(gates[0] - 1) % 2]

            def gate_taken(n, i=0):
                next_gate(i)
                dve.sem_inc(acc_free[n % 2], 1)

            aux_filled(dve, AUX[("gain0", 0)])
            dve.tensor_copy(gains[:, C_NORM:C_NORM + KD], bank(0, KD)).then_inc(aux_free[0], 1)
            aux_taken(dve, AUX[("gain0", 0)])

            def vectors():
                u = AUX[("gains", 0)]
                aux_filled(dve, u)
                dve.tensor_copy(gains[:, C_PE:C_END], bank(u, C_END)[:, C_PE:C_END]).then_inc(aux_free[u % 4], 1)
                aux_taken(dve, u)
                dve.tensor_tensor(gain_e[:, :], gains[:, C_ATTN:C_ATTN + KD], gains[:, C_FW:C_FW + KD], ALU.mult)
                dve.tensor_scalar(qn_scaled[:, :], gains[:, C_QN:C_QN + 1], SB_D ** -0.5, None, ALU.mult)
                lb_rows = gains[:, C_LB:C_LB + 16].rearrange("p (l h) -> p l h", l=2)
                link(dve.tensor_tensor(lb[:, 2, :], lb_rows[:, 0, :], lb_rows[:, 1, :], ALU.max))
                dve.tensor_tensor(lb[:, 0:2, :], lb_rows, lb[:, 2:3, :].to_broadcast([P, 2, 8]), ALU.subtract)\
                    .then_inc(sem("lb_in"), 1)

            def lower_bounds():
                dve.wait_ge(sem("lb_exp"), 1)
                link(dve.tensor_tensor(lb[:, 0, :], lb[:, 2, :], lb[:, 3, :], ALU.add))
                link(dve.reciprocal(lb[:, 1, :], lb[:, 0, :]))
                link(dve.tensor_tensor(lb[:, 0, :], lb[:, 2, :], lb[:, 1, :], ALU.mult))
                link(dve.tensor_scalar(lb[:, 1, :], lb[:, 0, :], -1.0, 1.0, ALU.mult, ALU.add))

            def hg_forget(half):
                aux_taken(dve, AUX[("tr", 3 * half, 1)])
                for h in range(4):
                    c = slice(h * S, (h + 1) * S)
                    e = half * 4 + h
                    ins = dve.tensor_scalar(Eb[0][:, c], Eb[1][:, c], lb[:, 1, e:e + 1], lb[:, 0, e:e + 1], ALU.mult, ALU.add)
                ins.then_inc(sem("hg_f"), 1)

            def hg_cumsum(half):
                dve.wait_ge(sem("hg_logf"), half + 1)
                for h in range(4):
                    e = half * 4 + h
                    c = slice(h * S, (h + 1) * S)
                    ins = dve.tensor_scalar(kF[:, c], kF[:, c], lb[:, 1, e:e + 1], None, ALU.mult)
                ins.then_inc(sem("hg_k"), 1)
                for j in range(8):
                    c = slice(j * P, (j + 1) * P)
                    ins = dve.tensor_tensor_scan(bF[:, c], ones[:, 0:P], Eb[1][:, c], 0.0, ALU.mult, ALU.add)
                link(ins)

            def hg_queries(half):
                for i in range(2):
                    u = AUX[("tr", 3 * half + 1, i)]
                    aux_filled(dve, u)
                    dve.tensor_copy(qF[:, i * 512:(i + 1) * 512], bank(u)).then_inc(aux_free[u % 4], 1)

            def hg_diagonal(half):
                for i in range(2):
                    u = AUX[("diag", half, i)]
                    aux_filled(dve, u)
                    dve.tensor_tensor(Am[:, 4 * i:4 * i + 4, :], bank(u).rearrange("p (g t) -> p g t", g=4),
                                      ident[:, :].unsqueeze(1).to_broadcast([P, 4, P]), ALU.mult).then_inc(aux_free[u % 4], 1)

            def halves(x, s):
                return x[:, :].rearrange("p (n u s) -> p n u s", u=2, s=s)

            def hg_sub(half, n):
                s = LEVELS[n]
                b, nb = halves(bF, s), 512 // s
                mid = b[:, :, 0, s - 1:s].to_broadcast([P, nb, s])
                e = Eb[n % 2][:, :].rearrange("p (x n s) -> p x n s", x=2, s=s)
                if n > 0:
                    dve.tensor_tensor(e[:, 0], b[:, :, 1, :], mid, ALU.subtract)
                dve.tensor_tensor(e[:, 1], mid, b[:, :, 0, :], ALU.subtract).then_inc(sem("hg_sub"), 1)

            def hg_mul(half, n):
                s = LEVELS[n]
                dve.wait_ge(sem("hg_exp"), half * 8 + n + 1)
                if n >= 2:
                    aux_filled(dve, AUX[("level", half, n - 2)])
                e = Eb[n % 2][:, :].rearrange("p (x n s) -> p x n s", x=2, s=s)
                dve.tensor_tensor(Qp[n % 2][:, :].rearrange("p (n s) -> p n s", s=s), halves(qF, s)[:, :, 1, :], e[:, 0], ALU.mult)
                dve.tensor_tensor(halves(Kp[n % 2], s)[:, :, 0, :], halves(kF, s)[:, :, 0, :], e[:, 1], ALU.mult)\
                    .then_inc(sem("hg_mul"), 1)

            def hg_take(half, n):
                s = LEVELS[n]
                u = AUX[("level", half, n)]
                aux_filled(dve, u)
                if n == 0:
                    ins = dve.tensor_copy(A01[:, :, :], bank(u).rearrange("p (h t) -> p h t", h=4))
                else:
                    aux_taken(dve, AUX[("diag", half, 1) if n == 1 else ("level", half, n - 1)])
                    nb = 64 // s
                    dst = Am[:, :, :].rearrange("p g (n u s) -> p g n u s", u=2, s=s)[:, :, :, 1, :]
                    m = lmask[:, n - 1, :].bitcast(I32).rearrange("p (n s) -> p n s", s=s).unsqueeze(1).to_broadcast([P, 8, nb, s])
                    ins = dve.copy_predicated(dst, m, bank(u).rearrange("p (g n s) -> p g n s", g=8, s=s))
                ins.then_inc(aux_free[u % 4], 1)

            def hg_output(half):
                aux_filled(dve, AUX[("pv", half, 1)])
                for t in range(T):
                    u = AUX[("pv", half, t)]
                    dve.tensor_copy(ob[:, t, half * 512:(half + 1) * 512], bank(u)).then_inc(aux_free[u % 4], 1)
                for t in range(T):
                    aux_taken(dve, AUX[("pv", half, t)])
                dve.sem_inc(sem("hg_out"), 1)

            def ml_conv(s):
                for i in range(2):
                    u = AUX[("tr", s, i)]
                    aux_filled(dve, u)
                    for tap in range(ML_TAPS - 1, -1, -1):
                        back = ML_TAPS - 1 - tap
                        for c in range(2):
                            ch = 4 * (s - 7) + 2 * i + c
                            x, y = bank(u)[:, c * S:(c + 1) * S], qk[:, ch, :]
                            w = gains[:, C_CONVW + tap * 8 + ch:C_CONVW + tap * 8 + ch + 1]
                            if back == 0:
                                ins = dve.tensor_scalar(y, x, w, gains[:, C_CONVB + ch:C_CONVB + ch + 1], ALU.mult, ALU.add)
                            else:
                                ins = dve.scalar_tensor_tensor(out=y[:, back:S], in0=x[:, 0:S - back], scalar=w,
                                                               in1=y[:, back:S], op0=ALU.mult, op1=ALU.add)
                            if tap > 0 and c == 1:
                                link(ins)
                    ins.then_inc(aux_free[u % 4], 1)
                    aux_taken(dve, u)
                dve.sem_inc(sem("ml_conv"), 1)

            def ml_gates_out():
                u = AUX[("gates", 0)]
                aux_filled(dve, u)
                dve.tensor_copy(gates_ch[:, :], aux[0:16, u % 4, 0:S]).then_inc(aux_free[u % 4], 1)

            def ml_gates():
                u = AUX[("gatesT", 0)]
                aux_filled(dve, u)
                dve.wait_ge(sem("gbias_loaded"), 32)
                for part in range(2):
                    for t in range(T):
                        x = bank(u)[:, t * 16 + part * 8:t * 16 + part * 8 + 8]
                        ins = dve.scalar_tensor_tensor(out=gtok[:, t, :], in0=x, scalar=r_tok("x", t),
                                                       in1=gtok[:, t, :] if part else gbias[:, :], op0=ALU.mult, op1=ALU.add)
                    if part == 0:
                        link(ins)
                ins.then_inc(aux_free[u % 4], 1)
                aux_taken(dve, u)
                f = gtok[:, :, 4:8]
                dve.scalar_tensor_tensor(out=gtmp[:, :, :], in0=f, scalar=-1.0, in1=f, op0=ALU.mult, op1=ALU.min)\
                    .then_inc(sem("ml_nf"), 1)

            def ml_logf():
                f = gtok[:, :, 4:8]
                dve.wait_ge(sem("ml_ln"), 1)
                dve.scalar_tensor_tensor(out=f, in0=f, scalar=0.0, in1=gtmp[:, :, :], op0=ALU.min, op1=ALU.subtract)\
                    .then_inc(sem("ml_lf"), 1)

            def ml_rows():
                u = AUX[("gtr", 0)]
                aux_filled(dve, u)
                gi, lf = aux[0:4, u % 4, 0:S], aux[0:4, u % 4, S:2 * S]
                link(dve.tensor_tensor_scan(hrow[:, 0, :], ones[0:4, :], lf, 0.0, ALU.mult, ALU.add))
                dve.tensor_tensor(hrow[:, 1, :], gi, hrow[:, 0, :], ALU.subtract).then_inc(aux_free[u % 4], 1)
                aux_taken(dve, u)
                link(dve.tensor_tensor_scan(hrow[:, 2, :], ones[0:4, :], hrow[:, 1, :], 0.0, ALU.mult, ALU.max))
                dve.tensor_scalar(hrow[:, 3, :], hrow[:, 2, :], -1.0, None, ALU.mult)
                dve.tensor_tensor(hrow[:, 4, :], hrow[:, 0, :], hrow[:, 2, :], ALU.add).then_inc(sem("ml_rows"), 1)

            def ml_weights():
                u = AUX[("atr", 0)]
                aux_filled(dve, u)
                dve.tensor_copy(acol[:, :], bank(u, 16)).then_inc(aux_free[u % 4], 1)
                aux_taken(dve, u)
                for i in range(2):
                    u = AUX[("bc", i)]
                    aux_filled(dve, u)
                    for j in range(2):
                        h = 2 * i + j
                        x = bank(u)[:, j * S:(j + 1) * S]
                        dve.tensor_scalar(Wd[:, h, 0:S], x, acol[:, h:h + 1], 0.0, ALU.add, ALU.min)
                        ins = dve.tensor_scalar(Wd[:, h, S:S + P], x[:, P:S], acol[:, 4 + h:5 + h], 0.0, ALU.add, ALU.min)
                    ins.then_inc(aux_free[u % 4], 1)
                aux_taken(dve, AUX[("bc", 1)])
                dve.sem_inc(sem("ml_w_in"), 1)

            def diagonal_blocks(x):
                return x[:, :, :].rearrange("p h (b t) -> p h b t", b=3)[:, :, 0:3:2, :]

            def ml_mask():
                dve.wait_ge(sem("ml_w_exp"), 1)
                d = diagonal_blocks(Wd)
                link(dve.tensor_tensor(d, d, causal[:, :].unsqueeze(1).unsqueeze(1).to_broadcast([P, 4, 2, P]), ALU.mult))
                dve.memset(vml[:, :, :, ML_DV:ML_DV + 2], 1.0)

            def ml_scores():
                for h in range(4):
                    u = AUX[("st", h)]
                    aux_filled(dve, u)
                    dve.scalar_tensor_tensor(out=Wd[:, h, :], in0=bank(u, 384), scalar=ML_DQK ** -0.5, in1=Wd[:, h, :],
                                             op0=ALU.mult, op1=ALU.mult).then_inc(aux_free[u % 4], 1)

            def ml_output(h):
                for t in range(T):
                    u = AUX[("mpv", h, t)]
                    aux_filled(dve, u)
                    d = den[:, h * 2 + t, :]
                    dn = bank(u)[:, ML_DV:ML_DV + 1]
                    link(dve.tensor_scalar(d[:, 0:1], dn, -1.0, acol[:, 8 + t * 4 + h:9 + t * 4 + h], ALU.mult, ALU.max))
                    link(dve.tensor_tensor(d[:, 0:1], d[:, 0:1], dn, ALU.max))
                    link(dve.reciprocal(d[:, 1:2], d[:, 0:1]))
                    dve.tensor_scalar(hA[:, t, h * ML_DV:(h + 1) * ML_DV], bank(u, ML_DV), d[:, 1:2], None, ALU.mult)\
                        .then_inc(aux_free[u % 4], 1)
                if h == 3:
                    for hh in range(2, 4):
                        for t in range(T):
                            aux_taken(dve, AUX[("mpv", hh, t)])
                    dve.sem_inc(sem("ml_h"), 1)

            def per_head(name):
                return rstd[:, SLOT[name], :].rearrange("p (t h) -> p t h", t=T)

            def a_evacuate(s):
                n = FIRST["A"] + s
                if s == 0:
                    powered(dve, "x")
                r = lambda t: r_tok("x", t)
                if s in A_TRANSPOSED:
                    scaled(n, gate[s % 2], r).then_inc(acc_free[n % 2], 1)
                elif s in (2, 5):
                    h = (s - 2) // 3
                    scaled(n, ob[:, :, h * 512:(h + 1) * 512], r).then_inc(acc_free[n % 2], 1)
                elif s in (9, 10):
                    scaled(n, vml[:, :, 2 * (s - 9):2 * (s - 8), 0:ML_DV], r).then_inc(acc_free[n % 2], 1)
                else:
                    x, half = (ob, s // 8) if s < 12 else (hA, s % 2)
                    y = x[:, :, half * COLS:(half + 1) * COLS]
                    link(dve.tensor_tensor(y, y, next_gate()[:, :, :], ALU.mult))
                    dve.sem_inc(acc_free[n % 2], 1)
                    if s < 12:
                        dve.sem_inc(sem("yb_ready"), 1)
                    if s >= 14:
                        dve.sem_inc(sem("ya_ready"), 1)

            for s in range(16):
                for p in range(8):
                    w = s * 8 + p
                    if w < 2:
                        lo_split(AUX[("xT", p)], actA, 2 * p, gains[:, C_NORM:C_NORM + KD])
                    split_lo(SLABS[FIRST["A"] + s][0] + p)
                    if 2 <= w < 8:
                        lo_split(AUX[("xT", p)], actA, 2 * p, gains[:, C_NORM:C_NORM + KD])
                    if (s, p) == (1, 0):
                        dve.wait_ge(sem("ss_x"), 1)
                        row_variance("x")
                    if (s, p) == (1, 4):
                        vectors()
                    if (s, p) == (1, 6):
                        lower_bounds()
                    if (s, p) == (1, 5):
                        dve.wait_ge(sem("consts_ready"), 1)
                        dve.memset(Kp[0][:, :], 0.0)
                        dve.memset(Kp[1][:, :], 0.0)
                    if (s, p) == (1, 7):
                        dve.wait_ge(sem("gw_hi"), 1)
                        dve.tensor_tensor(gw_hi_lo[:, :, 8:16], gw[:, :, :], gw_hi_lo[:, :, 0:8].bitcast(F32), ALU.subtract)\
                            .then_inc(sem("gw_lo"), 1)
                    if (s, p) == (2, 0):
                        for n in range(2):
                            lo_split(AUX[("p" if n == 0 else "p2", 0)], pT[n], 0)
                    for half, L0 in enumerate(HG_START):
                        if w == L0 - 7:
                            hg_forget(half)
                        if w == L0 - 5:
                            hg_cumsum(half)
                        if w == L0 - 1:
                            hg_queries(half)
                        if w == L0 + 1:
                            hg_diagonal(half)
                        n, odd = divmod(w - L0, 2)
                        if not odd:
                            if 0 <= n - 1 < 8:
                                hg_mul(half, n - 1)
                            if 0 <= n < 8:
                                hg_sub(half, n)
                        if odd and 0 <= n - 2 < 8:
                            hg_take(half, n - 2)
                        if w == L0 + 22:
                            hg_output(half)
                        if w == L0 + 25:
                            dve.wait_ge(sem("ss_hB"), half + 1)
                            variance(f"hB{half}", HG_E)
                        if w == L0 + 28:
                            powered(dve, f"hB{half}")
                            x = ob[:, :, half * 512:(half + 1) * 512].rearrange("p t (h c) -> p t h c", h=4)
                            link(dve.tensor_tensor(x, x, per_head(f"hB{half}").unsqueeze(3).to_broadcast([P, T, 4, P]), ALU.mult))
                    if p == 3 and s > 0:
                        a_evacuate(s - 1)
                    if (s, p) in ((9, 0), (9, 6)):
                        ml_conv(7 + p // 6)
                    if (s, p) == (10, 0):
                        ml_gates_out()
                    if (s, p) == (10, 3):
                        ml_gates()
                    if (s, p) == (10, 6):
                        ml_logf()
                    if (s, p) == (11, 0):
                        ml_rows()
                    if (s, p) == (11, 3):
                        ml_weights()
                    if (s, p) == (11, 6):
                        ml_mask()
                    if (s, p) == (12, 0):
                        ml_scores()
                    if s == 12 and 3 <= p <= 6:
                        ml_output(p - 3)
                    if (s, p) == (13, 1):
                        dve.wait_ge(sem("ss_hA"), 1)
                        variance("hA", ML_DV)
                    if (s, p) == (13, 2):
                        powered(dve, "hA")
                        x = hA[:, :, :].rearrange("p t (h c) -> p t h c", h=4)
                        link(dve.tensor_tensor(x, x, per_head("hA").unsqueeze(3).to_broadcast([P, T, 4, ML_DV]), ALU.mult))
                    if (s, p) == (15, 0):
                        for i in range(4, 8):
                            lo_split(AUX[("yT", i)], actB, 2 * i, gains[:, C_MIX:C_MIX + KD])
                    if (s, p) == (15, 6):
                        for i in range(2):
                            lo_split(AUX[("yT", i)], actB, 2 * i, gains[:, C_MIX:C_MIX + KD])

            def add_slab(n, s):
                slab_made(dve, n)
                x = resid[:, :, s * COLS:(s + 1) * COLS]
                dve.tensor_tensor(x, x, acc2(n), ALU.add).then_inc(acc_free[n % 2], 1)
                slab_taken(dve, n)
                dve.sem_inc(sem("h_added"), 1)

            for s in range(4):
                for p in range(8):
                    split_lo(SLABS[FIRST["C"] + s][0] + p)
                    if s == 0 and p == 3:
                        a_evacuate(15)
                    if s == 0 and p == 5:
                        for i in range(2, 4):
                            lo_split(AUX[("yT", i)], actB, 2 * i, gains[:, C_MIX:C_MIX + KD])
                    if s > 0 and p == 3:
                        add_slab(FIRST["C"] + s - 1, s - 1)
                    if s > 0 and p == 5:
                        for i in range(2):
                            lo_split(AUX[("hD", 2 * s - 2 + i)], actA, 4 * s - 4 + 2 * i, gains[:, C_PE:C_PE + KD])

            def d_gate(s):
                g = next_gate()
                n = FIRST["D"] + s
                dve.sem_inc(acc_free[n % 2], 1)
                link(dve.tensor_tensor(g[:, :, :], g[:, :, :], ple[:, :, s * COLS:(s + 1) * COLS], ALU.mult))
                x = resid[:, :, s * COLS:(s + 1) * COLS]
                dve.tensor_tensor(x, x, g[:, :, :], ALU.add).then_inc(sem("h_gated"), 1)

            def d_final(s):
                dve.wait_ge(sem("ss_f1"), s + 1)
                aux_filled(dve, AUX[("hE", 2 * s + 1)])
                x = resid[:, :, s * COLS:(s + 1) * COLS]
                dve.tensor_tensor(x, x, fw[:, s * COLS:(s + 1) * COLS].unsqueeze(1).to_broadcast([P, T, COLS]), ALU.mult)\
                    .then_inc(sem("h_final"), 1)

            def ple_slab(n, q, dst):
                slab_made(dve, n)
                dve.tensor_copy(dst[:, :, q * COLS:(q + 1) * COLS], acc2(n)).then_inc(acc_free[n % 2], 1)

            for t, (g, n, p) in enumerate(pieces(FIRST["DP"], 8)):
                split_lo(g)
                s = n - FIRST["D"]
                if t == 2:
                    add_slab(FIRST["C"] + 3, 3)
                if 3 <= t < 7:
                    ple_slab(FIRST["DP"] + t - 3, t - 3, ple)
                if t == 5:
                    for i in range(6, 8):
                        lo_split(AUX[("hD", i)], actA, 2 * i, gains[:, C_PE:C_PE + KD])
                if t == 7:
                    dve.wait_ge(sem("ss_h1"), 4)
                    row_variance("h1")
                    dve.wait_ge(sem("fw_loaded"), 16)
                    slab_taken(dve, FIRST["DP"] + 3)
                if s > 0 and p == 3:
                    d_gate(s - 1)
                if s > 0 and p == 7:
                    for i in range(2):
                        lo_split(AUX[("hE", 2 * s - 2 + i)], actB, 4 * s - 4 + 2 * i, gain_e)
                    d_final(s - 1)

            def rE(t):
                return r_e[:, t:t + 1]

            def qk_normalise(s):
                dve.wait_ge(sem("ss_qk"), s + 1)
                variance(f"qk{s}", SB_D)

            def qk_scale(s):
                powered(dve, f"qk{s}")
                x = gate[s % 2][:, :, :].rearrange("p t (h c) -> p t h c", h=4)
                dve.tensor_tensor(x, x, per_head(f"qk{s}").unsqueeze(3).to_broadcast([P, T, 4, P]), ALU.mult)\
                    .then_inc(sem("qk_normed"), 1)

            def qk_transposed(s):
                dst, gain = (qT, qn_scaled) if s < 2 else (kT, gains[:, C_KN:C_KN + 1])
                for i in range(2):
                    u = AUX[("tr2", s, i)]
                    aux_filled(dve, u)
                    c = 4 * (s % 2) + 2 * i
                    dve.tensor_scalar(dst[:, c:c + 2, :], bank(u).rearrange("p (h t) -> p h t", h=2), gain[:, 0:1], None, ALU.mult)\
                        .then_inc(aux_free[u % 4], 1)

            def att_take(b):
                for j in range(4):
                    u = AUX[("z", b, j)]
                    aux_filled(dve, u)
                    dve.tensor_copy(zt[:, j, :], bank(u, 384)).then_inc(aux_free[u % 4], 1)
                for j in range(4):
                    aux_taken(dve, AUX[("z", b, j)])
                dve.sem_inc(sem("att_z"), 1)

            def strict_blocks(x):
                d = diagonal_blocks(x)
                return dve.tensor_tensor(d, d, strict[:, :].unsqueeze(1).unsqueeze(1).to_broadcast([P, 4, 2, P]), ALU.mult)

            def att_logs(b):
                dve.wait_ge(sem("att_ln"), b + 1)
                link(dve.scalar_tensor_tensor(out=Lp[:, :, :], in0=zt[:, :, :], scalar=0.0, in1=ab[:, :, :], op0=ALU.max, op1=ALU.add))
                strict_blocks(Lp).then_inc(sem("att_l"), 1)
                link(dve.scalar_tensor_tensor(out=zt[:, :, :], in0=zt[:, :, :], scalar=0.0, in1=ab[:, :, :], op0=ALU.min,
                                              op1=ALU.subtract))

            def att_arg(b):
                for j in range(4):
                    u = AUX[("tail", b, j)]
                    aux_filled(dve, u)
                    dve.tensor_tensor(zt[:, j, :], zt[:, j, :], bank(u, 384), ALU.subtract).then_inc(aux_free[u % 4], 1)
                for j in range(4):
                    aux_taken(dve, AUX[("tail", b, j)])
                dve.sem_inc(sem("att_arg"), 1)

            def att_mask(b):
                dve.wait_ge(sem("att_w"), b + 1)
                strict_blocks(zt).then_inc(sem("att_masked"), 1)

            def att_output(b):
                aux_filled(dve, AUX[("att", b, 1)])
                for t in range(T):
                    u = AUX[("att", b, t)]
                    dve.tensor_copy(vA[:, t, b * 512:(b + 1) * 512], bank(u)).then_inc(aux_free[u % 4], 1)

            def vs_scale(half):
                powered(dve, f"s{half}")
                x = vs[:, :, half * 512:(half + 1) * 512].rearrange("p t (h c) -> p t h c", h=4)
                dve.tensor_tensor(x, x, per_head(f"s{half}").unsqueeze(3).to_broadcast([P, T, 4, P]), ALU.mult)\
                    .then_inc(sem("vs_ready"), 1)

            def spatial_gate(half):
                dve.wait_ge(sem("gbc_loaded"), 16)
                for i in range(2):
                    u = AUX[("sgu", 2 * half + i)]
                    aux_filled(dve, u)
                    g = 4 * half + 2 * i
                    t4 = ab[:, 0:2, 0:S].rearrange("p g (t c) -> p g t c", t=T)
                    for j in range(2):
                        ins = dve.tensor_tensor(t4[:, j], bank(u)[:, j * S:(j + 1) * S].rearrange("p (t c) -> p t c", t=T),
                                                gbc[:, (g + j) * P:(g + j + 1) * P].unsqueeze(1).to_broadcast([P, T, P]), ALU.mult)
                    ins.then_inc(aux_free[u % 4], 1)
                    aux_taken(dve, u)
                    for j in range(2):
                        x = u2[:, :, (g + j) * P:(g + j + 1) * P]
                        ins = dve.scalar_tensor_tensor(out=x, in0=t4[:, j], scalar=gains[:, C_BS + g + j:C_BS + g + j + 1], in1=x,
                                                       op0=ALU.add, op1=ALU.mult)
                    if i == 0:
                        link(ins)
                ins.then_inc(sem("ya2_ready"), 1)

            for s in range(10):
                n = FIRST["E1"] + s
                for p in range(8):
                    split_lo(SLABS[n][0] + p)
                    w = s * 8 + p
                    if s == 0:
                        if p == 3:
                            d_gate(3)
                        if p == 6:
                            dve.wait_ge(sem("ss_f1"), 4)
                            row_variance("f1")
                        if p == 7:
                            for i in range(6, 8):
                                lo_split(AUX[("hE", i)], actB, 2 * i, gain_e)
                            d_final(3)
                            dve.wait_ge(sem("h_final"), 4)
                            dve.sem_inc(sem("block1_done"), 1)
                    if (s, p) == (1, 1):
                        dve.wait_ge(sem("ss_f2"), 4)
                        powered(dve, "f1")
                        i, j = SLOT["f1"], SLOT["f2"]
                        link(dve.tensor_reduce(var[:, j, 4:6], ss[:, j, :].rearrange("p (t c) -> p t c", t=T), AX.X, ALU.add))
                        for _ in range(2):
                            link(dve.tensor_tensor(var[:, j, 4:6], var[:, j, 4:6], rstd[:, i, 0:T], ALU.mult))
                        variance("f2", D, var[:, j, 4:6])
                    if (s, p) == (1, 2):
                        powered(dve, "f2")
                        dve.tensor_tensor(r_e[:, :], rstd[:, SLOT["f1"], 0:T], rstd[:, SLOT["f2"], 0:T], ALU.mult)\
                            .then_inc(sem("r_e_ready"), 1)
                        dve.wait_ge(sem("r_e_ready"), 1)
                    if 1 <= s <= 4:
                        if p == 3:
                            scaled(n - 1, gate[(s - 1) % 2], rE).then_inc(acc_free[(n - 1) % 2], 1)
                            slab_taken(dve, n - 1)
                            dve.sem_inc(sem("qk_tok"), 1)
                        if p == 5:
                            qk_normalise(s - 1)
                        if p == 6:
                            qk_scale(s - 1)
                    if 2 <= s <= 5 and p == (4 if s == 5 else 2):
                        qk_transposed(s - 2)
                    if (s, p) == (2, 4):
                        for i in range(2):
                            u = AUX[("ws", i)]
                            aux_filled(dve, u)
                            dve.tensor_copy(wsT[:, 4 * i:4 * i + 4, :], bank(u).rearrange("p (g t) -> p g t", g=4))\
                                .then_inc(aux_free[u % 4], 1)
                    if s == 2 and p in (5, 6):
                        t = p - 5
                        link(dve.tensor_scalar(resid[:, t, :], resid[:, t, :], r_tok("f1", t), None, ALU.mult))
                    if s in (5, 6) and p == 3:
                        scaled(n - 1, vA[:, :, (s - 5) * 512:(s - 4) * 512], rE).then_inc(acc_free[(n - 1) % 2], 1)
                    for b, z0 in enumerate(ATT_START):
                        if w == z0 + 5:
                            att_take(b)
                        if w == z0 + 9:
                            att_logs(b)
                        if w == z0 + 14:
                            att_arg(b)
                        if w == z0 + 18:
                            att_mask(b)
                        if w == z0 + 21:
                            att_output(b)
                    if s in (7, 8) and p == 5:
                        dve.wait_ge(sem("ss_s"), s - 6)
                        variance(f"s{s - 7}", P)
                    if s in (7, 8) and p == 7:
                        vs_scale(s - 7)
                    if (s, p) == (9, 4):
                        slab_taken(dve, n - 1)
                        spatial_gate(0)
                    if (s, p) == (9, 7):
                        for i in range(2):
                            lo_split(AUX[("yaT", i)], actA, 2 * i)

            def merge_second(n, i):
                slab_made(dve, n, i)
                g = gate[1][:, :, :]
                dve.tensor_tensor(g, g, acc2(n), ALU.mult).then_inc(acc_free[n % 2], 1)
                slab_taken(dve, n, 2 * i)
                dve.tensor_tensor(merged[:, :, :], merged[:, :, :], g, ALU.add).then_inc(sem("merged_ready"), 1)

            def merge_round(n0, i, first):
                for t, (g, n, p) in enumerate(pieces(n0, 4)):
                    split_lo(g, i)
                    if first:
                        if t == 4:
                            slab_taken(dve, n - 1)
                            spatial_gate(1)
                        if t == 6:
                            for j in range(2, 4):
                                lo_split(AUX[("yaT", j)], actA, 2 * j)
                        if t == 7:
                            for j in range(4):
                                lo_split(AUX[("ybT", j)], actA, 8 + 2 * j)
                    else:
                        if t == 3:
                            merge_second(n0 - 1, i)
                        if t == 6:
                            four_lo(AUX[("mT", 0, 0)], [actM[x][:, bass.ds(4 * i, 4), :] for x in range(2)], i)
                    if t == 11:
                        gate_taken(n0, 2 * i)
                    if t == 15:
                        slab_made(dve, n0 + 1, i)
                        dve.tensor_tensor(merged[:, :, :], gate[0][:, :, :], acc2(n0 + 1), ALU.mult)\
                            .then_inc(acc_free[(n0 + 1) % 2], 1)
                    if t == 23:
                        gate_taken(n0 + 2, 2 * i)

            merge_round(FIRST["E2"], 0, True)
            with dve.Fori(0, D // COLS - 1) as i:
                merge_round(FIRST["E2"] + 4, i, False)
            gates[0] += 4
            splits[0] += 2

            for s in range(4):
                n = FIRST["G"] + s
                for p in range(8):
                    split_lo(SLABS[n][0] + p)
                    if s == 0 and p == 3:
                        merge_second(n - 1, 0)
                    if s == 0 and p == 5:
                        four_lo(AUX[("mT", 3, 0)], [actM[x][:, 12:16, :] for x in range(2)])
                    if s > 0 and p == 3:
                        add_slab(n - 1, s - 1)
                    if s > 0 and p == 5:
                        for i in range(2):
                            lo_split(AUX[("hH", 2 * s - 2 + i)], actA, 4 * s - 4 + 2 * i, gains[:, C_FFN:C_FFN + KD])

            def hidden(n, i=0):
                slab_made(dve, n, i)
                for t in range(T):
                    ins = dve.scalar_tensor_tensor(out=hid[:, t, :], in0=acc2(n)[:, t, :], scalar=r_tok("ffn", t),
                                                   in1=gate[0][:, t, :], op0=ALU.mult, op1=ALU.mult)
                ins.then_inc(acc_free[n % 2], 1)
                slab_taken(dve, n, 3 * i)
                dve.sem_inc(sem("hid_ready"), 1)

            for t, (g, n, p) in enumerate(pieces(FIRST["F0"], 2)):
                split_lo(g)
                if t == 3:
                    add_slab(FIRST["F0"] - 1, 3)
                if t == 5:
                    for i in range(6, 8):
                        lo_split(AUX[("hH", i)], actA, 2 * i, gains[:, C_FFN:C_FFN + KD])
                if t == 6:
                    dve.wait_ge(sem("ss_ffn"), 4)
                    row_variance("ffn")
                if t == 11:
                    gate_taken(FIRST["F0"])
            with dve.Fori(0, HIDDEN - 1) as i:
                n0 = FIRST["F"]
                for t, (g, n, p) in enumerate(pieces(n0, 6)):
                    split_lo(g, i)
                    if t == 3:
                        hidden(n0 - 1, i)
                    if t == 6:
                        four_lo(AUX[("hid", 0, 0)], [hidT[x][:, :, :] for x in range(2)], i)
                    if t == 11:
                        gate_taken(n0, i)
                    for q in range(4):
                        if t == 12 + 2 * q:
                            slab_made(dve, n0 + 1 + q, i)
                            x = resid[:, :, q * COLS:(q + 1) * COLS]
                            dve.tensor_tensor(x, x, acc2(n0 + 1 + q), ALU.add).then_inc(acc_free[(n0 + 1 + q) % 2], 1)
            gates[0] += HIDDEN - 2
            splits[0] += HIDDEN - 2

            def j_gate(s):
                n = FIRST["J"] + s
                g = gate[s % 2]
                gate_taken(n)
                link(dve.tensor_tensor(g[:, :, :], g[:, :, :], ple2[:, :, s * COLS:(s + 1) * COLS], ALU.mult))
                x = resid[:, :, s * COLS:(s + 1) * COLS]
                dve.tensor_tensor(x, x, g[:, :, :], ALU.add).then_inc(sem("out_ready"), 1)

            for t, (g, n, p) in enumerate(pieces(FIRST["JP"], 12)):
                split_lo(g)
                if t == 2:
                    hidden(FIRST["JP"] - 1)
                if 3 <= t < 7:
                    ple_slab(FIRST["JP"] + t - 3, t - 3, ple2)
                if t == 4:
                    four_lo(AUX[("hid", HIDDEN - 1, 0)], [hidT[x][:, :, :] for x in range(2)])
                for q in range(4):
                    if t == 8 + 2 * q:
                        add_slab(FIRST["FT"] + q, q)
                    if t == 11 + 2 * q:
                        for i in range(2):
                            lo_split(AUX[("hJ", 2 * q + i)], actB, 4 * q + 2 * i, gains[:, C_PLE:C_PLE + KD])
                if t == 18:
                    dve.wait_ge(sem("ss_ple"), 4)
                    row_variance("ple")
                if t >= 20 and p == 3:
                    j_gate(n - FIRST["J"] - 1)
            for t in range(T):
                dve.wait_ge(sem("last_gate"), t + 1)
                g, x = gate[1][:, t, :], resid[:, t, 3 * COLS:4 * COLS]
                link(dve.tensor_tensor(g, g, ple2[:, t, 3 * COLS:4 * COLS], ALU.mult))
                dve.tensor_tensor(x, x, g, ALU.add).then_inc(sem("out_ready"), 1)


_INS = ["x", "p", "norm_w", "w_in", "conv_w", "conv_b", "ml_b_i", "ml_b_f", "ml_norm_w", "hg_lb", "hg_norm_w", "w_out",
        "pe_norm_w", "w_pg", "w_pe", "final_norm_w", "p_2", "attn_norm_g_2", "w_in_2", "sgu_norm_g_2", "w_s_2", "b_s_2",
        "q_norm_g_2", "k_norm_g_2", "w_up_a_2", "w_up_b_2", "w_o_2", "ffn_norm_g_2", "w_ffn_in_2", "w_ffn_out_2",
        "ple_norm_g_2", "w_ple_gate_2", "w_ple_2"]


def kernel(**inputs):
    import numpy as _np
    import concourse.bacc as _bacc
    from concourse.bass_utils import run_bass_kernel_spmd as _run

    nc = _bacc.Bacc("TRN2", target_bir_lowering=False, num_devices=1)
    arrays, aps = {}, {}
    for name in _INS:
        a = _np.ascontiguousarray(inputs[name])
        arrays[f"in_{name}"] = a
        aps[name] = nc.dram_tensor(f"in_{name}", a.shape, mybir.dt.from_np(a.dtype), kind="ExternalInput").ap()
    out = nc.dram_tensor("out_0", (1, S, D), F32, kind="ExternalOutput").ap()
    two_blocks_kernel(nc, aps, out)
    r = _run(nc, [arrays], core_ids=[0])
    return r.results[0]["out_0"]
```
